# Optimizing a Trainium2 kernel written in Bass

```python
import jax, jax.numpy as jnp
from jax import lax
import numpy as np

D_MODEL = 1024
BATCH = 1
SEQ = 512
DEPTH = 1

N_META = 16
EPS = 1e-6
POOL_WINDOWS = (2, 4, 8, 16)
N_POOL_GROUPS = 4
D_POOL = D_MODEL // 2
POOL_GROUP = D_POOL // N_POOL_GROUPS
N_HEADS = 8
D_LAT = D_MODEL // 8
N_IDX_HEADS = 8
D_IDX = 32
INDEX_SCALE = (N_IDX_HEADS ** -0.5) * (D_IDX ** -0.5)
ATTN_SCALE = D_LAT ** -0.5
Q_BLOCK = 128
TOP_K_MAX = 256
D_CONV = D_MODEL // 2
CONV_WIDTH = 3
N_BRANCH = 3
D_FF = -(-8 * D_MODEL // (3 * 256)) * 256
SPLITS = (D_POOL, N_HEADS * D_LAT, D_LAT, N_IDX_HEADS * D_IDX, D_IDX,
          N_IDX_HEADS, D_CONV, D_CONV, D_CONV, N_BRANCH * D_MODEL)
N_IN = sum(SPLITS)


def rms_norm(x, g):
    xf = x.astype(jnp.float32)
    y = xf * lax.rsqrt(jnp.mean(xf * xf, axis=-1, keepdims=True) + EPS)
    return (y * g.astype(jnp.float32)).astype(x.dtype)

def split_columns(p):
    offs, acc = [], 0
    for s in SPLITS[:-1]:
        acc += s
        offs.append(acc)
    return jnp.split(p, offs, axis=-1)

def pool_mixer(u, pool_w, pool_scale):
    B, L, _ = u.shape
    uf = u.astype(jnp.float32)
    cs = lax.cumsum(uf, axis=1)
    pos1 = jnp.arange(1, L + 1)
    outs = []
    for g, w in enumerate(POOL_WINDOWS):
        csg = cs[..., g * POOL_GROUP:(g + 1) * POOL_GROUP]
        shifted = jnp.pad(csg, ((0, 0), (w, 0), (0, 0)))[:, :L]
        count = jnp.minimum(pos1, w).astype(jnp.float32)[None, :, None]
        mean = (csg - shifted) / count
        outs.append(mean - uf[..., g * POOL_GROUP:(g + 1) * POOL_GROUP])
    pooled = jnp.stack(outs, axis=2).astype(u.dtype)
    mixed = jnp.einsum('blgc,gcd->blgd', pooled, pool_w).reshape(B, L, D_POOL)
    return mixed * pool_scale

def dsa_attention(q, qi, wi, c, ki):
    B, L = q.shape[0], q.shape[1]
    k_top = min(TOP_K_MAX, SEQ // 4)
    nb = -(-L // Q_BLOCK)
    Lp = nb * Q_BLOCK
    pad = Lp - L

    def to_blocks(a):
        a = jnp.pad(a, [(0, 0), (0, pad)] + [(0, 0)] * (a.ndim - 2))
        return jnp.moveaxis(a.reshape(B, nb, Q_BLOCK, *a.shape[2:]), 1, 0)

    kpos = jnp.arange(L, dtype=jnp.int32)
    qpos = jnp.arange(Lp, dtype=jnp.int32).reshape(nb, Q_BLOCK)
    wi = wi * INDEX_SCALE

    def block(args):
        qb, qib, wb, pb = args
        s = jnp.einsum('bqhd,bkd->bqhk', qib, ki).astype(jnp.float32)
        score = jnp.einsum('bqhk,bqh->bqk', jax.nn.relu(s), wb.astype(jnp.float32))
        causal = kpos[None, None, :] <= pb[None, :, None]
        score = jnp.where(causal, score, -jnp.inf)
        _, sel = lax.top_k(score, k_top)
        c_sel = jax.vmap(lambda cb, ib: cb[ib])(c, sel)
        logits = jnp.einsum('bqhd,bqkd->bqhk', qb, c_sel).astype(jnp.float32) * ATTN_SCALE
        valid = (sel <= pb[None, :, None])[:, :, None, :]
        p = jax.nn.softmax(jnp.where(valid, logits, -jnp.inf), axis=-1).astype(c.dtype)
        return jnp.einsum('bqhk,bqkd->bqhd', p, c_sel)

    out = lax.map(block, (to_blocks(q), to_blocks(qi), to_blocks(wi), qpos))
    out = jnp.moveaxis(out, 0, 1).reshape(B, Lp, N_HEADS * D_LAT)
    return out[:, :L]

def short_conv_mixer(b_gate, c_gate, u, conv_w):
    v = c_gate * u
    rhs = conv_w.reshape(CONV_WIDTH, 1, D_CONV)
    y = lax.conv_general_dilated(v, rhs, window_strides=(1,),
                                 padding=[(CONV_WIDTH - 1, 0)],
                                 dimension_numbers=('NWC', 'WIO', 'NWC'),
                                 feature_group_count=D_CONV)
    return b_gate * y

def hybrid_layer(h, norm1_g, w_in, b_gate, pool_w, pool_scale, w_a, kv_norm_g,
                 w_b, conv_w, w_c, w_o, norm2_g, w_gate_up, w_down):
    B, L, _ = h.shape
    xn = rms_norm(h, norm1_g)
    p = xn @ w_in
    (u_pool, q, c_lat, q_idx, k_idx, w_idx, cb, cc, cu, g_raw) = split_columns(p)
    y_a = pool_mixer(u_pool, pool_w, pool_scale) @ w_a
    c_lat = rms_norm(c_lat, kv_norm_g)
    attn = dsa_attention(q.reshape(B, L, N_HEADS, D_LAT),
                         q_idx.reshape(B, L, N_IDX_HEADS, D_IDX),
                         w_idx, c_lat, k_idx)
    y_b = attn @ w_b
    y_c = short_conv_mixer(cb, cc, cu, conv_w) @ w_c
    g = jax.nn.sigmoid(g_raw + b_gate).reshape(B, L, N_BRANCH, D_MODEL)
    m = g[:, :, 0] * y_a + g[:, :, 1] * y_b + g[:, :, 2] * y_c
    h = h + m @ w_o
    hn = rms_norm(h, norm2_g)
    gate, up = jnp.split(hn @ w_gate_up, 2, axis=-1)
    return h + (jax.nn.silu(gate) * up) @ w_down

def first_inputs(seed: int = 0) -> dict:
    key = jax.random.key(seed)
    ks = jax.random.split(key, 20)
    f32 = jnp.float32

    def nrm(k, shape, fan):
        return jax.random.normal(k, shape, f32) * (fan ** -0.5)

    def gain(k, shape):
        return 1.0 + 0.1 * jax.random.normal(k, shape, f32)

    return {
        "x": jax.random.normal(ks[0], (BATCH, SEQ, D_MODEL), f32),
        "meta": jax.random.normal(ks[1], (N_META, D_MODEL), f32),
        "norm1_g": gain(ks[2], (DEPTH, D_MODEL)),
        "w_in": nrm(ks[3], (DEPTH, D_MODEL, N_IN), D_MODEL),
        "b_gate": 0.01 * jax.random.normal(ks[4], (DEPTH, N_BRANCH * D_MODEL), f32),
        "pool_w": nrm(ks[5], (DEPTH, N_POOL_GROUPS, POOL_GROUP, POOL_GROUP), POOL_GROUP),
        "pool_scale": gain(ks[6], (DEPTH, D_POOL)),
        "w_a": nrm(ks[7], (DEPTH, D_POOL, D_MODEL), D_POOL),
        "kv_norm_g": gain(ks[8], (DEPTH, D_LAT)),
        "w_b": nrm(ks[9], (DEPTH, N_HEADS * D_LAT, D_MODEL), N_HEADS * D_LAT),
        "conv_w": nrm(ks[10], (DEPTH, CONV_WIDTH, D_CONV), CONV_WIDTH),
        "w_c": nrm(ks[11], (DEPTH, D_CONV, D_MODEL), D_CONV),
        "w_o": nrm(ks[12], (DEPTH, D_MODEL, D_MODEL), D_MODEL),
        "norm2_g": gain(ks[13], (DEPTH, D_MODEL)),
        "w_gate_up": nrm(ks[14], (DEPTH, D_MODEL, 2 * D_FF), D_MODEL),
        "w_down": nrm(ks[15], (DEPTH, D_FF, D_MODEL), D_FF),
        "final_g": gain(ks[16], (D_MODEL,)),
    }

def first_block(x, meta, norm1_g, w_in, b_gate, pool_w, pool_scale, w_a, kv_norm_g,
              w_b, conv_w, w_c, w_o, norm2_g, w_gate_up, w_down, final_g):
    B = x.shape[0]
    meta_b = jnp.broadcast_to(meta[None], (B, N_META, D_MODEL)).astype(x.dtype)
    h = jnp.concatenate([meta_b, x], axis=1)
    for l in range(DEPTH):
        h = hybrid_layer(h, norm1_g[l], w_in[l], b_gate[l], pool_w[l], pool_scale[l],
                         w_a[l], kv_norm_g[l], w_b[l], conv_w[l], w_c[l], w_o[l],
                         norm2_g[l], w_gate_up[l], w_down[l])
    return rms_norm(h, final_g)[:, N_META:]


PLE_DIM = 256
HEAD_DIM = 64
FOX_HEADS = 8
SB_HEADS = 8
FOX_WIDTH = FOX_HEADS * HEAD_DIM
SB_WIDTH = SB_HEADS * HEAD_DIM
D_FF_2 = 2816
FORGET_BIAS_INIT = 2.0
IN_SIZES = (FOX_WIDTH, FOX_WIDTH, FOX_WIDTH, FOX_HEADS, SB_WIDTH, SB_WIDTH, SB_WIDTH, D_MODEL, D_MODEL)
IN_WIDTH = 3 * FOX_WIDTH + FOX_HEADS + 3 * SB_WIDTH + 2 * D_MODEL


def rms_norm_2(x, g):
    xf = x.astype(jnp.float32)
    y = xf * lax.rsqrt(jnp.mean(xf * xf, axis=-1, keepdims=True) + EPS)
    return (y * g.astype(jnp.float32)).astype(x.dtype)

def swiglu(h, w_gate, w_up, w_down):
    return (jax.nn.silu(h @ w_gate) * (h @ w_up)) @ w_down

def to_blocks(t):
    b, s = t.shape[0], t.shape[1]
    return jnp.moveaxis(t.reshape(b, s // Q_BLOCK, Q_BLOCK, *t.shape[2:]), 1, 0)

def from_blocks(t):
    nb, b = t.shape[0], t.shape[1]
    return jnp.moveaxis(t, 0, 1).reshape(b, nb * Q_BLOCK, -1)

def forgetting_attention(q, k, v, log_f):
    s_len = q.shape[1]
    scale = HEAD_DIM ** -0.5
    F = jnp.cumsum(log_f, axis=1)
    Fk = jnp.transpose(F, (0, 2, 1))[:, :, None, :]
    kpos = jnp.arange(s_len)
    qpos = kpos.reshape(s_len // Q_BLOCK, Q_BLOCK)

    def one_block(args):
        qi, Fi, pi = args
        logits = jnp.einsum('bqhd,bkhd->bhqk', qi, k).astype(jnp.float32) * scale
        logits = logits + jnp.transpose(Fi, (0, 2, 1))[..., None] - Fk
        mask = pi[:, None] >= kpos[None, :]
        logits = jnp.where(mask, logits, -jnp.inf)
        w = jax.nn.softmax(logits, axis=-1)
        return jnp.einsum('bhqk,bkhd->bqhd', w.astype(v.dtype), v)

    out = lax.map(one_block, (to_blocks(q), to_blocks(F), qpos))
    return from_blocks(out)

def stick_breaking_attention(q, k, v):
    s_len = q.shape[1]
    scale = HEAD_DIM ** -0.5
    kpos = jnp.arange(s_len)
    qpos = kpos.reshape(s_len // Q_BLOCK, Q_BLOCK)

    def one_block(args):
        qi, pi = args
        z = jnp.einsum('bqhd,bkhd->bhqk', qi, k).astype(jnp.float32) * scale
        mask = kpos[None, :] < pi[:, None]
        log_beta = jax.nn.log_sigmoid(z)
        log_1m = jnp.where(mask, jax.nn.log_sigmoid(-z), 0.0)
        after = lax.cumsum(log_1m, axis=3, reverse=True) - log_1m
        a = jnp.where(mask, jnp.exp(log_beta + after), 0.0)
        return jnp.einsum('bhqk,bkhd->bqhd', a.astype(v.dtype), v)

    out = lax.map(one_block, (to_blocks(q), qpos))
    return from_blocks(out)

def split_columns_2(t):
    outs, start = [], 0
    for size in IN_SIZES:
        outs.append(t[..., start:start + size])
        start += size
    return outs

def second_inputs(seed: int = 0) -> dict:
    key = jax.random.key(seed)
    ks = jax.random.split(key, 24)

    def w(k, shape, fan_in):
        return jax.random.normal(k, shape, jnp.float32) * (fan_in ** -0.5)

    def gain(k, shape):
        return 1.0 + 0.05 * jax.random.normal(k, shape, jnp.float32)

    L = DEPTH
    return {
        "x": jax.random.normal(ks[0], (BATCH, SEQ, D_MODEL), jnp.float32),
        "p": jax.random.normal(ks[1], (DEPTH, BATCH, SEQ, PLE_DIM), jnp.float32),
        "ffn1_norm": gain(ks[2], (L, D_MODEL)),
        "ffn1_w_gate": w(ks[3], (L, D_MODEL, D_FF_2), D_MODEL),
        "ffn1_w_up": w(ks[4], (L, D_MODEL, D_FF_2), D_MODEL),
        "ffn1_w_down": w(ks[5], (L, D_FF_2, D_MODEL), D_FF_2),
        "mix_norm": gain(ks[6], (L, D_MODEL)),
        "w_in": w(ks[7], (L, D_MODEL, IN_WIDTH), D_MODEL),
        "forget_bias": FORGET_BIAS_INIT + 0.1 * jax.random.normal(ks[8], (L, FOX_HEADS), jnp.float32),
        "q_norm": gain(ks[9], (L, HEAD_DIM)),
        "k_norm": gain(ks[10], (L, HEAD_DIM)),
        "w_branch_fox": w(ks[11], (L, FOX_WIDTH, D_MODEL), FOX_WIDTH),
        "w_branch_sb": w(ks[12], (L, SB_WIDTH, D_MODEL), SB_WIDTH),
        "w_out": w(ks[13], (L, D_MODEL, D_MODEL), D_MODEL),
        "ffn2_norm": gain(ks[14], (L, D_MODEL)),
        "ffn2_w_gate": w(ks[15], (L, D_MODEL, D_FF_2), D_MODEL),
        "ffn2_w_up": w(ks[16], (L, D_MODEL, D_FF_2), D_MODEL),
        "ffn2_w_down": w(ks[17], (L, D_FF_2, D_MODEL), D_FF_2),
        "ple_norm": gain(ks[18], (L, D_MODEL)),
        "w_ple_gate": w(ks[19], (L, D_MODEL, D_MODEL), D_MODEL),
        "w_ple_proj": w(ks[20], (L, PLE_DIM, D_MODEL), PLE_DIM),
    }

def second_block(x, p, ffn1_norm, ffn1_w_gate, ffn1_w_up, ffn1_w_down, mix_norm, w_in,
              forget_bias, q_norm, k_norm, w_branch_fox, w_branch_sb, w_out,
              ffn2_norm, ffn2_w_gate, ffn2_w_up, ffn2_w_down, ple_norm,
              w_ple_gate, w_ple_proj):
    b, s_len, _ = x.shape
    for i in range(DEPTH):
        x = x + 0.5 * swiglu(rms_norm_2(x, ffn1_norm[i]), ffn1_w_gate[i], ffn1_w_up[i], ffn1_w_down[i])

        h = rms_norm_2(x, mix_norm[i])
        fq, fk, fv, f_logit, sq, sk, sv, g_fox, g_sb = split_columns_2(h @ w_in[i])
        fq = rms_norm_2(fq.reshape(b, s_len, FOX_HEADS, HEAD_DIM), q_norm[i])
        fk = rms_norm_2(fk.reshape(b, s_len, FOX_HEADS, HEAD_DIM), k_norm[i])
        fv = fv.reshape(b, s_len, FOX_HEADS, HEAD_DIM)
        log_f = jax.nn.log_sigmoid((f_logit + forget_bias[i]).astype(jnp.float32))
        y_fox = forgetting_attention(fq, fk, fv, log_f)

        sq = sq.reshape(b, s_len, SB_HEADS, HEAD_DIM)
        sk = sk.reshape(b, s_len, SB_HEADS, HEAD_DIM)
        sv = sv.reshape(b, s_len, SB_HEADS, HEAD_DIM)
        y_sb = stick_breaking_attention(sq, sk, sv)

        merged = (jax.nn.sigmoid(g_fox) * (y_fox @ w_branch_fox[i])
                  + jax.nn.sigmoid(g_sb) * (y_sb @ w_branch_sb[i]))
        x = x + merged @ w_out[i]

        x = x + 0.5 * swiglu(rms_norm_2(x, ffn2_norm[i]), ffn2_w_gate[i], ffn2_w_up[i], ffn2_w_down[i])

        x = x + jax.nn.sigmoid(rms_norm_2(x, ple_norm[i]) @ w_ple_gate[i]) * (p[i] @ w_ple_proj[i])
    return x


def setup_inputs(seed=0):
    out = dict(first_inputs(seed))
    for name, value in second_inputs(seed + 1).items():
        if name != "x":
            out[name + "_2"] = value
    return out


def reference(
    x, meta, norm1_g, w_in, b_gate, pool_w, pool_scale, w_a, kv_norm_g, w_b, conv_w, w_c, w_o,
    norm2_g, w_gate_up, w_down, final_g, p_2, ffn1_norm_2, ffn1_w_gate_2, ffn1_w_up_2,
    ffn1_w_down_2, mix_norm_2, w_in_2, forget_bias_2, q_norm_2, k_norm_2, w_branch_fox_2,
    w_branch_sb_2, w_out_2, ffn2_norm_2, ffn2_w_gate_2, ffn2_w_up_2, ffn2_w_down_2, ple_norm_2,
    w_ple_gate_2, w_ple_proj_2,
):
    x = first_block(
        x, meta, norm1_g, w_in, b_gate, pool_w, pool_scale, w_a, kv_norm_g, w_b, conv_w, w_c,
        w_o, norm2_g, w_gate_up, w_down, final_g,
    )
    return second_block(
        x, p_2, ffn1_norm_2, ffn1_w_gate_2, ffn1_w_up_2, ffn1_w_down_2, mix_norm_2, w_in_2,
        forget_bias_2, q_norm_2, k_norm_2, w_branch_fox_2, w_branch_sb_2, w_out_2, ffn2_norm_2,
        ffn2_w_gate_2, ffn2_w_up_2, ffn2_w_down_2, ple_norm_2, w_ple_gate_2, w_ple_proj_2,
    )


_drawn_inputs = setup_inputs


def setup_inputs(seed=0):
    import zlib

    import numpy as np

    out = dict(_drawn_inputs(seed))
    spreads = {}
    factors = {'b_gate': 8.0,
     'kv_norm_g': 3.856,
     'ffn1_norm_2': 2.801,
     'forget_bias_2': 45.992,
     'q_norm_2': 8.0,
     'k_norm_2': 8.0,
     'ffn2_norm_2': 3.363,
     'ple_norm_2': 54.576}
    for name, (base, spread) in spreads.items():
        noise = np.random.default_rng([zlib.crc32(name.encode()), seed]).standard_normal(out[name].shape)
        drawn = base * np.exp(spread * noise) if base else spread * noise
        out[name] = __import__('jax').numpy.asarray(drawn.astype(out[name].dtype))
    for name, factor in factors.items():
        out[name] = (out[name] * factor).astype(out[name].dtype)
    return out
```

```python
from contextlib import ExitStack

import concourse.bass as bass
from concourse import mybir

F32 = mybir.dt.float32
F32R = mybir.dt.float32r
ACT = mybir.ActivationFunctionType
ALU = mybir.AluOpType

P = 128
D = 1024
DK = D // P
T = 512
META = 16
TM = T + META
HALF = TM // 2
QB = T // P
CH = 2048
CW = CH // DK
EPS = 1e-6
HEADS = 8
D_LAT = 128
ATTN_SCALE = D_LAT ** -0.5
D_IDX = 32
INDEX_SCALE = HEADS ** -0.5 * D_IDX ** -0.5
TOP_K = T // 4
D_FF = 2816
FK = D_FF // P
HEAD_DIM = 64
DOWN_K = (8, 8, 6)
NEG = -1.0e30
TAKEN = -3.0e38

O_U, O_Q, O_C, O_QI, O_KI, O_CB, O_CC, O_CU, O_G = 0, 512, 1536, 1664, 1920, 1960, 2472, 2984, 3496
KW = D_IDX + HEADS
S_FQ, S_FK, S_FV, S_FL, S_SQ, S_SK, S_SV, S_GF, S_GS = 0, 512, 1024, 1536, 1544, 2056, 2568, 3080, 4104

C_LAT, C_QI, C_Q, C_U, C_CC, C_CU, C_CB, C_AC, C_B, C_O = 0, 1, 2, 6, 8, 10, 12, 14, 26, 34
C_F = (38, 72, 135)
C_D = (60, 94, 157)
C_FQ, C_FK, C_FV, C_FL, C_SQ, C_SK, C_SV, C_MX, C_O2 = 106, 108, 110, 112, 113, 115, 117, 119, 131
C_PG, C_PP, N_CHUNKS = 169, 173, 174

V_N1, V_N2, V_FIN, V_F1, V_MX, V_F2, V_PL, V_BG, V_PS, V_CW, V_KV, V_QN, V_KN, V_ROWS = (
    0, 8, 16, 24, 32, 40, 48, 56, 80, 84, 96, 97, 98, 99)


def lin(value, per=0, i=None):
    return value if i is None else i * per + value


def one(t, n):
    return t[:, n, :] if isinstance(n, int) else t[:, bass.ds(n, 1), :].rearrange("p o t -> p (o t)")


def col(t, n):
    return t[:, n:n + 1] if isinstance(n, int) else t[:, bass.ds(n, 1)]


def build(nc, I, out):
    with ExitStack() as ctx:
        def sb(name, shape, dt=F32):
            return ctx.enter_context(nc.sbuf_tensor(name, shape, dt))

        def sem(name):
            return ctx.enter_context(nc.semaphore(name))

        hT = sb("hT", [P, DK, TM])
        xh = sb("xh", [P, DK, TM], F32R)
        xl = sb("xl", [P, DK, TM], F32R)
        raw = sb("raw", [P, 2, CH])
        whi = sb("whi", [P, 2, CH], F32R)
        wlo = sb("wlo", [P, 2, CH], F32R)
        rs = sb("rs", [P, TM])
        rt = sb("rt", [P, TM])
        sq = sb("sq", [P, TM])
        ssum = sb("ssum", [P, TM])
        vec = sb("vec", [P, V_ROWS])
        ident = sb("ident", [P, P])
        identr = sb("identr", [P, P], F32R)
        ones = sb("ones", [P, P])
        onesblk = sb("onesblk", [P, P])
        causal = sb("causal", [P, P])
        causalr = sb("causalr", [P, P], F32R)
        strict = sb("strict", [P, P])
        strict01 = sb("strict01", [P, P])
        eps = sb("eps", [P, 1])
        wi = sb("wi", [P, QB, HEADS])
        nmx = sb("nmx", [P, QB * HEADS])
        den = sb("den", [P, QB * HEADS])
        rden = sb("rden", [P, QB * HEADS])
        m8 = sb("m8", [P, 8])
        rtok = sb("rtok", [P, QB])
        fbias = sb("fbias", [8, 1])
        arena_cols = 24784
        start = (nc.sbuf_base + 31) // 32 * 32
        arena = sb("arena", [P, arena_cols])

        def at(name, off, shape, dt=F32):
            n = 1
            for s in shape[1:]:
                n *= s
            assert off + n <= arena_cols, name
            return nc.alloc_sbuf_tensor_at(name, shape, dt, offset=start + 4 * off)

        fh = at("fh", 0, [P, FK, T], F32R)
        fl = at("fl", FK * T, [P, FK, T], F32R)
        tmp = at("tmp", 2 * FK * T, [P, 4, T])
        xt = at("xt", 0, [P, QB, D])
        mt = at("mt", 4096, [META, D])
        vt = at("vt", 5120, [V_ROWS, P])
        cT = at("cT", 0, [P, TM])
        ctok = at("ctok", 528, [P, QB + 1, P])
        qT = at("qT", 1168, [P, HEADS, T])
        ath = at("ath", 1168, [P, HEADS, T], F32R)
        sc = at("sc", 5264, [P, QB, TM])
        ah = at("ah", 7376, [P, 4, T], F32R)
        al = at("al", 9424, [P, 4, T], F32R)
        coh = at("coh", 11472, [P, 4, T], F32R)
        col_ = at("col_", 13520, [P, 4, T], F32R)
        cl = at("cl", 15568, [P, TM])
        kw = at("kw", 16096, [KW, TM])
        kiT = at("kiT", 16624, [P, TM])
        qiT = at("qiT", 17152, [P, 2, T])
        rl = at("rl", 18176, [P, 2, TM])
        rc = at("rc", 19232, [P, TM])
        u = at("u", 19760, [P, 4, TM])
        pooled = at("pooled", 15568, [P, 4, T])
        win = at("win", 17616, [P, 2, TM])
        cc = at("cc", 18672, [P, 4, TM])
        cv = at("cv", 20784, [P, TM])
        cy = at("cy", 21312, [P, 4, T])
        pwt = at("pwt", 23360, [P, 4, P])
        co = at("co", 23872, [P, T])
        msum = at("msum", 15568, [P, DK, T])
        atl = at("atl", 7376, [P, HEADS, T], F32R)
        pT = [at("pT0", 11472, [P, QB + 1, T]), at("pT1", 19664, [P, QB + 1, T])]
        lm = at("lm", 22224, [P, 2, TM])
        pr = at("pr", 23280, [P, 2, TM])
        mh = at("mh", 11472, [P, DK, T], F32R)
        ml = at("ml", 19664, [P, DK, T], F32R)
        tmpb = at("tmpb", 23760, [P, 2, T])
        qF = at("qF", 0, [P, 4, T])
        kF = at("kF", 2048, [P, 4, T])
        qS = at("qS", 4096, [P, 4, T])
        kS = at("kS", 6144, [P, 4, T])
        yfh = at("yfh", 0, [P, 4, T], F32R)
        yfl = at("yfl", 2048, [P, 4, T], F32R)
        ysh = at("ysh", 4096, [P, 4, T], F32R)
        ysl = at("ysl", 6144, [P, 4, T], F32R)
        vF = at("vF", 8192, [P, QB, T])
        vS = at("vS", 10240, [P, QB, T])
        negsel = at("negsel", 12288, [8, HEADS, P])
        fz = at("fz", 13312, [8, T])
        ft = at("ft", 13824, [8, T])
        fF = at("fF", 14336, [8, T])
        fone = at("fone", 14848, [8, T])
        fb = at("fb", 15360, [P, 2, T])
        qs = at("qs", 16384, [P, 2, T])
        rtq = at("rtq", 17408, [P, 2, T])
        flm = at("flm", 18432, [P, 2, T])
        fp = at("fp", 19456, [P, 2, T])
        fpT = [at("fpT0", 20480, [P, QB, T]), at("fpT1", 22528, [P, QB, T])]
        sL = at("sL", 12288, [P, 2, T])
        sR = at("sR", 13312, [P, 2, T])
        m2h = at("m2h", 8192, [P, DK, T], F32R)
        m2l = at("m2l", 12288, [P, DK, T], F32R)
        sg = at("sg", 0, [P, DK, T])
        pTh = at("pTh", 4096, [P, 2, T], F32R)
        pTl = at("pTl", 5120, [P, 2, T], F32R)
        pt = at("pt", 6144, [P, QB, 256])
        ptT = at("ptT", 7168, [P, 2, T])
        ot = at("ot", 8192, [P, QB, D])

        ps = ctx.enter_context(nc.psum_tensor("ps", [P, 8, 512], F32))

        raw_in = [sem("raw_in0"), sem("raw_in1")]
        raw_taken = sem("raw_taken")
        w_hi = sem("w_hi")
        w_lo = sem("w_lo")
        tile_done = sem("tile_done")
        acc_free = sem("acc_free")
        consts, ones_done = sem("consts"), sem("ones_done")
        x_in, vec_in, misc_in = sem("x_in"), sem("vec_in"), sem("misc_in")
        x_turned, x_copied, vec_turned, vec_done = sem("x_turned"), sem("x_copied"), sem("vec_turned"), sem("vec_done")
        sq_done, ssum_done, xh_done, x_split = sem("sq_done"), sem("ssum_done"), sem("xh_done"), sem("x_split")
        ss_done, rt_done, rs_done = sem("ss_done"), sem("rt_done"), sem("rs_done")
        dve_seq = sem("dve_seq")
        act_seq = sem("act_seq")
        ki_rep, wi_turned, wi_done = sem("ki_rep"), sem("wi_turned"), sem("wi_done")
        s_ready, relu_done, score_acc = sem("s_ready"), sem("relu_done"), sem("score_acc")
        csq_done, css_done, crt_done, c_done, c_turned, ctok_done = (
            sem("csq_done"), sem("css_done"), sem("crt_done"), sem("c_done"), sem("c_turned"), sem("ctok_done"))
        pooled_done, mix_done, ah_done, a_split = sem("pooled_done"), sem("mix_done"), sem("ah_done"), sem("a_split")
        co_done, coh_done, co_split = sem("co_done"), sem("coh_done"), sem("co_split")
        sig_done, mul_done, m_done, mh_done, m_split = (
            sem("sig_done"), sem("mul_done"), sem("m_done"), sem("mh_done"), sem("m_split"))
        silu_done, h_done, h_hi, h_split = sem("silu_done"), sem("h_done"), sem("h_hi"), sem("h_split")
        xn_done = sem("xn_done")
        att = {k: {n: sem(f"{k}_{n}") for n in (
            "lg_ready", "lg_read", "exp_done", "p_ready", "pt_ready", "pt_copy_a", "pt_copy_d", "pv_ready", "hi_done",
            "y_split")} for k in ("dsa", "fox", "sb")}
        hq_done, hq_ss, hq_rt, hq_out = sem("hq_done"), sem("hq_ss"), sem("hq_rt"), sem("hq_out")
        rtok_turned, rtok_done = sem("rtok_turned"), sem("rtok_done")
        fz_done, ft_done, f_done, fb_ready, fb_done = (
            sem("fz_done"), sem("ft_done"), sem("f_done"), sem("fb_ready"), sem("fb_done"))
        sp_done, sl_done = sem("sp_done"), sem("sl_done")
        p_in, p_turned, p_copied, ph_done, p_split = (
            sem("p_in"), sem("p_turned"), sem("p_copied"), sem("ph_done"), sem("p_split"))
        o_done, o_turned, o_copied, o_out = sem("o_done"), sem("o_turned"), sem("o_copied"), sem("o_out")

        def bank(c, t):
            return 4 * (c % 2) + 2 * t

        def n_cols(c):
            if c == C_LAT:
                return DK * (P + KW)
            if c == C_FL:
                return DK * HEADS
            for d in C_D:
                if d <= c < d + 12 and (c - d) % 3 == 2:
                    return DOWN_K[2] * CW
            return CH

        def raw_level(c, per, i):
            return lin(32 * (c // 2 + 1), 16 * per, i)

        kin = "(k p) n -> p k n"
        w1 = I["w_in"][0].rearrange(kin, p=P)
        w2 = I["w_in_2"][0].rearrange(kin, p=P)

        block = ctx.enter_context(nc.Block())

        @block.sync
        def _(sp):
            def slot(c, k, w):
                return raw[:, c % 2, 0:k * w].rearrange("p (k n) -> p k n", k=k)

            def load(c, parts, per=0, i=None):
                if c >= 2:
                    sp.wait_ge(w_lo, lin(c - 1, per, i))
                    sp.sem_inc(raw_taken, 1)
                for dst, src in parts:
                    sp.dma_start(dst, src).then_inc(raw_in[c % 2], 16)

            def square(c, w, at_col, per=0, i=None):
                s = slot(c, DK, CW)
                sel = slice(at_col, at_col + CW) if isinstance(at_col, int) else bass.ds(sp.snap(at_col), CW)
                load(c, [(s[:, 0:4], w[:, 0:4, sel]), (s[:, 4:8], w[:, 4:8, sel])], per, i)

            def two(c, wa, wb, at_col, per, i):
                s = slot(c, DK, CW)
                sel = bass.ds(sp.snap(at_col), CW)
                load(c, [(s[:, 0:4], wa[:, :, sel]), (s[:, 4:8], wb[:, :, sel])], per, i)

            def ffn(f, gate, up, down):
                with sp.Fori(0, FK // 2) as i:
                    for j in range(2):
                        c = C_F[f] + j
                        s = slot(c, DK, CW)
                        sel = bass.ds(sp.snap(i * CW + P * j), P)
                        load(c, [(s[:, :, 0:P], gate[:, :, sel]), (s[:, :, P:CW], up[:, :, sel])], 2, i)
                with sp.Fori(0, 2) as i:
                    for j in range(2):
                        sel = bass.ds(sp.snap(i * (2 * CW) + j * CW), CW)
                        for r, kn in enumerate(DOWN_K):
                            c = C_D[f] + 3 * j + r
                            s = slot(c, kn, CW)
                            k0, hk = sum(DOWN_K[:r]), kn // 2
                            load(c, [(s[:, 0:hk], down[:, k0:k0 + hk, sel]),
                                     (s[:, hk:kn], down[:, k0 + hk:k0 + kn, sel])], 6, i)

            s = slot(C_LAT, DK, P + KW)
            load(C_LAT, [(s[:, :, 0:P], w1[:, :, O_C:O_C + P]), (s[:, :, P:P + KW], w1[:, :, O_KI:O_KI + KW])])
            square(C_QI, w1, O_QI)
            for c0, o, n in ((C_Q, O_Q, 4), (C_U, O_U, 2), (C_CC, O_CC, 2), (C_CU, O_CU, 2), (C_CB, O_CB, 2)):
                for j in range(n):
                    square(c0 + j, w1, o + CW * j)
            wa = I["w_a"][0].rearrange(kin, p=P)
            wc = I["w_c"][0].rearrange(kin, p=P)
            with sp.Fori(0, 2) as i:
                for q in range(2):
                    c = C_AC + 3 * q
                    square(c, w1, i * (2 * CW) + (O_G + CW * q), 6, i)
                    square(c + 1, w1, i * (2 * CW) + (O_G + 2 * D + CW * q), 6, i)
                    two(c + 2, wa, wc, i * (2 * CW) + CW * q, 6, i)
            wb = I["w_b"][0].rearrange(kin, p=P)
            with sp.Fori(0, 4) as i:
                square(C_B, w1, i * CW + (O_G + D), 2, i)
                square(C_B + 1, wb, i * CW, 2, i)
            wo = I["w_o"][0].rearrange(kin, p=P)
            with sp.Fori(0, 2) as i:
                for j in range(2):
                    square(C_O + j, wo, i * (2 * CW) + CW * j, 2, i)
            gu = I["w_gate_up"][0].rearrange(kin, p=P)
            ffn(0, gu[:, :, 0:D_FF], gu[:, :, D_FF:2 * D_FF], I["w_down"][0].rearrange(kin, p=P))
            ffn(1, I["ffn1_w_gate_2"][0].rearrange(kin, p=P), I["ffn1_w_up_2"][0].rearrange(kin, p=P),
                I["ffn1_w_down_2"][0].rearrange(kin, p=P))
            for c0, o in ((C_FQ, S_FQ), (C_FK, S_FK), (C_FV, S_FV)):
                for j in range(2):
                    square(c0 + j, w2, o + CW * j)
            s = slot(C_FL, DK, HEADS)
            load(C_FL, [(s[:, 0:4], w2[:, 0:4, S_FL:S_FL + HEADS]), (s[:, 4:8], w2[:, 4:8, S_FL:S_FL + HEADS])])
            for c0, o in ((C_SQ, S_SQ), (C_SK, S_SK), (C_SV, S_SV)):
                for j in range(2):
                    square(c0 + j, w2, o + CW * j)
            wf = I["w_branch_fox_2"][0].rearrange(kin, p=P)
            ws = I["w_branch_sb_2"][0].rearrange(kin, p=P)
            with sp.Fori(0, 2) as i:
                for q in range(2):
                    c = C_MX + 3 * q
                    square(c, w2, i * (2 * CW) + (S_GF + CW * q), 6, i)
                    square(c + 1, w2, i * (2 * CW) + (S_GS + CW * q), 6, i)
                    two(c + 2, wf, ws, i * (2 * CW) + CW * q, 6, i)
            wo2 = I["w_out_2"][0].rearrange(kin, p=P)
            with sp.Fori(0, 2) as i:
                for j in range(2):
                    square(C_O2 + j, wo2, i * (2 * CW) + CW * j, 2, i)
            ffn(2, I["ffn2_w_gate_2"][0].rearrange(kin, p=P), I["ffn2_w_up_2"][0].rearrange(kin, p=P),
                I["ffn2_w_down_2"][0].rearrange(kin, p=P))
            wg = I["w_ple_gate_2"][0].rearrange(kin, p=P)
            for j in range(4):
                square(C_PG + j, wg, CW * j)
                if j == 0:
                    sp.wait_ge(tile_done, 2 * C_PG)
                    sp.dma_start(pt[:], I["p_2"][0, 0].rearrange("(b p) d -> p b d", p=P)).then_inc(p_in, 16)
            wp = I["w_ple_proj_2"][0].rearrange(kin, p=P)
            s = slot(C_PP, 2, D)
            load(C_PP, [(s[:, 0:1], wp[:, 0:1]), (s[:, 1:2], wp[:, 1:2])])
            for n in range(DK):
                sp.wait_ge(o_copied, n + 1)
                sp.dma_start(out[0].rearrange("(b p) d -> p b d", p=P)[:, :, P * n:P * n + P],
                             ot[:, :, P * n:P * n + P]).then_inc(o_out, 16)
            sp.wait_ge(o_out, 16 * DK)

        @block.gpsimd
        def _(pool):
            pool.memset(ident[:], 0.0).then_inc(consts, 1)
            pool.memset(causal[:], 0.0).then_inc(consts, 1)
            pool.memset(strict[:], 0.0).then_inc(consts, 1)
            pool.memset(strict01[:], 1.0).then_inc(consts, 1)
            pool.memset(onesblk[:], 0.0).then_inc(consts, 1)
            pool.wait_ge(consts, 5)
            tri = dict(pattern=[[-1, P]], channel_multiplier=1)
            pool.affine_select(out=ident[:], in_=ident[:], compare_op=ALU.not_equal, fill=1.0, base=0, **tri).then_inc(consts, 1)
            pool.affine_select(out=causal[:], in_=causal[:], compare_op=ALU.is_ge, fill=NEG, base=0, **tri).then_inc(consts, 1)
            pool.affine_select(out=strict[:], in_=strict[:], compare_op=ALU.is_ge, fill=NEG, base=-1, **tri).then_inc(consts, 1)
            pool.affine_select(out=strict01[:], in_=strict01[:], compare_op=ALU.is_ge, fill=0.0, base=-1, **tri).then_inc(consts, 1)
            for z, o in enumerate((0, HEAD_DIM)):
                pool.wait_ge(consts, 9 + z)
                pool.memset(onesblk[o:o + HEAD_DIM, o:o + HEAD_DIM], 1.0).then_inc(consts, 1)

            def low(c, per=0, i=None):
                n = n_cols(c)
                pool.wait_ge(w_hi, lin(c + 1, per, i))
                pool.tensor_tensor(wlo[:, c % 2, 0:n], raw[:, c % 2, 0:n], whi[:, c % 2, 0:n].bitcast(F32),
                                   ALU.subtract).then_inc(w_lo, 1)

            def run(c0, c1, body):
                with pool.Fori(0, (c1 - c0) // body) as i:
                    for j in range(body):
                        low(c0 + j, body, i)

            pool.wait_ge(consts, 11)
            low(C_LAT)
            low(C_QI)
            run(C_Q, C_D[0], 2)
            run(C_D[0], C_F[1], 6)
            run(C_F[1], C_D[1], 2)
            run(C_D[1], C_FQ, 6)
            run(C_FQ, C_FL, 2)
            pool.wait_ge(tile_done, 2 * C_FQ)
            pool.memset(negsel[:], 0.0).then_inc(consts, 1)
            pool.memset(fone[:], 1.0).then_inc(consts, 1)
            pool.wait_ge(consts, 13)
            pool.affine_select(out=negsel[:], in_=negsel[:], compare_op=ALU.not_equal, fill=-1.0, base=0,
                               pattern=[[-1, HEADS], [0, P]], channel_multiplier=1).then_inc(consts, 1)
            low(C_FL)
            run(C_SQ, C_D[2], 2)
            run(C_D[2], C_PG, 6)
            run(C_PG, C_PP, 2)
            low(C_PP)

        @block.tensor
        def _(pe):
            def passes(o, s, w_of, xhi, xlo, first, last):
                pe.matmul(o, w_of(whi), xhi, start=first, stop=False)
                pe.matmul(o, w_of(whi), xlo, start=False, stop=False)
                return pe.matmul(o, w_of(wlo), xhi, start=False, stop=last)

            def x_ready(X, k, t):
                if t == 0:
                    pe.wait_ge(x_split, DK * X + k + 1)

            def chunk(c, hi, lo, per=0, i=None, X=None, full=(False, False), widths=(P, P), between=None):
                s, w = c % 2, sum(widths)
                pe.wait_ge(w_lo, lin(c + 1, per, i))
                for t in range(2):
                    if c >= 2:
                        pe.wait_ge(acc_free, lin(2 * (c - 2) + t + 1, 2 * per, i))
                    b, m, o0 = bank(c, t), widths[t], sum(widths[:t])
                    for k in range(DK):
                        if X is not None:
                            x_ready(X, k, t)
                        w_of = lambda wt: wt[:, s, w * k + o0:w * k + o0 + m]
                        if full[t]:
                            for z in range(2):
                                cs = slice(HALF * z, HALF * z + HALF)
                                mm = passes(ps[0:m, b + z, 0:HALF], s, w_of, hi[:, k, cs], lo[:, k, cs], k == 0, k == DK - 1)
                        else:
                            cs = slice(0, T) if hi.shape[2] == T else slice(META, TM)
                            mm = passes(ps[0:m, b, :], s, w_of, hi[:, k, cs], lo[:, k, cs], k == 0, k == DK - 1)
                    mm.then_inc(tile_done, 1)
                    if t == 0 and between:
                        between()

            def norm_sums(S, c):
                pe.wait_ge(ssum_done, 9 * (S + 1))
                if S == 0:
                    for z in range(2):
                        mm = pe.matmul(ps[:, 6 + z, 0:HALF], ones[:], ssum[:, HALF * z:HALF * z + HALF], start=True, stop=True)
                else:
                    mm = pe.matmul(ps[:, bank(c + 1, 0) + 1, :], ones[:], ssum[:, META:TM], start=True, stop=True)
                mm.then_inc(ss_done, 1)

            def pair(c, hi_a, lo_a, hi_b, lo_b, per, i):
                s = c % 2
                pe.wait_ge(w_lo, lin(c + 1, per, i))
                for t in range(2):
                    pe.wait_ge(acc_free, lin(2 * (c - 2) + t + 1, 2 * per, i))
                    for z, (h, l) in enumerate(((hi_a, lo_a), (hi_b, lo_b))):
                        for k in range(4):
                            o = CW * (4 * z + k) + P * t
                            mm = passes(ps[:, bank(c, t) + z, :], s, lambda wt: wt[:, s, o:o + P],
                                        h[:, k, :], l[:, k, :], k == 0, k == 3)
                    mm.then_inc(tile_done, 1)

            def ffn(f, S, X):
                c = C_F[f]
                chunk(c, xh, xl, X=X, between=lambda: norm_sums(S, c))
                chunk(c + 1, xh, xl)
                with pe.Fori(0, FK // 2 - 1) as i:
                    for j in range(2):
                        chunk(c + 2 + j, xh, xl, 2, i)
                c = C_D[f]
                with pe.Fori(0, 2) as i:
                    for j in range(2):
                        for r, kn in enumerate(DOWN_K):
                            cr, k0 = c + 3 * j + r, sum(DOWN_K[:r])
                            pe.wait_ge(w_lo, lin(cr + 1, 6, i))
                            if j == 0:
                                pe.wait_ge(h_split, FK * f + k0 + kn)
                            for t in range(2):
                                if r == 0:
                                    pe.wait_ge(acc_free, lin(2 * (c - 2 + j) + t + 1, 4 * j + 2 * t + 6, i))
                                for k in range(kn):
                                    o = CW * k + P * t
                                    mm = passes(ps[:, bank(c + j, t), :], cr % 2, lambda wt: wt[:, cr % 2, o:o + P],
                                                fh[:, k0 + k, :], fl[:, k0 + k, :], r == 0 and k == 0, r == 2 and k == kn - 1)
                                mm.then_inc(tile_done, 1)

            pe.wait_ge(consts, 11)
            pe.wait_ge(x_in, 32)
            for n in range(DK):
                b = 2 * (n % 4)
                if n >= 4:
                    pe.wait_ge(x_copied, 2 * (n - 3))
                for q in range(QB):
                    pe.transpose(ps[:, b, P * q:P * q + P], xt[:, q, P * n:P * n + P], ident[:])
                pe.transpose(ps[:, b + 1, 0:META], mt[:, P * n:P * n + P], ident[0:META, 0:META]).then_inc(x_turned, 1)
                if n == 3:
                    pe.wait_ge(vec_in, 16 * 15)
                    pe.wait_ge(x_copied, 2)
                    pe.transpose(ps[:, 0, 0:V_ROWS], vt[:], ident[0:V_ROWS, 0:V_ROWS]).then_inc(vec_turned, 1)
                    pe.wait_ge(vec_done, 1)

            pe.wait_ge(x_copied, 2 * DK)
            chunk(C_LAT, xh, xl, X=0, full=(True, True), widths=(P, KW), between=lambda: norm_sums(0, C_LAT))
            chunk(C_QI, xh, xl, between=lambda: pe.wait_ge(rt_done, 1))
            chunk(C_Q, xh, xl)
            pe.wait_ge(acc_free, 2)
            for q in range(QB):
                mm = pe.transpose(ps[:, 1, HEADS * q:HEADS * q + HEADS], kw[D_IDX:KW, META + P * q:META + P * q + P],
                                  ident[D_IDX:KW, D_IDX:KW])
            mm.then_inc(wi_turned, 1)
            pe.wait_ge(ki_rep, 64)
            pe.wait_ge(acc_free, 2 * C_QI + 2)
            pe.wait_ge(wi_done, 1)
            for n in range(QB * HEADS):
                q, h = divmod(n, HEADS)
                wq = (META + P * (q + 1)) // 2
                g = D_IDX * (h % 4)
                if n >= 2:
                    pe.wait_ge(relu_done, n - 1)
                for z in range(2):
                    mm = pe.matmul(ps[:, 4 + 2 * (n % 2) + z, 0:wq], qiT[g:g + D_IDX, h // 4, P * q:P * q + P],
                                   kiT[g:g + D_IDX, wq * z:wq * z + wq], start=True, stop=True)
                mm.then_inc(s_ready, 1)
            pe.wait_ge(csq_done, 1)
            pe.wait_ge(acc_free, 2 * C_Q + 1)
            for z in range(2):
                mm = pe.matmul(ps[:, z, 0:HALF], ones[:], sq[:, HALF * z:HALF * z + HALF], start=True, stop=True)
            mm.then_inc(css_done, 1)
            pe.wait_ge(relu_done, QB * HEADS)
            chunk(C_Q + 1, xh, xl)
            pe.wait_ge(c_done, 1)
            for q in range(QB):
                pe.transpose(ps[:, 5, P * q:P * q + P], cT[:, META + P * q:META + P * q + P], ident[:])
            pe.transpose(ps[0:META, 7, 0:P], cT[:, 0:META], ident[:]).then_inc(c_turned, 1)
            chunk(C_Q + 2, xh, xl)
            chunk(C_Q + 3, xh, xl)
            pe.wait_ge(ctok_done, 2)
            for c in range(C_U, C_CB):
                chunk(c, xh, xl, full=(True, True))
            chunk(C_CB, xh, xl)
            pe.wait_ge(misc_in, 32)
            pe.wait_ge(acc_free, 2 * C_CB)
            for g in range(4):
                pe.wait_ge(pooled_done, g + 1)
                pe.matmul(ps[:, 2 * g + 1, :], pwt[:, g, :], pooled[:, g, :], start=True, stop=True).then_inc(mix_done, 1)
            chunk(C_CB + 1, xh, xl)

            pe.wait_ge(a_split, 4)
            with pe.Fori(0, 2) as i:
                for q in range(2):
                    c = C_AC + 3 * q
                    chunk(c, xh, xl, 6, i)
                    chunk(c + 1, xh, xl, 6, i)
                    if q == 0:
                        pe.wait_ge(co_split, 4)
                    pair(c + 2, ah, al, coh, col_, 6, i)

            def attention(A, units, scores, key_tiles, value, bank_left):
                def qk(n):
                    if n >= 2:
                        pe.wait_ge(A["lg_read"], n - 1)
                    scores(n).then_inc(A["lg_ready"], 1)

                qk(0)
                qk(1)
                for n in range(units + 1):
                    if n + 2 < units:
                        qk(n + 2)
                    if n < units:
                        h, q = divmod(n, QB)
                        pe.wait_ge(A["p_ready"], n + 1)
                        if n >= 1:
                            pe.wait_ge(A["pt_copy_a"], n)
                            pe.wait_ge(A["pt_copy_d"], n)
                        key_tiles(n, q).then_inc(A["pt_ready"], 1)
                    if n % QB == 0 and n:
                        h = n // QB - 1
                        pe.wait_ge(A["pt_copy_a"], n)
                        pe.wait_ge(A["pt_copy_d"], n)
                        bank_left(h)
                        value(h).then_inc(A["pv_ready"], 1)

            A = att["dsa"]
            pe.wait_ge(acc_free, 2 * C_B)

            def dsa_scores(n):
                h, q = divmod(n, QB)
                w = META + P * (q + 1)
                b = 2 * (n % 2)
                mm = pe.matmul(ps[:, b, 0:min(w, 512)], qT[:, h, P * q:P * q + P], cT[:, 0:min(w, 512)], start=True, stop=True)
                if w > 512:
                    mm = pe.matmul(ps[:, b + 1, 0:w - 512], qT[:, h, P * q:P * q + P], cT[:, 512:w], start=True, stop=True)
                return mm

            def dsa_turn(n, q):
                src = pr[:, n % 2]
                for j in range(q + 1):
                    pe.transpose(ps[:, 4, P * j:P * j + P], src[:, META + P * j:META + P * j + P], ident[:])
                return pe.transpose(ps[0:META, 5, 0:P], src[:, 0:META], ident[:])

            def dsa_value(h):
                o, p = ps[:, 6 + h % 2, :], pT[h % 2]
                pe.matmul(o, ctok[0:META, QB, :], p[0:META, QB, :], start=True, stop=False)
                for j in range(QB):
                    mm = pe.matmul(o[:, P * j:T], ctok[:, j, :], p[:, j, P * j:T], start=False, stop=j == QB - 1)
                return mm

            def dsa_split(h):
                if h >= 2:
                    pe.wait_ge(A["y_split"], h - 1)

            attention(A, QB * HEADS, dsa_scores, dsa_turn, dsa_value, dsa_split)

            pe.wait_ge(A["y_split"], HEADS)
            with pe.Fori(0, 4) as i:
                chunk(C_B, xh, xl, 2, i)
                chunk(C_B + 1, ath, atl, 2, i)
            pe.wait_ge(m_split, DK)
            with pe.Fori(0, 2) as i:
                for j in range(2):
                    chunk(C_O + j, mh, ml, 2, i)
            ffn(0, 1, 1)
            norm_sums(2, C_F[1])

            ffn(1, 3, 2)
            chunk(C_FQ, xh, xl, X=3, between=lambda: norm_sums(4, C_FQ))

            def head_sums(n):
                pe.wait_ge(hq_done, n + 1)
                if n >= 2:
                    pe.wait_ge(hq_rt, n - 1)
                pe.matmul(ps[:, 5 + 2 * (n % 2), :], onesblk[:], rtq[:, n % 2, :], start=True, stop=True).then_inc(hq_ss, 1)

            chunk(C_FQ + 1, xh, xl)
            pe.wait_ge(rs_done, 5)
            for q in range(QB):
                mm = pe.transpose(ps[:, 1, P * q:P * q + P], rs[:, META + P * q:META + P * q + P], ident[:])
            mm.then_inc(rtok_turned, 1)
            head_sums(0)
            head_sums(1)
            for n, c in ((2, C_FK), (4, C_FK + 1)):
                chunk(c, xh, xl)
                head_sums(n)
                head_sums(n + 1)

            def tokens(c):
                s = c % 2
                pe.wait_ge(w_lo, c + 1)
                for t in range(2):
                    pe.wait_ge(acc_free, 2 * (c - 2) + t + 1)
                    for z in range(2):
                        q = 2 * t + z
                        o = ps[:, bank(c, t), CW * z:CW * z + CW]
                        for k in range(DK):
                            th, tl = (x[:, k, META + P * q:META + P * q + P] for x in (xh, xl))
                            ch, clo = (wt[:, s, CW * k:CW * k + CW] for wt in (whi, wlo))
                            pe.matmul(o, th, ch, start=k == 0, stop=False)
                            pe.matmul(o, th, clo, start=False, stop=False)
                            mm = pe.matmul(o, tl, ch, start=False, stop=k == DK - 1)
                    mm.then_inc(tile_done, 1)

            tokens(C_FV)
            head_sums(6)
            head_sums(7)
            tokens(C_FV + 1)
            pe.wait_ge(w_lo, C_FL + 1)
            pe.wait_ge(acc_free, 2 * (C_FL - 2) + 1)
            for k in range(DK):
                mm = passes(ps[0:HEADS, bank(C_FL, 0), :], 0, lambda wt: wt[:, C_FL % 2, HEADS * k:HEADS * k + HEADS],
                            xh[:, k, META:TM], xl[:, k, META:TM], k == 0, k == DK - 1)
            mm.then_inc(tile_done, 2)
            for c in range(C_SQ, C_SV):
                chunk(c, xh, xl)
            tokens(C_SV)
            tokens(C_SV + 1)

            F = att["fox"]
            pe.wait_ge(acc_free, 2 * C_MX)
            pe.wait_ge(hq_out, 8)
            pe.wait_ge(consts, 14)

            def row(h):
                return HEAD_DIM * (h % 2)

            def fox_scores(n):
                h, q = divmod(n, QB)
                w, r = P * (q + 1), row(h)
                if q == 0:
                    if h == 0:
                        pe.wait_ge(f_done, 1)
                    else:
                        pe.wait_ge(fb_done, h)
                    pe.matmul(ps[:, 1, :], negsel[:, h, :], fF[:], start=True, stop=True).then_inc(fb_ready, 1)
                b = 2 * (n % 2)
                pe.matmul(ps[:, b, 0:w], qF[r:r + HEAD_DIM, h // 2, P * q:P * q + P], kF[r:r + HEAD_DIM, h // 2, 0:w],
                          start=True, stop=False, skip_group_check=True)
                return pe.matmul(ps[:, b, P * q:w], identr[:], causalr[:], start=False, stop=True, skip_group_check=True)

            def fox_turn(n, q):
                for j in range(q + 1):
                    mm = pe.transpose(ps[:, 4, P * j:P * j + P], fp[:, n % 2, P * j:P * j + P], ident[:])
                return mm

            def values(v, h):
                o, p, r = ps[row(h):row(h) + HEAD_DIM, 6 + (h // 2) % 2, :], fpT[h % 2], row(h)
                for j in range(QB):
                    mm = pe.matmul(o[:, P * j:T], v[:, j, HEAD_DIM * h:HEAD_DIM * h + HEAD_DIM], p[:, j, P * j:T],
                                   start=j == 0, stop=j == QB - 1)
                return mm

            def pair_split(A):
                def wait(h):
                    if h >= 4:
                        pe.wait_ge(A["y_split"], h // 2 - 1)
                return wait

            attention(F, QB * HEADS, fox_scores, fox_turn, lambda h: values(vF, h), pair_split(F))

            B = att["sb"]
            pe.wait_ge(F["y_split"], 4)

            def sb_scores(n):
                h, q = divmod(n, QB)
                w, r = P * (q + 1), row(h)
                return pe.matmul(ps[:, n % 2 * 2, 0:w], qS[r:r + HEAD_DIM, h // 2, P * q:P * q + P],
                                 kS[r:r + HEAD_DIM, h // 2, 0:w], start=True, stop=True)

            attention(B, QB * HEADS, sb_scores, fox_turn, lambda h: values(vS, h), pair_split(B))

            pe.wait_ge(B["y_split"], 4)
            with pe.Fori(0, 2) as i:
                for q in range(2):
                    c = C_MX + 3 * q
                    chunk(c, xh, xl, 6, i)
                    chunk(c + 1, xh, xl, 6, i)
                    pair(c + 2, yfh, yfl, ysh, ysl, 6, i)
            pe.wait_ge(m_split, 2 * DK)
            with pe.Fori(0, 2) as i:
                for j in range(2):
                    chunk(C_O2 + j, m2h, m2l, 2, i)
            ffn(2, 5, 4)

            chunk(C_PG, xh, xl, X=5, between=lambda: norm_sums(6, C_PG))
            chunk(C_PG + 1, xh, xl)
            pe.wait_ge(p_in, 16)
            pe.wait_ge(rs_done, 7)
            for j in range(2):
                for q in range(QB):
                    mm = pe.transpose(ps[:, 1 + 2 * j, P * q:P * q + P], pt[:, q, P * j:P * j + P], ident[:])
                mm.then_inc(p_turned, 1)
            chunk(C_PG + 2, xh, xl)
            chunk(C_PG + 3, xh, xl)
            pe.wait_ge(p_split, 2)
            pe.wait_ge(w_lo, C_PP + 1)
            for n in range(DK):
                if n >= 4:
                    pe.wait_ge(acc_free, 2 * C_PP + n - 3)
                for k in range(2):
                    o = D * k + P * n
                    mm = passes(ps[:, 2 * (n % 4) + 1, :], 0, lambda wt: wt[:, C_PP % 2, o:o + P],
                                pTh[:, k, :], pTl[:, k, :], k == 0, k == 1)
                mm.then_inc(tile_done, 1)
            pe.wait_ge(acc_free, 2 * C_PP)
            for n in range(DK):
                pe.wait_ge(o_done, n + 1)
                if n >= 4:
                    pe.wait_ge(o_copied, n - 3)
                for q in range(QB):
                    mm = pe.transpose(ps[:, 2 * (n % 4), P * q:P * q + P], hT[:, n, META + P * q:META + P * q + P], ident[:])
                mm.then_inc(o_turned, 1)

        @block.scalar
        def _(act):
            act.dma_start(xt[:], I["x"][0].rearrange("(b p) d -> p b d", p=P)).then_inc(x_in, 16)
            act.dma_start(mt[:], I["meta"]).then_inc(x_in, 16)
            for r0, a in ((V_N1, "norm1_g"), (V_N2, "norm2_g"), (V_FIN, "final_g"), (V_F1, "ffn1_norm_2"), (V_MX, "mix_norm_2"),
                          (V_F2, "ffn2_norm_2"), (V_PL, "ple_norm_2"), (V_BG, "b_gate"), (V_PS, "pool_scale"), (V_KV, "kv_norm_g")):
                a = I[a] if len(I[a].shape) == 1 else I[a][0]
                n = a.shape[0] // P
                act.dma_start(vt[r0:r0 + n, :], a.rearrange("(r c) -> r c", c=P)).then_inc(vec_in, 16)
            act.dma_start(vt[V_CW:V_CW + 12, :], I["conv_w"][0].rearrange("w (r c) -> (w r) c", c=P)).then_inc(vec_in, 16)
            for r0, a in ((V_QN, "q_norm_2"), (V_KN, "k_norm_2")):
                for z in range(2):
                    act.dma_start(vt[r0:r0 + 1, HEAD_DIM * z:HEAD_DIM * z + HEAD_DIM], I[a]).then_inc(vec_in, 16)

            def high(c, per=0, i=None):
                n = n_cols(c)
                act.wait_ge(raw_in[c % 2], raw_level(c, per, i))
                if c >= 2:
                    act.wait_ge(tile_done, lin(2 * (c - 1), 2 * per, i))
                act.activation(whi[:, c % 2, 0:n], raw[:, c % 2, 0:n], ACT.Copy).then_inc(w_hi, 1)

            def feed(S, X, n, gain, per=0, i=None, lo=META):
                nn = lin(n, per, i)
                if S or n:
                    act.wait_ge(ssum_done, lin(9 * S + n + (1 if n else 0), per, i))
                act.activation(sq[:, lo:TM], one(hT, nn)[:, lo:TM], ACT.Square).then_inc(sq_done, 1)
                if X is not None:
                    act.activation(one(xh, nn)[:, lo:TM], one(hT, nn)[:, lo:TM], ACT.Copy,
                                   scale=col(vec, lin(gain + n, per, i))).then_inc(xh_done, 1)

            def root(S):
                act.wait_ge(ss_done, S + 1)
                if S == 0:
                    act.activation(rt[:].rearrange("p (z t) -> p z t", z=2), ps[:, 6:8, 0:HALF], ACT.Sqrt,
                                   bias=eps[:], scale=1.0 / D).then_inc(rt_done, 1)
                else:
                    c = {1: C_F[0], 2: C_F[1], 3: C_F[1], 4: C_FQ, 5: C_F[2], 6: C_PG}[S]
                    act.activation(rt[:, META:TM], ps[:, bank(c + 1, 0) + 1, :], ACT.Sqrt,
                                   bias=eps[:], scale=1.0 / D).then_inc(rt_done, 1)

            def ffn(f, S, S_next, X_next, gain):
                c = C_F[f]

                def up(c, n, per=0, i=None):
                    act.wait_ge(acc_free, lin(2 * c + 1, 2 * per, i))
                    act.activation(tmp[:, 1, :], tmp[:, 0, :], ACT.Silu).then_inc(silu_done, 1)
                    high(c + 2, per, i)
                    act.wait_ge(h_done, lin(FK * f + n + 1, per, i))
                    act.activation(one(fh, lin(n, per, i)), tmp[:, 3, :], ACT.Copy).then_inc(h_hi, 1)

                root(S)
                with act.Fori(0, FK // 2) as i:
                    for j in range(2):
                        up(c + j, j, 2, i)
                d = C_D[f]
                with act.Fori(0, 2) as i:
                    for j in range(2):
                        high(d + 3 * j + 2, 6, i)
                        high(d + 3 * j + 3, 6, i)
                        act.wait_ge(acc_free, lin(2 * d + 6 * j + 3, 12, i))
                        feed(S_next, X_next, 2 * j, gain, 4, i)
                        high(d + 3 * j + 4, 6, i)
                        act.wait_ge(acc_free, lin(2 * d + 6 * j + 6, 12, i))
                        feed(S_next, X_next, 2 * j + 1, gain, 4, i)

            def project(c, S, X, gain):
                with act.Fori(0, 2) as i:
                    for j in range(2):
                        act.wait_ge(acc_free, lin(2 * (c + j) + 1, 4, i))
                        feed(S, X, 2 * j, gain, 4, i)
                        high(c + j + 2, 2, i)
                        act.wait_ge(acc_free, lin(2 * (c + j) + 2, 4, i))
                        feed(S, X, 2 * j + 1, gain, 4, i)

            high(0)
            high(1)
            for n in range(DK):
                act.wait_ge(x_turned, n + 1)
                act.activation(hT[:, n, META:TM], ps[:, 2 * (n % 4), :], ACT.Copy).then_inc(x_copied, 1)
                act.activation(hT[:, n, 0:META], ps[:, 2 * (n % 4) + 1, 0:META], ACT.Copy).then_inc(x_copied, 1)
                if n == 3:
                    act.wait_ge(vec_turned, 1)
                    act.activation(vec[:], ps[:, 0, 0:V_ROWS], ACT.Copy).then_inc(vec_done, 1)
            act.wait_ge(vec_done, 1)
            act.wait_ge(x_copied, 2 * DK)
            for n in range(DK):
                feed(0, 0, n, V_N1, lo=0)
            act.wait_ge(ones_done, 1)
            root(0)
            high(C_LAT + 2)
            act.wait_ge(acc_free, 2 * C_LAT + 2)
            for g in range(4):
                act.dma_start(kiT[D_IDX * g:D_IDX * g + D_IDX, :], kw[0:D_IDX, :]).then_inc(ki_rep, 16)
            act.activation(sq[:], cl[:], ACT.Square).then_inc(csq_done, 1)
            high(C_QI + 2)
            high(C_Q + 2)
            for n in range(QB * HEADS):
                q = n // HEADS
                wq = (META + P * (q + 1)) // 2
                act.wait_ge(s_ready, n + 1)
                if n >= 2:
                    act.wait_ge(score_acc, n - 1)
                b = 4 + 2 * (n % 2)
                act.activation(rl[:, n % 2, 0:2 * wq].rearrange("p (z k) -> p z k", z=2), ps[:, b:b + 2, 0:wq],
                               ACT.Relu).then_inc(relu_done, 1)
            act.wait_ge(css_done, 1)
            act.activation(rt[:].rearrange("p (z t) -> p z t", z=2), ps[:, 0:2, 0:HALF], ACT.Sqrt,
                           bias=eps[:], scale=1.0 / D_LAT).then_inc(crt_done, 1)
            high(C_Q + 3)
            act.wait_ge(c_turned, 1)
            act.activation(ctok[:, 0:QB, :].rearrange("p q d -> p (q d)"), ps[:, 5, :], ACT.Copy).then_inc(ctok_done, 1)
            act.activation(ctok[0:META, QB, :], ps[0:META, 7, 0:P], ACT.Copy).then_inc(ctok_done, 1)
            act.dma_start(pwt[:], I["pool_w"][0].rearrange("g c d -> c g d")).then_inc(misc_in, 16)
            act.dma_start(fbias[:], I["forget_bias_2"][0].rearrange("(h o) -> h o", o=1)).then_inc(misc_in, 16)
            for c in range(C_Q + 2, C_CB):
                high(c + 2)
            high(C_CB + 2)
            for g in range(2):
                act.wait_ge(co_done, g + 1)
                act.activation(coh[:, g, :], co[:], ACT.Copy).then_inc(coh_done, 1)
            for g in range(4):
                act.wait_ge(mix_done, g + 1)
                act.activation(ah[:, g, :], ps[:, 2 * g + 1, :], ACT.Copy, scale=col(vec, V_PS + g)).then_inc(ah_done, 1)
            high(C_CB + 3)
            for g in range(2, 4):
                act.wait_ge(co_done, g + 1)
                act.activation(coh[:, g, :], co[:], ACT.Copy).then_inc(coh_done, 1)

            def gate(c, kind, q, bias, per, i):
                for t in range(2):
                    act.wait_ge(acc_free, lin(2 * c + t + 1, 2 * per, i))
                    g = tmp[:, 2 * kind + t, :]
                    b = {} if bias is None else {"bias": col(vec, lin(bias + 2 * q + t, 4, i))}
                    act.activation(g, g, ACT.Sigmoid, **b).then_inc(sig_done, 1)

            with act.Fori(0, 2) as i:
                for q in range(2):
                    c = C_AC + 3 * q
                    high(c + 2, 6, i)
                    gate(c, 0, q, V_BG, 6, i)
                    high(c + 3, 6, i)
                    gate(c + 1, 1, q, V_BG + 2 * DK, 6, i)
                    high(c + 4, 6, i)

            def softmax_units(A, src, dst, turned, before=None, split=None):
                for n in range(QB * HEADS + 1):
                    if n < QB * HEADS:
                        h, q = divmod(n, QB)
                        w = src(n)[1]
                        if before:
                            before(n)
                        act.wait_ge(A["lg_read"], n + 1)
                        if n >= 2:
                            act.wait_ge(A["pt_ready"], n - 1)
                        act.activation(dst[:, n % 2, 0:w], src(n)[0], ACT.Exp, bias=nmx[:, n:n + 1], scale=-1.0,
                                       accum_out=den[:, n:n + 1]).then_inc(A["exp_done"], 1)
                    if n >= 1:
                        copy_turned(A, n - 1, turned)
                    if n >= 2 and (n - 2) % QB == QB - 1 and split:
                        split((n - 2) // QB)
                if split:
                    split(HEADS - 1)

            def copy_turned(A, n, turned):
                h, q = divmod(n, QB)
                act.wait_ge(A["pt_ready"], n + 1)
                if h >= 2:
                    act.wait_ge(A["pv_ready"], h - 1)
                act.activation(turned[h % 2][:, 0:q + 1, P * q:P * q + P],
                               ps[:, 4, 0:P * (q + 1)].rearrange("p (j t) -> p j t", j=q + 1), ACT.Copy).then_inc(A["pt_copy_a"], 1)

            def dsa_split(h):
                act.wait_ge(att["dsa"]["pv_ready"], h + 1)
                act.activation(ath[:, h, :], ps[:, 6 + h % 2, :], ACT.Copy).then_inc(att["dsa"]["hi_done"], 1)

            softmax_units(att["dsa"], lambda n: (lm[:, n % 2, 0:META + P * (n % QB + 1)], META + P * (n % QB + 1)), pr, pT,
                          split=dsa_split)

            def merged(hi, n, t, buf, m0, per, i):
                act.wait_ge(m_done, lin(m0 + n, per, i))
                act.activation(one(hi, lin(n - 1, per, i)), buf, ACT.Copy).then_inc(mh_done, 1)

            with act.Fori(0, 4) as i:
                for t in range(2):
                    act.wait_ge(acc_free, lin(2 * C_B + t + 1, 4, i))
                    act.activation(tmpb[:, t, :], tmpb[:, t, :], ACT.Sigmoid,
                                   bias=col(vec, lin(V_BG + DK + t, 2, i))).then_inc(sig_done, 1)
                high(C_B + 2, 2, i)
                merged(mh, 1, 0, tmpb[:, 0, :], DK, 2, i)
                high(C_B + 3, 2, i)
                merged(mh, 2, 1, tmpb[:, 1, :], DK, 2, i)
            project(C_O, 1, 1, V_N2)
            ffn(0, 1, 2, None, None)
            root(2)
            for n in range(DK):
                act.wait_ge(xn_done, n + 1)
                feed(3, 2, n, V_F1)

            ffn(1, 3, 4, 3, V_MX)
            root(4)

            def head_root(n):
                act.wait_ge(hq_ss, n + 1)
                act.activation(rtq[:, n % 2, :], ps[:, 5 + 2 * (n % 2), :], ACT.Sqrt, bias=eps[:],
                               scale=1.0 / HEAD_DIM).then_inc(hq_rt, 1)

            def head_square(n, c):
                act.wait_ge(acc_free, 2 * c + n % 2 + 1)
                if n >= 2:
                    act.wait_ge(hq_out, n - 1)
                act.activation(rtq[:, n % 2, :], qs[:, n % 2, :], ACT.Square).then_inc(hq_done, 1)

            for n0, c in ((0, C_FQ), (2, C_FQ + 1), (4, C_FK), (6, C_FK + 1)):
                if n0:
                    head_root(n0 - 2)
                    head_root(n0 - 1)
                high(c + 2)
                head_square(n0, c)
                head_square(n0 + 1, c)
            head_root(6)
            head_root(7)
            high(C_FV + 2)
            high(C_FV + 3)
            act.wait_ge(fz_done, 1)
            act.activation(ft[:], fz[:], ACT.Abs).then_inc(act_seq, 1)
            act.wait_ge(act_seq, 1)
            act.activation(ft[:], ft[:], ACT.Exp, scale=-1.0).then_inc(act_seq, 1)
            act.wait_ge(act_seq, 2)
            act.activation(ft[:], ft[:], ACT.Ln, bias=ones[0:HEADS, 0:1]).then_inc(ft_done, 1)
            for c in range(C_FL, C_MX):
                high(c + 2)

            def fox_before(n):
                h, q = divmod(n, QB)
                if q == 0:
                    act.wait_ge(fb_ready, h + 1)
                    if h >= 2:
                        act.wait_ge(att["fox"]["lg_read"], QB * (h - 1))
                    act.activation(fb[:, h % 2, :], ps[:, 1, :], ACT.Copy).then_inc(fb_done, 1)

            def pair_split(A, hi):
                def split(h):
                    if h % 2:
                        act.wait_ge(A["pv_ready"], h + 1)
                        act.activation(hi[:, h // 2, :], ps[:, 6 + (h // 2) % 2, :], ACT.Copy).then_inc(A["hi_done"], 1)
                return split

            softmax_units(att["fox"], lambda n: (flm[:, n % 2, 0:P * (n % QB + 1)], P * (n % QB + 1)), fp, fpT,
                          before=fox_before, split=pair_split(att["fox"], yfh))

            B = att["sb"]
            split = pair_split(B, ysh)
            seq = 2
            for n in range(QB * HEADS + 1):
                if n < QB * HEADS:
                    h, q = divmod(n, QB)
                    w = P * (q + 1)
                    z, t = ps[:, n % 2 * 2, 0:w], flm[:, n % 2, 0:w]
                    act.wait_ge(B["lg_ready"], n + 1)
                    if n >= 2:
                        act.wait_ge(sl_done, n - 1)
                    act.activation(t, z, ACT.Abs).then_inc(act_seq, 1)
                    seq += 1
                    act.wait_ge(act_seq, seq)
                    act.activation(t, t, ACT.Exp, scale=-1.0).then_inc(act_seq, 1)
                    seq += 1
                    act.wait_ge(act_seq, seq)
                    act.activation(t, t, ACT.Ln, bias=ones[:, 0:1]).then_inc(sp_done, 1)
                if n >= 1:
                    k = n - 1
                    act.wait_ge(B["lg_read"], k + 1)
                    if k >= 2:
                        act.wait_ge(B["pt_ready"], k - 1)
                    w = P * (k % QB + 1)
                    act.activation(fp[:, k % 2, 0:w], sR[:, k % 2, 0:w], ACT.Exp).then_inc(B["p_ready"], 1)
                    copy_turned(B, k, fpT)
                if n >= 2 and (n - 2) % QB == QB - 1:
                    split((n - 2) // QB)
            split(HEADS - 1)

            with act.Fori(0, 2) as i:
                for q in range(2):
                    c = C_MX + 3 * q
                    high(c + 2, 6, i)
                    gate(c, 0, q, None, 6, i)
                    high(c + 3, 6, i)
                    gate(c + 1, 1, q, None, 6, i)
                    merged(m2h, 2 * q + 1, 0, tmp[:, 0, :], 2 * DK, 4, i)
                    high(c + 4, 6, i)
                    merged(m2h, 2 * q + 2, 1, tmp[:, 1, :], 2 * DK, 4, i)
            project(C_O2, 5, 4, V_F2)
            ffn(2, 5, 6, 5, V_PL)
            root(6)

            for j in range(4):
                c = C_PG + j
                if c + 2 < N_CHUNKS:
                    high(c + 2)
                for t in range(2):
                    act.wait_ge(acc_free, 2 * c + t + 1)
                    act.activation(sg[:, 2 * j + t, :], sg[:, 2 * j + t, :], ACT.Sigmoid).then_inc(sig_done, 1)
                if j == 1:
                    for k in range(2):
                        act.wait_ge(p_turned, k + 1)
                        act.activation(ptT[:, k, :], ps[:, 1 + 2 * k, :], ACT.Copy).then_inc(p_copied, 1)
                        act.wait_ge(p_copied, k + 1)
                        act.activation(pTh[:, k, :], ptT[:, k, :], ACT.Copy).then_inc(ph_done, 1)
            for n in range(DK):
                act.wait_ge(o_turned, n + 1)
                act.activation(ot[:, :, P * n:P * n + P], ps[:, 2 * (n % 4), :].rearrange("p (q t) -> p q t", q=QB),
                               ACT.Copy).then_inc(o_copied, 1)

        @block.vector
        def _(dve):
            steps = [0]

            def link(ins):
                ins.then_inc(dve_seq, 1)
                steps[0] += 1
                dve.wait_ge(dve_seq, steps[0])

            def stt(o, a, s, b, op0, op1):
                return dve.scalar_tensor_tensor(o, a, s, b, op0, op1)

            def clear(S):
                if S:
                    dve.wait_ge(ss_done, S)
                dve.memset(ssum[:], 0.0).then_inc(ssum_done, 1)

            def feed(S, X, n, gain, per=0, i=None, lo=META):
                nn = lin(n, per, i)
                dve.wait_ge(sq_done, lin(DK * S + n + 1, per, i))
                dve.wait_ge(ssum_done, lin(9 * S + 1 + n, per, i))
                dve.tensor_tensor(ssum[:, lo:TM], ssum[:, lo:TM], sq[:, lo:TM], ALU.add).then_inc(ssum_done, 1)
                if X is not None:
                    dve.wait_ge(xh_done, lin(DK * X + n + 1, per, i))
                    stt(one(xl, nn)[:, lo:TM], one(hT, nn)[:, lo:TM], col(vec, lin(gain + n, per, i)),
                        one(xh, nn)[:, lo:TM].bitcast(F32), ALU.mult, ALU.subtract).then_inc(x_split, 1)

            def root(S):
                lo = 0 if S == 0 else META
                dve.wait_ge(rt_done, S + 1)
                dve.reciprocal(rs[:, lo:TM], rt[:, lo:TM]).then_inc(rs_done, 1)
                dve.wait_ge(rs_done, S + 1)

            rsx = rs[:, META:TM]
            rs2 = rs[:].rearrange("p (z t) -> p z t", z=2)

            def done(c, t, per=0, i=None):
                dve.wait_ge(tile_done, lin(2 * c + t + 1, 2 * per, i))

            def scaled(o, c, t, per=0, i=None):
                done(c, t, per, i)
                dve.tensor_tensor(o, ps[0:o.shape[0], bank(c, t), :], rsx[0:o.shape[0]], ALU.mult).then_inc(acc_free, 1)

            def scaled_full(o, c, t):
                done(c, t)
                m, b = o.shape[0], bank(c, t)
                dve.tensor_tensor(o.rearrange("p (z t) -> p z t", z=2), ps[0:m, b:b + 2, 0:HALF], rs2[0:m],
                                  ALU.mult).then_inc(acc_free, 1)

            def update(n, b, factor, inc, per=0, i=None):
                x = one(hT, lin(n, per, i))[:, META:TM]
                stt(x, ps[:, b, :], factor, x, ALU.mult, ALU.add).then_inc(acc_free, inc)

            def ffn(f, S, factor, S_next, X_next, gain):
                c = C_F[f]
                root(S)
                with dve.Fori(0, FK // 2) as i:
                    for j in range(2):
                        n = FK * f + j
                        scaled(tmp[:, 0, :], c + j, 0, 2, i)
                        scaled(tmp[:, 2, :], c + j, 1, 2, i)
                        dve.wait_ge(silu_done, lin(n + 1, 2, i))
                        dve.wait_ge(acc_free, lin(2 * (c + j) + 2, 4, i))
                        dve.tensor_tensor(tmp[:, 3, :], tmp[:, 1, :], tmp[:, 2, :], ALU.mult).then_inc(h_done, 1)
                        dve.wait_ge(h_hi, lin(n + 1, 2, i))
                        nn = lin(j, 2, i)
                        dve.tensor_tensor(one(fl, nn), tmp[:, 3, :], one(fh, nn).bitcast(F32), ALU.subtract).then_inc(h_split, 1)
                        dve.wait_ge(h_split, lin(n + 1, 2, i))
                d = C_D[f]
                clear(S_next)
                with dve.Fori(0, 2) as i:
                    for j in range(2):
                        for t in range(2):
                            n = 2 * j + t
                            done(d + 3 * j + 2, t, 6, i)
                            update(n, bank(d + j, t), factor, 3, 4, i)
                            dve.wait_ge(acc_free, lin(2 * d + 6 * j + 3 * t + 3, 12, i))
                            feed(S_next, X_next, n, gain, 4, i)

            def project(c, S, X, gain):
                clear(S)
                with dve.Fori(0, 2) as i:
                    for j in range(2):
                        for t in range(2):
                            n = 2 * j + t
                            done(c + j, t, 2, i)
                            update(n, bank(c + j, t), 1.0, 1, 4, i)
                            dve.wait_ge(acc_free, lin(2 * (c + j) + t + 1, 4, i))
                            feed(S, X, n, gain, 4, i)

            dve.memset(eps[:], EPS)
            dve.memset(ones[:], 1.0).then_inc(ones_done, 1)
            clear(0)
            dve.wait_ge(consts, 11)
            dve.tensor_copy(identr[:], ident[:])
            dve.tensor_copy(causalr[:], causal[:])
            dve.wait_ge(vec_done, 1)
            for n in range(DK):
                feed(0, 0, n, V_N1, lo=0)
            root(0)

            scaled_full(cl[:], C_LAT, 0)
            scaled_full(kw[:], C_LAT, 1)
            for t in range(2):
                scaled(qiT[:, t, :], C_QI, t)

            def query(c):
                for t in range(2):
                    done(c, t)
                    stt(qT[:, 2 * (c - C_Q) + t, :], ps[:, bank(c, t), :], ATTN_SCALE, rsx, ALU.mult, ALU.mult).then_inc(acc_free, 1)

            query(C_Q)
            dve.wait_ge(wi_turned, 1)
            dve.tensor_scalar(wi[:].rearrange("p q h -> p (q h)"), ps[:, 1, 0:QB * HEADS], INDEX_SCALE, None,
                              ALU.mult).then_inc(wi_done, 1)
            dve.wait_ge(wi_done, 1)
            for n in range(QB * HEADS):
                q, h = divmod(n, HEADS)
                w = META + P * (q + 1)
                dve.wait_ge(relu_done, n + 1)
                if h == 0:
                    dve.tensor_scalar(sc[:, q, 0:w], rl[:, n % 2, 0:w], wi[:, q, h:h + 1], None, ALU.mult).then_inc(score_acc, 1)
                else:
                    dve.wait_ge(score_acc, n)
                    stt(sc[:, q, 0:w], rl[:, n % 2, 0:w], wi[:, q, h:h + 1], sc[:, q, 0:w], ALU.mult, ALU.add).then_inc(score_acc, 1)
            dve.wait_ge(crt_done, 1)
            link(dve.reciprocal(rc[:], rt[:]))
            stt(cT[:], cl[:], vec[:, V_KV:V_KV + 1], rc[:], ALU.mult, ALU.mult).then_inc(c_done, 1)
            dve.wait_ge(score_acc, QB * HEADS)

            def search():
                for q in range(QB):
                    w = META + P * (q + 1)
                    s, diag = sc[:, q, 0:w], sc[:, q, w - P:w]
                    link(stt(diag, causal[:], -TAKEN / -NEG, diag, ALU.mult, ALU.add))
                    for _ in range(TOP_K // 8):
                        link(dve.max(m8[:], s))
                        link(dve.match_replace(s, m8[:], s, TAKEN))
                        yield
                    link(dve.tensor_scalar(s, s, TAKEN, NEG, ALU.not_equal, ALU.mult))
                    link(dve.tensor_tensor(diag, diag, causal[:], ALU.add))
                    yield

            steps_of_search = search()

            def some_search(n):
                for _ in range(n):
                    next(steps_of_search, None)

            for c in range(C_Q + 1, C_U):
                query(c)
                some_search(6)

            def pool_group(g):
                cur = u[:, g, :]
                if g:
                    dve.wait_ge(pooled_done, g)
                for d in range(g + 1):
                    sh, lo = 1 << d, (2 << d) - 1
                    nxt = win[:, d % 2, :]
                    link(dve.tensor_tensor(nxt[:, lo:TM], cur[:, lo:TM], cur[:, lo - sh:TM - sh], ALU.add))
                    cur = nxt
                stt(pooled[:, g, :], cur[:, META:TM], 1.0 / (2 << g), u[:, g, META:TM], ALU.mult, ALU.subtract).then_inc(pooled_done, 1)

            for j in range(2):
                for t in range(2):
                    scaled_full(u[:, 2 * j + t, :], C_U + j, t)
                some_search(5)
                dve.wait_ge(acc_free, 2 * (C_U + j) + 2)
                pool_group(2 * j)
                pool_group(2 * j + 1)
            dve.wait_ge(pooled_done, 4)
            for j in range(2):
                for t in range(2):
                    scaled_full(cc[:, 2 * j + t, :], C_CC + j, t)
                some_search(7)
            for j in range(2):
                for t in range(2):
                    g = 2 * j + t
                    scaled_full(cv[:], C_CU + j, t)
                    dve.wait_ge(acc_free, 2 * (C_CU + j) + t + 1)
                    link(dve.tensor_tensor(cv[:], cv[:], cc[:, g, :], ALU.mult))
                    link(dve.tensor_scalar(cy[:, g, :], cv[:, META - 2:TM - 2], vec[:, V_CW + g:V_CW + g + 1], None, ALU.mult))
                    for r in (1, 2):
                        w = V_CW + 4 * r + g
                        link(stt(cy[:, g, :], cv[:, META - 2 + r:TM - 2 + r], vec[:, w:w + 1], cy[:, g, :], ALU.mult, ALU.add))
                some_search(5)

            def gated_conv(c):
                for t in range(2):
                    g = 2 * (c - C_CB) + t
                    if g:
                        dve.wait_ge(co_split, g)
                    scaled(co[:], c, t)
                    dve.wait_ge(acc_free, 2 * c + t + 1)
                    dve.tensor_tensor(co[:], co[:], cy[:, g, :], ALU.mult).then_inc(co_done, 1)
                    dve.wait_ge(coh_done, g + 1)
                    dve.wait_ge(co_done, g + 1)
                    dve.tensor_tensor(col_[:, g, :], co[:], coh[:, g, :].bitcast(F32), ALU.subtract).then_inc(co_split, 1)

            gated_conv(C_CB)
            for g in range(4):
                dve.wait_ge(ah_done, g + 1)
                stt(al[:, g, :], ps[:, 2 * g + 1, :], vec[:, V_PS + g:V_PS + g + 1], ah[:, g, :].bitcast(F32),
                    ALU.mult, ALU.subtract).then_inc(a_split, 1)
            some_search(5)
            gated_conv(C_CB + 1)
            dve.wait_ge(co_split, 4)
            some_search(1000)

            with dve.Fori(0, 2) as i:
                for q in range(2):
                    c = C_AC + 3 * q
                    for kind in range(2):
                        for t in range(2):
                            scaled(tmp[:, 2 * kind + t, :], c + kind, t, 6, i)
                    for t in range(2):
                        done(c + 2, t, 6, i)
                        b = bank(c + 2, t)
                        dve.wait_ge(sig_done, lin(4 * q + 2 + t + 1, 8, i))
                        dve.tensor_tensor(tmp[:, t, :], tmp[:, t, :], ps[:, b, :], ALU.mult).then_inc(mul_done, 1)
                        dve.tensor_tensor(tmp[:, 2 + t, :], tmp[:, 2 + t, :], ps[:, b + 1, :], ALU.mult).then_inc(acc_free, 1)
                        dve.wait_ge(mul_done, lin(2 * q + t + 1, 4, i))
                        dve.wait_ge(acc_free, lin(2 * (c + 2) + t + 1, 12, i))
                        dve.tensor_tensor(one(msum, lin(2 * q + t, 4, i)), tmp[:, t, :], tmp[:, 2 + t, :], ALU.add).then_inc(m_done, 1)
                    dve.wait_ge(m_done, lin(2 * q + 2, 4, i))

            def softmax_units(A, logits, mask, dst, probs, width, turned, meta, split):
                def masked(n):
                    w = width(n)
                    dve.wait_ge(A["lg_ready"], n + 1)
                    if n >= 2:
                        dve.wait_ge(A["exp_done"], n - 1)
                    dve.tensor_tensor_reduce(dst[:, n % 2, 0:w], logits(n), mask(n), -1.0, 3.0e38, ALU.add, ALU.min,
                                             nmx[:, n:n + 1]).then_inc(A["lg_read"], 1)

                masked(0)
                for n in range(QB * HEADS):
                    h, q = divmod(n, QB)
                    if n + 1 < QB * HEADS:
                        masked(n + 1)
                    w = width(n)
                    dve.wait_ge(A["exp_done"], n + 1)
                    link(dve.reciprocal(rden[:, n:n + 1], den[:, n:n + 1]))
                    dve.tensor_scalar(probs[:, n % 2, 0:w], probs[:, n % 2, 0:w], rden[:, n:n + 1], None, ALU.mult).then_inc(A["p_ready"], 1)
                    if n >= 1:
                        meta_copy(A, n - 1, turned, meta)
                    if n >= 2 and (n - 2) % QB == QB - 1:
                        split((n - 2) // QB)
                meta_copy(A, QB * HEADS - 1, turned, meta)
                split(HEADS - 1)

            def meta_copy(A, n, turned, meta):
                h, q = divmod(n, QB)
                dve.wait_ge(A["pt_ready"], n + 1)
                if meta:
                    if h >= 2:
                        dve.wait_ge(A["pv_ready"], h - 1)
                    dve.tensor_copy(turned[h % 2][0:META, QB, P * q:P * q + P], ps[0:META, 5, 0:P]).then_inc(A["pt_copy_d"], 1)
                else:
                    dve.sem_inc(A["pt_copy_d"], 1)

            def dsa_split(h):
                A = att["dsa"]
                dve.wait_ge(A["hi_done"], h + 1)
                dve.tensor_tensor(atl[:, h, :], ps[:, 6 + h % 2, :], ath[:, h, :].bitcast(F32), ALU.subtract).then_inc(A["y_split"], 1)

            def dsa_logits(n):
                w, b = META + P * (n % QB + 1), 2 * (n % 2)
                return ps[:, b:b + 2, :].rearrange("p b k -> p (b k)")[:, 0:w]

            softmax_units(att["dsa"], dsa_logits, lambda n: sc[:, n % QB, 0:META + P * (n % QB + 1)], lm, pr,
                          lambda n: META + P * (n % QB + 1), pT, True, dsa_split)

            def merged(lo_part, hi_part, buf, n, m0, per, i):
                nn = lin(n, per, i)
                dve.wait_ge(mh_done, lin(m0 + n + 1, per, i))
                dve.tensor_tensor(one(lo_part, nn), buf, one(hi_part, nn).bitcast(F32), ALU.subtract).then_inc(m_split, 1)

            with dve.Fori(0, 4) as i:
                for t in range(2):
                    scaled(tmpb[:, t, :], C_B, t, 2, i)
                for t in range(2):
                    g = tmpb[:, t, :]
                    done(C_B + 1, t, 2, i)
                    dve.wait_ge(sig_done, lin(16 + t + 1, 2, i))
                    dve.tensor_tensor(g, g, ps[:, bank(C_B + 1, t), :], ALU.mult).then_inc(acc_free, 1)
                    dve.wait_ge(acc_free, lin(2 * (C_B + 1) + t + 1, 4, i))
                    dve.tensor_tensor(g, g, one(msum, lin(t, 2, i)), ALU.add).then_inc(m_done, 1)
                    merged(ml, mh, g, t, 0, 2, i)
                dve.wait_ge(m_split, lin(2, 2, i))
            project(C_O, 1, 1, V_N2)
            ffn(0, 1, 1.0, 2, None, None)
            root(2)
            clear(3)
            for n in range(DK):
                x = hT[:, n, META:TM]
                stt(x, x, vec[:, V_FIN + n:V_FIN + n + 1], rsx, ALU.mult, ALU.mult).then_inc(xn_done, 1)
            dve.wait_ge(xn_done, DK)
            for n in range(DK):
                feed(3, 2, n, V_F1)

            ffn(1, 3, 0.5, 4, 3, V_MX)
            root(4)

            def head_scaled(n, c):
                if n >= 2:
                    dve.wait_ge(hq_out, n - 1)
                scaled(qs[:, n % 2, :], c, n % 2)

            def head_normed(n):
                dst, g = (qF, V_QN) if n < 4 else (kF, V_KN)
                dve.wait_ge(hq_rt, n + 1)
                r = rtq[:, n % 2, :]
                link(dve.reciprocal(r, r))
                if n < 4:
                    link(dve.tensor_scalar(r, r, HEAD_DIM ** -0.5, None, ALU.mult))
                stt(dst[:, n % 4, :], qs[:, n % 2, :], vec[:, g:g + 1], r, ALU.mult, ALU.mult).then_inc(hq_out, 1)

            for n0, c in ((0, C_FQ), (2, C_FQ + 1), (4, C_FK), (6, C_FK + 1)):
                if n0 == 2:
                    dve.wait_ge(rtok_turned, 1)
                    dve.tensor_copy(rtok[:], ps[:, 1, :].rearrange("p (q t) -> p q t", q=QB)[:, :, 0]).then_inc(rtok_done, 1)
                if n0:
                    head_normed(n0 - 2)
                    head_normed(n0 - 1)
                head_scaled(n0, c)
                head_scaled(n0 + 1, c)
            head_normed(6)
            head_normed(7)

            def tokens(v, c, j):
                for t in range(2):
                    done(c, t)
                    for z in range(2):
                        q = 2 * t + z
                        ins = dve.tensor_scalar(v[:, q, CW * j:CW * j + CW], ps[:, bank(c, t), CW * z:CW * z + CW],
                                                rtok[:, q:q + 1], None, ALU.mult)
                    ins.then_inc(acc_free, 1)

            dve.wait_ge(rtok_done, 1)
            tokens(vF, C_FV, 0)
            tokens(vF, C_FV + 1, 1)
            dve.wait_ge(tile_done, 2 * C_FL + 2)
            dve.wait_ge(misc_in, 32)
            dve.tensor_tensor(fz[:], ps[0:HEADS, bank(C_FL, 0), :], rsx[0:HEADS], ALU.mult).then_inc(acc_free, 2)
            dve.wait_ge(acc_free, 2 * C_FL + 2)
            dve.tensor_scalar(fz[:], fz[:], fbias[:, 0:1], None, ALU.add).then_inc(fz_done, 1)
            dve.wait_ge(ft_done, 1)
            dve.wait_ge(fz_done, 1)
            link(stt(fz[:], fz[:], 0.0, ft[:], ALU.min, ALU.subtract))
            dve.wait_ge(consts, 14)
            dve.tensor_tensor_scan(fF[:], fone[:], fz[:], 0.0, ALU.mult, ALU.add).then_inc(f_done, 1)
            for j in range(2):
                for t in range(2):
                    done(C_SQ + j, t)
                    stt(qS[:, 2 * j + t, :], ps[:, bank(C_SQ + j, t), :], HEAD_DIM ** -0.5, rsx, ALU.mult, ALU.mult).then_inc(acc_free, 1)
            for j in range(2):
                for t in range(2):
                    scaled(kS[:, 2 * j + t, :], C_SK + j, t)
            for j in range(2):
                tokens(vS, C_SV + j, j)

            def pair_split(A, hi_part, lo_part):
                def split(h):
                    if h % 2:
                        dve.wait_ge(A["hi_done"], h // 2 + 1)
                        dve.tensor_tensor(lo_part[:, h // 2, :], ps[:, 6 + (h // 2) % 2, :], hi_part[:, h // 2, :].bitcast(F32),
                                          ALU.subtract).then_inc(A["y_split"], 1)
                return split

            def fox_mask(n):
                h, q = divmod(n, QB)
                dve.wait_ge(fb_done, h + 1)
                return fb[:, h % 2, 0:P * (q + 1)]

            softmax_units(att["fox"], lambda n: ps[:, 2 * (n % 2), 0:P * (n % QB + 1)], fox_mask, flm, fp,
                          lambda n: P * (n % QB + 1), fpT, False, pair_split(att["fox"], yfh, yfl))

            B = att["sb"]
            split = pair_split(B, ysh, ysl)
            dve.wait_ge(att["fox"]["y_split"], 4)
            for n in range(QB * HEADS):
                h, q = divmod(n, QB)
                w = P * (q + 1)
                z, L, R = ps[:, n % 2 * 2, 0:w], sL[:, n % 2, 0:w], sR[:, n % 2, 0:w]
                dve.wait_ge(sp_done, n + 1)
                if n >= 2:
                    dve.wait_ge(B["p_ready"], n - 1)
                stt(L, z, 0.0, flm[:, n % 2, 0:w], ALU.max, ALU.add).then_inc(sl_done, 1)
                dve.wait_ge(sl_done, n + 1)
                link(dve.tensor_tensor(L[:, w - P:w], L[:, w - P:w], strict01[:], ALU.mult))
                link(dve.tensor_tensor_scan(R[:, ::-1], L[:, ::-1], L[:, ::-1], 0.0, ALU.add, ALU.bypass))
                link(dve.tensor_tensor(R, z, R, ALU.subtract))
                dve.tensor_tensor(R[:, w - P:w], R[:, w - P:w], strict[:], ALU.add).then_inc(B["lg_read"], 1)
                if n >= 1:
                    meta_copy(B, n - 1, None, False)
                if n >= 2 and (n - 2) % QB == QB - 1:
                    split((n - 2) // QB)
            meta_copy(B, QB * HEADS - 1, None, False)
            split(HEADS - 1)

            with dve.Fori(0, 2) as i:
                for q in range(2):
                    c = C_MX + 3 * q
                    for kind in range(2):
                        for t in range(2):
                            scaled(tmp[:, 2 * kind + t, :], c + kind, t, 6, i)
                    for t in range(2):
                        done(c + 2, t, 6, i)
                        b = bank(c + 2, t)
                        n = 2 * q + t
                        dve.wait_ge(sig_done, lin(24 + 4 * q + 2 + t + 1, 8, i))
                        dve.tensor_tensor(tmp[:, t, :], tmp[:, t, :], ps[:, b, :], ALU.mult).then_inc(mul_done, 1)
                        dve.tensor_tensor(tmp[:, 2 + t, :], tmp[:, 2 + t, :], ps[:, b + 1, :], ALU.mult).then_inc(acc_free, 1)
                        dve.wait_ge(mul_done, lin(DK + n + 1, 4, i))
                        dve.wait_ge(acc_free, lin(2 * (c + 2) + t + 1, 12, i))
                        dve.tensor_tensor(tmp[:, t, :], tmp[:, t, :], tmp[:, 2 + t, :], ALU.add).then_inc(m_done, 1)
                        merged(m2l, m2h, tmp[:, t, :], n, DK, 4, i)
                    dve.wait_ge(m_split, lin(DK + 2 * q + 2, 4, i))
            project(C_O2, 5, 4, V_F2)
            ffn(2, 5, 0.5, 6, 5, V_PL)
            root(6)

            for j in range(4):
                for t in range(2):
                    scaled(sg[:, 2 * j + t, :], C_PG + j, t)
                if j == 1:
                    for k in range(2):
                        dve.wait_ge(ph_done, k + 1)
                        dve.tensor_tensor(pTl[:, k, :], ptT[:, k, :], pTh[:, k, :].bitcast(F32), ALU.subtract).then_inc(p_split, 1)
            for n in range(DK):
                dve.wait_ge(tile_done, 2 * C_PP + n + 1)
                dve.wait_ge(sig_done, 40 + n + 1)
                g, x = sg[:, n, :], hT[:, n, META:TM]
                dve.tensor_tensor(g, g, ps[:, 2 * (n % 4) + 1, :], ALU.mult).then_inc(acc_free, 1)
                dve.wait_ge(acc_free, 2 * C_PP + n + 1)
                dve.tensor_tensor(x, x, g, ALU.add).then_inc(o_done, 1)


def kernel(**inputs):
    import numpy as np
    from concourse import bacc
    from concourse.bass_utils import run_bass_kernel_spmd

    nc = bacc.Bacc("TRN2", target_bir_lowering=False, num_devices=1)
    arrays, args = {}, {}
    for name, value in inputs.items():
        a = np.ascontiguousarray(value)
        arrays[f"in_{name}"] = a
        args[name] = nc.dram_tensor(f"in_{name}", a.shape, mybir.dt.from_np(a.dtype), kind="ExternalInput").ap()
    o = nc.dram_tensor("out_0", (1, T, D), F32, kind="ExternalOutput").ap()
    build(nc, args, o)
    r = run_bass_kernel_spmd(nc, [arrays], core_ids=[0])
    return r.results[0]["out_0"]
```

```python
from contextlib import ExitStack

import concourse.bass as bass
from concourse import mybir

F32 = mybir.dt.float32
F32R = mybir.dt.float32r
ACT = mybir.ActivationFunctionType
ALU = mybir.AluOpType
AX = mybir.AxisListType

P = 128
D = 1024
DK = D // P
T = 512
META = 16
TM = T + META
HALF = TM // 2
QB = T // P
CH = 2048
CW = CH // DK
EPS = 1e-6
HEADS = 8
D_LAT = 128
ATTN_SCALE = D_LAT ** -0.5
D_IDX = 32
INDEX_SCALE = HEADS ** -0.5 * D_IDX ** -0.5
TOP_K = T // 4
D_FF = 2816
FK = D_FF // P
HEAD_DIM = 64
DOWN_K = (8, 8, 6)
NEG = -1.0e30
SEL_LO = 32
UNITS = 4
Z_TOP = 60.0
TAKEN = -3.0e38

O_U, O_Q, O_C, O_QI, O_KI, O_CB, O_CC, O_CU, O_G = 0, 512, 1536, 1664, 1920, 1960, 2472, 2984, 3496
KW = D_IDX + HEADS
S_FQ, S_FK, S_FV, S_FL, S_SQ, S_SK, S_SV, S_GF, S_GS = 0, 512, 1024, 1536, 1544, 2056, 2568, 3080, 4104

C_LAT, C_QI, C_Q, C_U, C_CC, C_CU, C_CB, C_AC, C_B, C_O = 0, 1, 2, 6, 8, 10, 12, 14, 26, 34
C_F = (38, 72, 135)
C_D = (60, 94, 157)
C_FQ, C_FK, C_FL, C_FV, C_SQ, C_SK, C_SV, C_GF, C_GS, C_MX, C_O2 = 106, 108, 110, 111, 113, 115, 117, 119, 123, 127, 131
C_PG, C_PP, N_CHUNKS = 169, 173, 174

V_N1, V_N2, V_FIN, V_F1, V_MX, V_F2, V_PL, V_BG, V_PS, V_CW, V_KV, V_QN, V_KN, V_ROWS, V_FP = (
    0, 8, 16, 24, 32, 40, 48, 56, 80, 84, 96, 97, 98, 99, 99)

SB_STEPS, _n = [], 0
for _third in range(48):
    _k = 1 if _third < 18 or _third % 3 != 1 and _third < 42 or _third in (44, 47) else 0
    SB_STEPS.append(range(_n, _n + _k))
    _n += _k


def lin(value, per=0, i=None):
    return value if i is None else i * per + value


def one(t, n):
    return t[:, n, :] if isinstance(n, int) else t[:, bass.ds(n, 1), :].rearrange("p o t -> p (o t)")


def col(t, n):
    return t[:, n:n + 1] if isinstance(n, int) else t[:, bass.ds(n, 1)]


def build(nc, I, out):
    with ExitStack() as ctx:
        def sb(name, shape, dt=F32):
            return ctx.enter_context(nc.sbuf_tensor(name, shape, dt))

        def sem(name):
            return ctx.enter_context(nc.semaphore(name))

        hT = sb("hT", [P, DK, TM])
        xh = sb("xh", [P, DK, TM], F32R)
        xl = sb("xl", [P, DK, TM], F32R)
        raw = sb("raw", [P, 2, CH])
        whi = sb("whi", [P, 2, CH], F32R)
        wlo = sb("wlo", [P, 2, CH], F32R)
        rs = sb("rs", [P, TM])
        rt = sb("rt", [P, TM])
        sq = sb("sq", [P, TM])
        ssum = sb("ssum", [P, TM])
        vec = sb("vec", [P, V_ROWS + DK])
        ident = sb("ident", [P, P])
        identr = sb("identr", [P, P], F32R)
        ones = sb("ones", [P, P])
        onesblk = sb("onesblk", [P, P])
        causal = sb("causal", [P, P])
        causalr = sb("causalr", [P, P], F32R)
        strict = sb("strict", [P, P])
        strictr = sb("strictr", [P, P], F32R)
        eps = sb("eps", [P, 1])
        wi = sb("wi", [P, QB, HEADS])
        nmx = sb("nmx", [P, QB * HEADS])
        den = sb("den", [P, QB * HEADS])
        rden = sb("rden", [P, QB * HEADS])
        m8 = sb("m8", [P, 8])
        rtok = sb("rtok", [P, QB])
        fbias = sb("fbias", [8, 1])
        arena_cols = 24784
        start = (nc.sbuf_base + 31) // 32 * 32
        arena = sb("arena", [P, arena_cols])

        def at(name, off, shape, dt=F32):
            n = 1
            for s in shape[1:]:
                n *= s
            assert off + n <= arena_cols, name
            return nc.alloc_sbuf_tensor_at(name, shape, dt, offset=start + 4 * off)

        fh = at("fh", 0, [P, FK, T], F32R)
        fl = at("fl", FK * T, [P, FK, T], F32R)
        tmp = at("tmp", 2 * FK * T, [P, 4, T])
        sq2, ssum2 = tmp[:, 0, :], tmp[:, 1, :]
        xt = at("xt", 0, [P, QB, D])
        mt = at("mt", 4096, [META, D])
        vt = at("vt", 5120, [V_ROWS, P])
        cT = at("cT", 0, [P, TM])
        ctok = at("ctok", 528, [P, QB + 1, P])
        qT = at("qT", 1168, [P, HEADS, T])
        ath = at("ath", 1168, [P, HEADS, T], F32R)
        sc = at("sc", 5264, [P, QB, TM])
        ah = at("ah", 7376, [P, 4, T], F32R)
        al = at("al", 9424, [P, 4, T], F32R)
        coh = at("coh", 11472, [P, 4, T], F32R)
        col_ = at("col_", 13520, [P, 4, T], F32R)
        cl = at("cl", 15568, [P, TM])
        kw = at("kw", 16096, [KW, TM])
        kiT = at("kiT", 16624, [P, TM])
        qiT = at("qiT", 17152, [P, 2, T])
        rl = at("rl", 18176, [P, 2, TM])
        rc = at("rc", 19232, [P, TM])
        u = at("u", 19760, [P, 4, TM])
        pooled = at("pooled", 15568, [P, 4, T])
        win = at("win", 17616, [P, 2, TM])
        cc = at("cc", 18672, [P, 4, TM])
        cv = at("cv", 20784, [P, TM])
        cy = at("cy", 21312, [P, 4, T])
        pwt = at("pwt", 23360, [P, 4, P])
        co = at("co", 23872, [P, T])
        msum = at("msum", 15568, [P, DK, T])
        atl = at("atl", 7376, [P, HEADS, T], F32R)
        pT = [at("pT0", 11472, [P, QB + 1, T]), at("pT1", 19664, [P, QB + 1, T])]
        lm = at("lm", 22224, [P, 2, TM])
        pr = at("pr", 23280, [P, 2, TM])
        mh = at("mh", 11472, [P, DK, T], F32R)
        ml = at("ml", 19664, [P, DK, T], F32R)
        tmpb = at("tmpb", 23760, [P, 2, T])
        qF = at("qF", 0, [P, 4, T])
        kF = at("kF", 2048, [P, 4, T])
        qS = at("qS", 4096, [P, 4, T])
        kS = at("kS", 6144, [P, 4, T])
        yfh = at("yfh", 0, [P, 4, T], F32R)
        yfl = at("yfl", 2048, [P, 4, T], F32R)
        ysh = at("ysh", 4096, [P, 4, T], F32R)
        ysl = at("ysl", 6144, [P, 4, T], F32R)
        vF = at("vF", 8192, [P, QB, T])
        sel = at("sel", 10240, [P, HEADS, P])
        selr = at("selr", 11264, [P, HEADS, P], F32R)
        fz = at("fz", 12288, [8, T])
        ft = at("ft", 12800, [8, T])
        fF = at("fF", 13312, [P, T])
        fFs = at("fFs", 13824, [P, T], F32R)
        fone = at("fone", 14336, [8, T])
        qs = at("qs", 14848, [P, 4, T])
        rtq = at("rtq", 22528, [P, 4, T])
        vS = at("vS", 16384, [P, QB, T])
        pu = at("pu", 22528, [P, UNITS, T])
        fpT = [at("fpT0", 18432, [P, QB, T]), at("fpT1", 20480, [P, QB, T])]
        gates = at("gates", 8192, [P, 2 * DK, T])
        m2h = at("m2h", 16384, [P, DK, T], F32R)
        m2l = at("m2l", 20480, [P, DK, T], F32R)
        sg = at("sg", 0, [P, DK, T])
        pTh = at("pTh", 4096, [P, 2, T], F32R)
        pTl = at("pTl", 5120, [P, 2, T], F32R)
        pt = at("pt", 6144, [P, QB, 256])
        ptT = at("ptT", 7168, [P, 2, T])
        ot = at("ot", 8192, [P, QB, D])

        ps = ctx.enter_context(nc.psum_tensor("ps", [P, 8, 512], F32))

        raw_in = [sem("raw_in0"), sem("raw_in1")]
        raw_taken = sem("raw_taken")
        w_hi = sem("w_hi")
        w_lo = sem("w_lo")
        tile_done = sem("tile_done")
        acc_free = sem("acc_free")
        consts, ones_done = sem("consts"), sem("ones_done")
        x_in, vec_in, misc_in = sem("x_in"), sem("vec_in"), sem("misc_in")
        x_turned, x_copied, vec_turned, vec_done = sem("x_turned"), sem("x_copied"), sem("vec_turned"), sem("vec_done")
        sq_done, ssum_done, xh_done, x_split = sem("sq_done"), sem("ssum_done"), sem("xh_done"), sem("x_split")
        ss_done, rt_done, rs_done = sem("ss_done"), sem("rt_done"), sem("rs_done")
        dve_seq = sem("dve_seq")
        act_seq = sem("act_seq")
        ki_rep, wi_turned, wi_done = sem("ki_rep"), sem("wi_turned"), sem("wi_done")
        s_ready, relu_done, score_acc = sem("s_ready"), sem("relu_done"), sem("score_acc")
        csq_done, css_done, crt_done, c_done, c_turned, ctok_done = (
            sem("csq_done"), sem("css_done"), sem("crt_done"), sem("c_done"), sem("c_turned"), sem("ctok_done"))
        pooled_done, mix_done, ah_done, a_split = sem("pooled_done"), sem("mix_done"), sem("ah_done"), sem("a_split")
        co_done, coh_done, co_split = sem("co_done"), sem("coh_done"), sem("co_split")
        sig_done, mul_done, m_done, mh_done, m_split = (
            sem("sig_done"), sem("mul_done"), sem("m_done"), sem("mh_done"), sem("m_split"))
        silu_done, h_done, h_hi, h_split = sem("silu_done"), sem("h_done"), sem("h_hi"), sem("h_split")
        xn_done, gain_done = sem("xn_done"), sem("gain_done")
        sq2_done, ssum2_done, ms2_done, rt2_done = sem("sq2_done"), sem("ssum2_done"), sem("ms2_done"), sem("rt2_done")
        att = {k: {n: sem(f"{k}_{n}") for n in (
            "lg_ready", "mx_done", "lg_read", "exp_done", "p_ready", "pt_ready", "pt_copy_a", "pt_copy_d", "pv_ready", "hi_done",
            "y_split")} for k in ("dsa", "fox", "sb")}
        hq_done, hq_ss, hq_rt, hq_out = sem("hq_done"), sem("hq_ss"), sem("hq_rt"), sem("hq_out")
        rtok_turned, rtok_done = sem("rtok_turned"), sem("rtok_done")
        fz_done, ft_done, f_done, f_hi, f_lo, sel_done = (
            sem("fz_done"), sem("ft_done"), sem("f_done"), sem("f_hi"), sem("f_lo"), sem("sel_done"))
        z_capped, sp_done = sem("z_capped"), sem("sp_done")
        p_in, p_turned, p_copied, ph_done, p_split = (
            sem("p_in"), sem("p_turned"), sem("p_copied"), sem("ph_done"), sem("p_split"))
        o_done, o_turned, o_copied, o_out = sem("o_done"), sem("o_turned"), sem("o_copied"), sem("o_out")

        def bank(c, t):
            return 4 * (c % 2) + 2 * t

        def n_cols(c):
            if c == C_LAT:
                return DK * (P + KW)
            if c == C_FL:
                return DK * HEADS
            for d in C_D:
                if d <= c < d + 12 and (c - d) % 3 == 2:
                    return DOWN_K[2] * CW
            return CH

        def raw_level(c, per, i):
            return lin(32 * (c // 2 + 1), 16 * per, i)

        kin = "(k p) n -> p k n"
        w1 = I["w_in"][0].rearrange(kin, p=P)
        w2 = I["w_in_2"][0].rearrange(kin, p=P)

        block = ctx.enter_context(nc.Block())

        @block.sync
        def _(sp):
            def slot(c, k, w):
                return raw[:, c % 2, 0:k * w].rearrange("p (k n) -> p k n", k=k)

            def load(c, parts, per=0, i=None):
                if c >= 2:
                    sp.wait_ge(w_lo, lin(c - 1, per, i))
                    sp.sem_inc(raw_taken, 1)
                for dst, src in parts:
                    sp.dma_start(dst, src).then_inc(raw_in[c % 2], 16)

            def square(c, w, at_col, per=0, i=None):
                s = slot(c, DK, CW)
                sel = slice(at_col, at_col + CW) if isinstance(at_col, int) else bass.ds(sp.snap(at_col), CW)
                load(c, [(s[:, 0:4], w[:, 0:4, sel]), (s[:, 4:8], w[:, 4:8, sel])], per, i)

            def two(c, wa, wb, at_col, per, i):
                s = slot(c, DK, CW)
                sel = bass.ds(sp.snap(at_col), CW)
                load(c, [(s[:, 0:4], wa[:, :, sel]), (s[:, 4:8], wb[:, :, sel])], per, i)

            def ffn(f, gate, up, down):
                with sp.Fori(0, FK // 2) as i:
                    for j in range(2):
                        c = C_F[f] + j
                        s = slot(c, DK, CW)
                        sel = bass.ds(sp.snap(i * CW + P * j), P)
                        load(c, [(s[:, :, 0:P], gate[:, :, sel]), (s[:, :, P:CW], up[:, :, sel])], 2, i)
                with sp.Fori(0, 2) as i:
                    for j in range(2):
                        sel = bass.ds(sp.snap(i * (2 * CW) + j * CW), CW)
                        for r, kn in enumerate(DOWN_K):
                            c = C_D[f] + 3 * j + r
                            s = slot(c, kn, CW)
                            k0, hk = sum(DOWN_K[:r]), kn // 2
                            load(c, [(s[:, 0:hk], down[:, k0:k0 + hk, sel]),
                                     (s[:, hk:kn], down[:, k0 + hk:k0 + kn, sel])], 6, i)

            sp.dma_start(xt[:], I["x"][0].rearrange("(b p) d -> p b d", p=P)).then_inc(x_in, 16)
            s = slot(C_LAT, DK, P + KW)
            load(C_LAT, [(s[:, :, 0:P], w1[:, :, O_C:O_C + P]), (s[:, :, P:P + KW], w1[:, :, O_KI:O_KI + KW])])
            sp.wait_ge(x_in, 32)
            square(C_QI, w1, O_QI)
            for c0, o, n in ((C_Q, O_Q, 4), (C_U, O_U, 2), (C_CC, O_CC, 2), (C_CU, O_CU, 2), (C_CB, O_CB, 2)):
                for j in range(n):
                    square(c0 + j, w1, o + CW * j)
            wa = I["w_a"][0].rearrange(kin, p=P)
            wc = I["w_c"][0].rearrange(kin, p=P)
            with sp.Fori(0, 2) as i:
                for q in range(2):
                    c = C_AC + 3 * q
                    square(c, w1, i * (2 * CW) + (O_G + CW * q), 6, i)
                    square(c + 1, w1, i * (2 * CW) + (O_G + 2 * D + CW * q), 6, i)
                    two(c + 2, wa, wc, i * (2 * CW) + CW * q, 6, i)
            wb = I["w_b"][0].rearrange(kin, p=P)
            with sp.Fori(0, 4) as i:
                square(C_B, w1, i * CW + (O_G + D), 2, i)
                square(C_B + 1, wb, i * CW, 2, i)
            wo = I["w_o"][0].rearrange(kin, p=P)
            with sp.Fori(0, 2) as i:
                for j in range(2):
                    square(C_O + j, wo, i * (2 * CW) + CW * j, 2, i)
            gu = I["w_gate_up"][0].rearrange(kin, p=P)
            ffn(0, gu[:, :, 0:D_FF], gu[:, :, D_FF:2 * D_FF], I["w_down"][0].rearrange(kin, p=P))
            ffn(1, I["ffn1_w_gate_2"][0].rearrange(kin, p=P), I["ffn1_w_up_2"][0].rearrange(kin, p=P),
                I["ffn1_w_down_2"][0].rearrange(kin, p=P))
            for c0, o in ((C_FQ, S_FQ), (C_FK, S_FK)):
                for j in range(2):
                    square(c0 + j, w2, o + CW * j)
            s = slot(C_FL, DK, HEADS)
            load(C_FL, [(s[:, 0:4], w2[:, 0:4, S_FL:S_FL + HEADS]), (s[:, 4:8], w2[:, 4:8, S_FL:S_FL + HEADS])])
            for c0, o, n in ((C_FV, S_FV, 2), (C_SQ, S_SQ, 2), (C_SK, S_SK, 2), (C_SV, S_SV, 2), (C_GF, S_GF, 4), (C_GS, S_GS, 4)):
                for j in range(n):
                    square(c0 + j, w2, o + CW * j)
            wf = I["w_branch_fox_2"][0].rearrange(kin, p=P)
            ws = I["w_branch_sb_2"][0].rearrange(kin, p=P)
            with sp.Fori(0, 2) as i:
                for q in range(2):
                    two(C_MX + q, wf, ws, i * (2 * CW) + CW * q, 2, i)
            wo2 = I["w_out_2"][0].rearrange(kin, p=P)
            with sp.Fori(0, 2) as i:
                for j in range(2):
                    square(C_O2 + j, wo2, i * (2 * CW) + CW * j, 2, i)
            ffn(2, I["ffn2_w_gate_2"][0].rearrange(kin, p=P), I["ffn2_w_up_2"][0].rearrange(kin, p=P),
                I["ffn2_w_down_2"][0].rearrange(kin, p=P))
            wg = I["w_ple_gate_2"][0].rearrange(kin, p=P)
            for j in range(4):
                square(C_PG + j, wg, CW * j)
                if j == 0:
                    sp.wait_ge(tile_done, 2 * C_PG)
                    sp.dma_start(pt[:], I["p_2"][0, 0].rearrange("(b p) d -> p b d", p=P)).then_inc(p_in, 16)
            wp = I["w_ple_proj_2"][0].rearrange(kin, p=P)
            s = slot(C_PP, 2, D)
            load(C_PP, [(s[:, 0:1], wp[:, 0:1]), (s[:, 1:2], wp[:, 1:2])])
            for n in range(DK):
                sp.wait_ge(o_copied, n + 1)
                sp.dma_start(out[0].rearrange("(b p) d -> p b d", p=P)[:, :, P * n:P * n + P],
                             ot[:, :, P * n:P * n + P]).then_inc(o_out, 16)
            sp.wait_ge(o_out, 16 * DK)

        @block.gpsimd
        def _(pool):
            pool.memset(ident[:], 0.0).then_inc(consts, 1)
            pool.memset(causal[:], 0.0).then_inc(consts, 1)
            pool.memset(strict[:], 0.0).then_inc(consts, 1)
            pool.memset(onesblk[:], 0.0).then_inc(consts, 1)
            pool.wait_ge(consts, 4)
            tri = dict(pattern=[[-1, P]], channel_multiplier=1)
            pool.affine_select(out=ident[:], in_=ident[:], compare_op=ALU.not_equal, fill=1.0, base=0, **tri).then_inc(consts, 1)
            pool.affine_select(out=causal[:], in_=causal[:], compare_op=ALU.is_ge, fill=NEG, base=0, **tri).then_inc(consts, 1)
            pool.affine_select(out=strict[:], in_=strict[:], compare_op=ALU.is_ge, fill=NEG, base=-1, **tri).then_inc(consts, 1)
            for z, o in enumerate((0, HEAD_DIM)):
                pool.wait_ge(consts, 7 + z)
                pool.memset(onesblk[o:o + HEAD_DIM, o:o + HEAD_DIM], 1.0).then_inc(consts, 1)

            def low(c, per=0, i=None):
                n = n_cols(c)
                pool.wait_ge(w_hi, lin(c + 1, per, i))
                pool.tensor_tensor(wlo[:, c % 2, 0:n], raw[:, c % 2, 0:n], whi[:, c % 2, 0:n].bitcast(F32),
                                   ALU.subtract).then_inc(w_lo, 1)

            def run(c0, c1, body):
                with pool.Fori(0, (c1 - c0) // body) as i:
                    for j in range(body):
                        low(c0 + j, body, i)

            pool.wait_ge(consts, 9)
            low(C_LAT)
            low(C_QI)
            run(C_Q, C_D[0], 2)
            run(C_D[0], C_F[1], 6)
            run(C_F[1], C_D[1], 2)
            run(C_D[1], C_FQ, 6)
            run(C_FQ, C_FL, 2)
            pool.wait_ge(tile_done, 2 * C_FQ)
            pool.memset(sel[:], 0.0).then_inc(consts, 1)
            pool.memset(fF[:], 0.0).then_inc(consts, 1)
            pool.memset(fone[:], 1.0).then_inc(consts, 1)
            for z, first in enumerate((0, SEL_LO)):
                pool.wait_ge(consts, 12 + z)
                pool.affine_select(out=sel[:], in_=sel[:], compare_op=ALU.not_equal, fill=1.0, base=-first,
                                   pattern=[[-1, HEADS], [0, P]], channel_multiplier=1).then_inc(consts, 1)
            low(C_FL)
            run(C_FV, C_D[2], 2)
            run(C_D[2], C_PG, 6)
            run(C_PG, C_PP, 2)
            low(C_PP)

        @block.tensor
        def _(pe):
            def passes(o, s, w_of, xhi, xlo, first, last):
                pe.matmul(o, w_of(whi), xhi, start=first, stop=False)
                pe.matmul(o, w_of(whi), xlo, start=False, stop=False)
                return pe.matmul(o, w_of(wlo), xhi, start=False, stop=last)

            def x_ready(X, k, t):
                if t == 0:
                    pe.wait_ge(x_split, DK * X + k + 1)

            def chunk(c, hi, lo, per=0, i=None, X=None, full=(False, False), widths=(P, P), between=None, steps=None, ready=None):
                s, w = c % 2, sum(widths)
                pe.wait_ge(w_lo, lin(c + 1, per, i))
                for t in range(2):
                    if c >= 2:
                        pe.wait_ge(acc_free, lin(2 * (c - 2) + t + 1, 2 * per, i))
                    b, m, o0 = bank(c, t), widths[t], sum(widths[:t])
                    for k in range(DK):
                        if X is not None:
                            x_ready(X, k, t)
                        if ready is not None and t == 0:
                            pe.wait_ge(m_split, ready + k + 1)
                        w_of = lambda wt: wt[:, s, w * k + o0:w * k + o0 + m]
                        if full[t]:
                            for z in range(2):
                                cs = slice(HALF * z, HALF * z + HALF)
                                mm = passes(ps[0:m, b + z, 0:HALF], s, w_of, hi[:, k, cs], lo[:, k, cs], k == 0, k == DK - 1)
                        else:
                            cs = slice(0, T) if hi.shape[2] == T else slice(META, TM)
                            mm = passes(ps[0:m, b, :], s, w_of, hi[:, k, cs], lo[:, k, cs], k == 0, k == DK - 1)
                        if k == DK - 1:
                            mm.then_inc(tile_done, 1)
                        if steps and k in THIRDS:
                            steps(3 * t + THIRDS.index(k))
                    if t == 0 and between:
                        between()

            THIRDS = (2, 5, DK - 1)

            def norm_sums(S, c):
                pe.wait_ge(ssum_done, 9 * (S + 1))
                if S == 0:
                    for z in range(2):
                        mm = pe.matmul(ps[:, 5 + 2 * z, 0:HALF], ones[:], ssum[:, HALF * z:HALF * z + HALF], start=True, stop=True)
                else:
                    mm = pe.matmul(ps[:, bank(c + 1, 0) + 1, :], ones[:], ssum[:, META:TM], start=True, stop=True)
                if S == 2:
                    pe.wait_ge(ssum2_done, 9)
                    mm = pe.matmul(ps[:, bank(c + 1, 1) + 1, :], ones[:], ssum2, start=True, stop=True)
                mm.then_inc(ss_done, 1)

            def pair(c, hi_a, lo_a, hi_b, lo_b, per, i):
                s = c % 2
                pe.wait_ge(w_lo, lin(c + 1, per, i))
                for t in range(2):
                    pe.wait_ge(acc_free, lin(2 * (c - 2) + t + 1, 2 * per, i))
                    for z, (h, l) in enumerate(((hi_a, lo_a), (hi_b, lo_b))):
                        for k in range(4):
                            o = CW * (4 * z + k) + P * t
                            mm = passes(ps[:, bank(c, t) + z, :], s, lambda wt: wt[:, s, o:o + P],
                                        h[:, k, :], l[:, k, :], k == 0, k == 3)
                    mm.then_inc(tile_done, 1)

            def ffn(f, S, X):
                c = C_F[f]
                chunk(c, xh, xl, X=X, between=lambda: norm_sums(S, c))
                chunk(c + 1, xh, xl)
                with pe.Fori(0, FK // 2 - 1) as i:
                    for j in range(2):
                        chunk(c + 2 + j, xh, xl, 2, i)
                c = C_D[f]
                with pe.Fori(0, 2) as i:
                    for j in range(2):
                        for r, kn in enumerate(DOWN_K):
                            cr, k0 = c + 3 * j + r, sum(DOWN_K[:r])
                            pe.wait_ge(w_lo, lin(cr + 1, 6, i))
                            if j == 0:
                                pe.wait_ge(h_split, FK * f + k0 + kn)
                            for t in range(2):
                                if r == 0:
                                    pe.wait_ge(acc_free, lin(2 * (c - 2 + j) + t + 1, 4 * j + 2 * t + 6, i))
                                for k in range(kn):
                                    o = CW * k + P * t
                                    mm = passes(ps[:, bank(c + j, t), :], cr % 2, lambda wt: wt[:, cr % 2, o:o + P],
                                                fh[:, k0 + k, :], fl[:, k0 + k, :], r == 0 and k == 0, r == 2 and k == kn - 1)
                                mm.then_inc(tile_done, 1)

            pe.wait_ge(consts, 9)
            pe.wait_ge(vec_in, 16 * 15)
            pe.transpose(ps[:, 7, 0:V_ROWS], vt[:], ident[0:V_ROWS, 0:V_ROWS]).then_inc(vec_turned, 1)
            pe.wait_ge(x_in, 32)
            for n in range(DK):
                b = 2 * (n % 4)
                if n >= 4:
                    pe.wait_ge(x_copied, 2 * (n - 3))
                for q in range(QB):
                    pe.transpose(ps[:, b, P * q:P * q + P], xt[:, q, P * n:P * n + P], ident[:])
                if n == 3:
                    pe.wait_ge(vec_done, 1)
                pe.transpose(ps[:, b + 1, 0:META], mt[:, P * n:P * n + P], ident[0:META, 0:META]).then_inc(x_turned, 1)

            pe.wait_ge(x_copied, 12)
            chunk(C_LAT, xh, xl, X=0, full=(True, True), widths=(P, KW))
            chunk(C_QI, xh, xl, between=lambda: norm_sums(0, C_QI))
            chunk(C_Q, xh, xl)
            pe.wait_ge(acc_free, 2)
            for q in range(QB):
                mm = pe.transpose(ps[:, 1, HEADS * q:HEADS * q + HEADS], kw[D_IDX:KW, META + P * q:META + P * q + P],
                                  ident[D_IDX:KW, D_IDX:KW])
            mm.then_inc(wi_turned, 1)
            pe.wait_ge(ki_rep, 64)
            pe.wait_ge(acc_free, 2 * C_QI + 2)
            pe.wait_ge(wi_done, 1)
            for n in range(QB * HEADS):
                q, h = divmod(n, HEADS)
                wq = (META + P * (q + 1)) // 2
                g = D_IDX * (h % 4)
                if n >= 2:
                    pe.wait_ge(relu_done, n - 1)
                for z in range(2):
                    mm = pe.matmul(ps[:, 4 + 2 * (n % 2) + z, 0:wq], qiT[g:g + D_IDX, h // 4, P * q:P * q + P],
                                   kiT[g:g + D_IDX, wq * z:wq * z + wq], start=True, stop=True)
                mm.then_inc(s_ready, 1)
            pe.wait_ge(csq_done, 1)
            pe.wait_ge(acc_free, 2 * C_Q + 1)
            for z in range(2):
                mm = pe.matmul(ps[:, z, 0:HALF], ones[:], sq[:, HALF * z:HALF * z + HALF], start=True, stop=True)
            mm.then_inc(css_done, 1)
            pe.wait_ge(relu_done, QB * HEADS)
            chunk(C_Q + 1, xh, xl)
            pe.wait_ge(c_done, 1)
            for q in range(QB):
                pe.transpose(ps[:, 5, P * q:P * q + P], cT[:, META + P * q:META + P * q + P], ident[:])
            pe.transpose(ps[0:META, 7, 0:P], cT[:, 0:META], ident[:]).then_inc(c_turned, 1)
            chunk(C_Q + 2, xh, xl)
            chunk(C_Q + 3, xh, xl)
            pe.wait_ge(ctok_done, 2)
            for c in range(C_U, C_CB):
                chunk(c, xh, xl, full=(True, True))
            chunk(C_CB, xh, xl)
            pe.wait_ge(misc_in, 32)
            pe.wait_ge(acc_free, 2 * C_CB)
            for g in range(4):
                pe.wait_ge(pooled_done, g + 1)
                pe.matmul(ps[:, 2 * g + 1, :], pwt[:, g, :], pooled[:, g, :], start=True, stop=True).then_inc(mix_done, 1)
            chunk(C_CB + 1, xh, xl)

            with pe.Fori(0, 2) as i:
                for q in range(2):
                    c = C_AC + 3 * q
                    chunk(c, xh, xl, 6, i)
                    chunk(c + 1, xh, xl, 6, i)
                    if q == 0:
                        pe.wait_ge(a_split, 4)
                        pe.wait_ge(co_split, 4)
                    pair(c + 2, ah, al, coh, col_, 6, i)

            def attention(A, read, scores, key_tiles, value_piece, bank_left, extra=0):
                def qk(n):
                    if n >= 2:
                        pe.wait_ge(A[read], n - 1)
                    scores(n).then_inc(A["lg_ready"], 1)

                def step(n):
                    if n + 2 < QB * HEADS:
                        qk(n + 2)
                    h, q = divmod(n, QB)
                    if n < QB * HEADS:
                        pe.wait_ge(A["p_ready"], n + 1)
                        if n >= 1:
                            pe.wait_ge(A["pt_copy_a"], n)
                            if extra:
                                pe.wait_ge(A["pt_copy_d"], n)
                        key_tiles(n, q).then_inc(A["pt_ready"], 1)
                    if h >= 1:
                        if q == 0:
                            pe.wait_ge(A["pt_copy_a"], n)
                            if extra:
                                pe.wait_ge(A["pt_copy_d"], n)
                            bank_left(h - 1)
                        mm = value_piece(h - 1, q)
                        if q == QB - 1:
                            mm.then_inc(A["pv_ready"], 1)
                return qk, step

            A = att["dsa"]
            pe.wait_ge(acc_free, 2 * C_B)

            def dsa_scores(n):
                h, q = divmod(n, QB)
                w = META + P * (q + 1)
                b = 2 * (n % 2)
                mm = pe.matmul(ps[:, b, 0:min(w, 512)], qT[:, h, P * q:P * q + P], cT[:, 0:min(w, 512)], start=True, stop=True)
                if w > 512:
                    mm = pe.matmul(ps[:, b + 1, 0:w - 512], qT[:, h, P * q:P * q + P], cT[:, 512:w], start=True, stop=True)
                return mm

            def dsa_turn(n, q):
                src = pr[:, n % 2]
                for j in range(q + 1):
                    pe.transpose(ps[:, 4, P * j:P * j + P], src[:, META + P * j:META + P * j + P], ident[:])
                return pe.transpose(ps[0:META, 5, 0:P], src[:, 0:META], ident[:])

            def dsa_piece(h, q):
                o, p = ps[:, 6 + h % 2, :], pT[h % 2]
                if q == 0:
                    return pe.matmul(o, ctok[0:META, QB, :], p[0:META, QB, :], start=True, stop=False)
                for j in ((0,), (1,), (2, 3))[q - 1]:
                    mm = pe.matmul(o[:, P * j:T], ctok[:, j, :], p[:, j, P * j:T], start=False, stop=j == QB - 1)
                return mm

            def dsa_split(h):
                if h >= 2:
                    pe.wait_ge(A["y_split"], h - 1)

            qk, step = attention(A, "mx_done", dsa_scores, dsa_turn, dsa_piece, dsa_split, extra=1)
            qk(0)
            qk(1)
            for n in range(QB * HEADS + QB):
                step(n)

            with pe.Fori(0, 4) as i:
                chunk(C_B, xh, xl, 2, i)
                pe.wait_ge(att["dsa"]["y_split"], HEADS)
                chunk(C_B + 1, ath, atl, 2, i)
            with pe.Fori(0, 2) as i:
                for j in range(2):
                    chunk(C_O + j, mh, ml, 2, i, ready=0)
            ffn(0, 1, 1)

            ffn(1, 2, 2)
            chunk(C_FQ, xh, xl, X=3, between=lambda: norm_sums(3, C_FQ))

            def head_sums(n):
                pe.wait_ge(hq_done, n + 1)
                if n >= 2:
                    pe.wait_ge(hq_rt, n - 1)
                pe.matmul(ps[:, 5 + 2 * (n % 2), :], onesblk[:], rtq[:, n % 4, :], start=True, stop=True).then_inc(hq_ss, 1)

            chunk(C_FQ + 1, xh, xl)
            pe.wait_ge(rs_done, 4)
            for q in range(QB):
                mm = pe.transpose(ps[:, 1, P * q:P * q + P], rs[:, META + P * q:META + P * q + P], ident[:])
            mm.then_inc(rtok_turned, 1)
            head_sums(0)
            head_sums(1)
            for n, c in ((2, C_FK), (4, C_FK + 1)):
                chunk(c, xh, xl)
                head_sums(n)
                head_sums(n + 1)

            def tokens(c, steps=None):
                s = c % 2
                pe.wait_ge(w_lo, c + 1)
                for t in range(2):
                    pe.wait_ge(acc_free, 2 * (c - 2) + t + 1)
                    for z in range(2):
                        q = 2 * t + z
                        o = ps[:, bank(c, t), CW * z:CW * z + CW]
                        for k in range(DK):
                            th, tl = (x[:, k, META + P * q:META + P * q + P] for x in (xh, xl))
                            ch, clo = (wt[:, s, CW * k:CW * k + CW] for wt in (whi, wlo))
                            pe.matmul(o, th, ch, start=k == 0, stop=False)
                            pe.matmul(o, th, clo, start=False, stop=False)
                            mm = pe.matmul(o, tl, ch, start=False, stop=k == DK - 1)
                            if z and k == DK - 1:
                                mm.then_inc(tile_done, 1)
                            if steps and (z, k) in ((0, 4), (1, 2), (1, DK - 1)):
                                steps(3 * t + ((0, 4), (1, 2), (1, DK - 1)).index((z, k)))

            pe.wait_ge(w_lo, C_FL + 1)
            pe.wait_ge(acc_free, 2 * (C_FL - 2) + 1)
            for k in range(DK):
                mm = passes(ps[0:HEADS, bank(C_FL, 0), :], 0, lambda wt: wt[:, C_FL % 2, HEADS * k:HEADS * k + HEADS],
                            xh[:, k, META:TM], xl[:, k, META:TM], k == 0, k == DK - 1)
            mm.then_inc(tile_done, 2)
            head_sums(6)
            head_sums(7)
            tokens(C_FV)
            tokens(C_FV + 1)

            F = att["fox"]

            def row(h):
                return HEAD_DIM * (h % 2)

            def fox_scores(n):
                h, q = divmod(n, QB)
                w, r = P * (q + 1), row(h)
                b = 2 * (n % 2) + 1
                pe.matmul(ps[:, b, 0:w], qF[r:r + HEAD_DIM, h // 2, P * q:P * q + P], kF[r:r + HEAD_DIM, h // 2, 0:w],
                          start=True, stop=False, skip_group_check=True)
                pe.matmul(ps[:, b, 0:w], selr[:, h, :], fFs[:, 0:w], start=False, stop=False, skip_group_check=True)
                return pe.matmul(ps[:, b, P * q:w], identr[:], causalr[:], start=False, stop=True, skip_group_check=True)

            def turn(n, q):
                for j in range(q + 1):
                    mm = pe.transpose(ps[:, 5, P * j:P * j + P], pu[:, n % UNITS, P * j:P * j + P], ident[:])
                return mm

            def value_piece(v):
                def piece(h, j):
                    o, r = ps[row(h):row(h) + HEAD_DIM, 7, :], row(h)
                    return pe.matmul(o[:, P * j:T], v[:, j, HEAD_DIM * h:HEAD_DIM * h + HEAD_DIM],
                                     fpT[h % 2][:, j, P * j:T], start=j == 0, stop=j == QB - 1)
                return piece

            def pair_split(A):
                def wait(h):
                    if h % 2 == 0 and h:
                        pe.wait_ge(A["y_split"], h // 2)
                return wait

            qk, step = attention(F, "exp_done", fox_scores, turn, value_piece(vF), pair_split(F))
            pe.wait_ge(hq_out, 8)
            pe.wait_ge(f_lo, 1)
            pe.wait_ge(sel_done, 1)
            pe.wait_ge(rtok_done, 1)
            qk(0)
            qk(1)
            for j in range(6):
                c = C_SQ + j
                run = lambda third: step(6 * j + third)
                if c < C_SV:
                    chunk(c, xh, xl, steps=run)
                else:
                    tokens(c, steps=run)

            B = att["sb"]

            def sb_scores(n):
                h, q = divmod(n, QB)
                w, r = P * (q + 1), row(h)
                b = 2 * (n % 2) + 1
                pe.matmul(ps[:, b, 0:w], qS[r:r + HEAD_DIM, h // 2, P * q:P * q + P],
                          kS[r:r + HEAD_DIM, h // 2, 0:w], start=True, stop=False, skip_group_check=True)
                return pe.matmul(ps[:, b, P * q:w], identr[:], strictr[:], start=False, stop=True, skip_group_check=True)

            qk, step = attention(B, "lg_read", sb_scores, turn, value_piece(vS), pair_split(B))
            pe.wait_ge(acc_free, 2 * C_SV)
            pe.wait_ge(F["exp_done"], QB * HEADS)
            qk(0)
            qk(1)
            pe.wait_ge(acc_free, 2 * C_GF)
            pe.wait_ge(F["y_split"], 4)
            for j in range(8):
                def run(third):
                    for n in SB_STEPS[6 * j + third]:
                        step(n)
                chunk(C_GF + j, xh, xl, steps=run)

            pe.wait_ge(B["y_split"], 4)
            with pe.Fori(0, 2) as i:
                for q in range(2):
                    pair(C_MX + q, yfh, yfl, ysh, ysl, 2, i)
            with pe.Fori(0, 2) as i:
                for j in range(2):
                    chunk(C_O2 + j, m2h, m2l, 2, i, ready=DK)
            ffn(2, 4, 4)

            chunk(C_PG, xh, xl, X=5, between=lambda: norm_sums(5, C_PG))
            chunk(C_PG + 1, xh, xl)
            pe.wait_ge(p_in, 16)
            pe.wait_ge(rs_done, 6)
            for j in range(2):
                for q in range(QB):
                    mm = pe.transpose(ps[:, 1 + 2 * j, P * q:P * q + P], pt[:, q, P * j:P * j + P], ident[:])
                mm.then_inc(p_turned, 1)
            chunk(C_PG + 2, xh, xl)
            chunk(C_PG + 3, xh, xl)
            pe.wait_ge(p_split, 2)
            pe.wait_ge(w_lo, C_PP + 1)
            pe.wait_ge(acc_free, 2 * C_PP)

            def turn_back(n):
                pe.wait_ge(o_done, n + 1)
                if n >= 4:
                    pe.wait_ge(o_copied, n - 3)
                for q in range(QB):
                    mm = pe.transpose(ps[:, 2 * (n % 4), P * q:P * q + P], hT[:, n, META + P * q:META + P * q + P], ident[:])
                mm.then_inc(o_turned, 1)

            for n in range(DK):
                if n >= 4:
                    pe.wait_ge(acc_free, 2 * C_PP + n - 3)
                for k in range(2):
                    o = D * k + P * n
                    mm = passes(ps[:, 2 * (n % 4) + 1, :], 0, lambda wt: wt[:, C_PP % 2, o:o + P],
                                pTh[:, k, :], pTl[:, k, :], k == 0, k == 1)
                mm.then_inc(tile_done, 1)
                if n >= 2:
                    turn_back(n - 2)
            turn_back(DK - 2)
            turn_back(DK - 1)

        @block.scalar
        def _(act):
            for r0, a in ((V_N1, "norm1_g"), (V_N2, "norm2_g"), (V_FIN, "final_g"), (V_F1, "ffn1_norm_2"), (V_MX, "mix_norm_2"),
                          (V_F2, "ffn2_norm_2"), (V_PL, "ple_norm_2"), (V_BG, "b_gate"), (V_PS, "pool_scale"), (V_KV, "kv_norm_g")):
                a = I[a] if len(I[a].shape) == 1 else I[a][0]
                n = a.shape[0] // P
                act.dma_start(vt[r0:r0 + n, :], a.rearrange("(r c) -> r c", c=P)).then_inc(vec_in, 16)
            act.dma_start(vt[V_CW:V_CW + 12, :], I["conv_w"][0].rearrange("w (r c) -> (w r) c", c=P)).then_inc(vec_in, 16)
            for r0, a in ((V_QN, "q_norm_2"), (V_KN, "k_norm_2")):
                for z in range(2):
                    act.dma_start(vt[r0:r0 + 1, HEAD_DIM * z:HEAD_DIM * z + HEAD_DIM], I[a]).then_inc(vec_in, 16)
            act.dma_start(mt[:], I["meta"]).then_inc(x_in, 16)

            def high(c, per=0, i=None):
                n = n_cols(c)
                act.wait_ge(raw_in[c % 2], raw_level(c, per, i))
                if c >= 2:
                    act.wait_ge(tile_done, lin(2 * (c - 1), 2 * per, i))
                act.activation(whi[:, c % 2, 0:n], raw[:, c % 2, 0:n], ACT.Copy).then_inc(w_hi, 1)

            def gained(n, gain, per=0, i=None, lo=META):
                nn = lin(n, per, i)
                act.activation(one(xh, nn)[:, lo:TM], one(hT, nn)[:, lo:TM], ACT.Copy,
                               scale=col(vec, lin(gain + n, per, i))).then_inc(xh_done, 1)

            def added(S, n, per=0, i=None):
                if S or n:
                    act.wait_ge(ssum_done, lin(9 * S + n + (1 if n else 0), per, i))

            def square(n, per=0, i=None, lo=META):
                act.activation(sq[:, lo:TM], one(hT, lin(n, per, i))[:, lo:TM], ACT.Square).then_inc(sq_done, 1)

            def feed(S, n, gain, per=0, i=None):
                added(S, n, per, i)
                if S == 2 and n:
                    act.wait_ge(ssum2_done, lin(n + 1, per, i))
                gained(n, gain, per, i)
                square(n, per, i)
                if S == 2:
                    act.activation(sq2, one(hT, lin(n, per, i))[:, META:TM], ACT.Square,
                                   scale=col(vec, lin(V_FIN + n, per, i))).then_inc(sq2_done, 1)

            def root(S):
                act.wait_ge(ss_done, S + 1)
                if S == 0:
                    act.activation(rt[:, 0:HALF], ps[:, 5, 0:HALF], ACT.Sqrt, bias=eps[:], scale=1.0 / D)
                    act.activation(rt[:, HALF:TM], ps[:, 7, 0:HALF], ACT.Sqrt, bias=eps[:], scale=1.0 / D).then_inc(rt_done, 1)
                else:
                    c = {1: C_F[0], 2: C_F[1], 3: C_FQ, 4: C_F[2], 5: C_PG}[S]
                    act.activation(rt[:, META:TM], ps[:, bank(c + 1, 0) + 1, :], ACT.Sqrt,
                                   bias=eps[:], scale=1.0 / D).then_inc(rt_done, 1)

            def ffn(f, S, gain):
                c = C_F[f]

                def up(c, n, per=0, i=None):
                    high(c + 2, per, i)
                    act.wait_ge(acc_free, lin(2 * c + 1, 2 * per, i))
                    act.activation(tmp[:, 1, :], tmp[:, 0, :], ACT.Silu).then_inc(silu_done, 1)
                    act.wait_ge(h_done, lin(FK * f + n + 1, per, i))
                    act.activation(one(fh, lin(n, per, i)), tmp[:, 3, :], ACT.Copy).then_inc(h_hi, 1)

                root(S)
                if f == 1:
                    act.wait_ge(ms2_done, 1)
                    act.activation(rt[:, META:TM], ssum2, ACT.Sqrt, bias=eps[:], scale=1.0 / D).then_inc(rt2_done, 1)
                with act.Fori(0, FK // 2) as i:
                    for j in range(2):
                        up(c + j, j, 2, i)
                d = C_D[f]
                with act.Fori(0, 2) as i:
                    for j in range(2):
                        high(d + 3 * j + 2, 6, i)
                        high(d + 3 * j + 3, 6, i)
                        act.wait_ge(acc_free, lin(2 * d + 6 * j + 3, 12, i))
                        feed(S + 1, 2 * j, gain, 4, i)
                        act.wait_ge(acc_free, lin(2 * d + 6 * j + 6, 12, i))
                        feed(S + 1, 2 * j + 1, gain, 4, i)
                        high(d + 3 * j + 4, 6, i)

            def project(c, S, gain):
                with act.Fori(0, 2) as i:
                    for j in range(2):
                        act.wait_ge(acc_free, lin(2 * (c + j) + 1, 4, i))
                        feed(S, 2 * j, gain, 4, i)
                        act.wait_ge(acc_free, lin(2 * (c + j) + 2, 4, i))
                        feed(S, 2 * j + 1, gain, 4, i)
                        high(c + j + 2, 2, i)

            act.wait_ge(vec_turned, 1)
            act.activation(vec[:, 0:V_ROWS], ps[:, 7, 0:V_ROWS], ACT.Copy).then_inc(vec_done, 1)
            act.wait_ge(vec_done, 1)
            for n in range(DK):
                act.wait_ge(x_turned, n + 1)
                act.activation(hT[:, n, META:TM], ps[:, 2 * (n % 4), :], ACT.Copy).then_inc(x_copied, 1)
                act.activation(hT[:, n, 0:META], ps[:, 2 * (n % 4) + 1, 0:META], ACT.Copy).then_inc(x_copied, 1)
                act.wait_ge(x_copied, 2 * n + 2)
                gained(n, V_N1, lo=0)
                if n == 0:
                    high(0)
            high(1)
            for n in range(DK):
                added(0, n)
                square(n, lo=0)
            act.wait_ge(ones_done, 1)
            root(0)
            high(C_LAT + 2)
            act.wait_ge(acc_free, 2 * C_LAT + 2)
            for g in range(4):
                act.dma_start(kiT[D_IDX * g:D_IDX * g + D_IDX, :], kw[0:D_IDX, :]).then_inc(ki_rep, 16)
            act.activation(sq[:], cl[:], ACT.Square).then_inc(csq_done, 1)
            high(C_QI + 2)
            high(C_Q + 2)
            for n in range(QB * HEADS):
                q = n // HEADS
                wq = (META + P * (q + 1)) // 2
                act.wait_ge(s_ready, n + 1)
                if n >= 2:
                    act.wait_ge(score_acc, n - 1)
                b = 4 + 2 * (n % 2)
                act.activation(rl[:, n % 2, 0:2 * wq].rearrange("p (z k) -> p z k", z=2), ps[:, b:b + 2, 0:wq],
                               ACT.Relu).then_inc(relu_done, 1)
            act.wait_ge(css_done, 1)
            act.activation(rt[:].rearrange("p (z t) -> p z t", z=2), ps[:, 0:2, 0:HALF], ACT.Sqrt,
                           bias=eps[:], scale=1.0 / D_LAT).then_inc(crt_done, 1)
            high(C_Q + 3)
            act.wait_ge(c_turned, 1)
            act.activation(ctok[:, 0:QB, :].rearrange("p q d -> p (q d)"), ps[:, 5, :], ACT.Copy).then_inc(ctok_done, 1)
            act.activation(ctok[0:META, QB, :], ps[0:META, 7, 0:P], ACT.Copy).then_inc(ctok_done, 1)
            act.dma_start(pwt[:], I["pool_w"][0].rearrange("g c d -> c g d")).then_inc(misc_in, 16)
            act.dma_start(fbias[:], I["forget_bias_2"][0].rearrange("(h o) -> h o", o=1)).then_inc(misc_in, 16)
            for c in range(C_Q + 2, C_CB):
                high(c + 2)
            high(C_CB + 2)
            for g in range(2):
                act.wait_ge(co_done, g + 1)
                act.activation(coh[:, g, :], co[:], ACT.Copy).then_inc(coh_done, 1)
            for g in range(4):
                act.wait_ge(mix_done, g + 1)
                act.activation(ah[:, g, :], ps[:, 2 * g + 1, :], ACT.Copy, scale=col(vec, V_PS + g)).then_inc(ah_done, 1)
            high(C_CB + 3)
            for g in range(2, 4):
                act.wait_ge(co_done, g + 1)
                act.activation(coh[:, g, :], co[:], ACT.Copy).then_inc(coh_done, 1)

            def gate(c, kind, q, bias, per, i):
                for t in range(2):
                    act.wait_ge(acc_free, lin(2 * c + t + 1, 2 * per, i))
                    g = tmp[:, 2 * kind + t, :]
                    b = {} if bias is None else {"bias": col(vec, lin(bias + 2 * q + t, 4, i))}
                    act.activation(g, g, ACT.Sigmoid, **b).then_inc(sig_done, 1)

            with act.Fori(0, 2) as i:
                for q in range(2):
                    c = C_AC + 3 * q
                    high(c + 2, 6, i)
                    gate(c, 0, q, V_BG, 6, i)
                    high(c + 3, 6, i)
                    gate(c + 1, 1, q, V_BG + 2 * DK, 6, i)
                    high(c + 4, 6, i)

            def probabilities(A, n, src, dst):
                act.wait_ge(A["mx_done"], n + 1)
                act.activation(dst, src, ACT.Exp, bias=nmx[:, n:n + 1], scale=-1.0,
                               accum_out=den[:, n:n + 1]).then_inc(A["exp_done"], 1)

            def copy_turned(A, n, bank_no, turned):
                h, q = divmod(n, QB)
                act.wait_ge(A["pt_ready"], n + 1)
                if h >= 2:
                    act.wait_ge(A["pv_ready"], h - 1)
                act.activation(turned[h % 2][:, 0:q + 1, P * q:P * q + P],
                               ps[:, bank_no, 0:P * (q + 1)].rearrange("p (j t) -> p j t", j=q + 1),
                               ACT.Copy).then_inc(A["pt_copy_a"], 1)

            A = att["dsa"]
            act.preload_act_table_set("exp_and_others")

            def dsa_unit(n):
                w = META + P * (n % QB + 1)
                if n >= 2:
                    act.wait_ge(A["pt_ready"], n - 1)
                probabilities(A, n, lm[:, n % 2, 0:w], pr[:, n % 2, 0:w])

            dsa_unit(0)
            dsa_unit(1)
            for n in range(QB * HEADS + QB):
                if n < QB * HEADS:
                    copy_turned(A, n, 4, pT)
                if n + 2 < QB * HEADS:
                    dsa_unit(n + 2)
                if n % QB == QB - 1 and n >= QB:
                    h = n // QB - 1
                    act.wait_ge(A["pv_ready"], h + 1)
                    act.activation(ath[:, h, :], ps[:, 6 + h % 2, :], ACT.Copy).then_inc(A["hi_done"], 1)

            def merged(hi, n, t, buf, m0, per, i):
                act.wait_ge(m_done, lin(m0 + n, per, i))
                act.activation(one(hi, lin(n - 1, per, i)), buf, ACT.Copy).then_inc(mh_done, 1)

            with act.Fori(0, 4) as i:
                for t in range(2):
                    act.wait_ge(acc_free, lin(2 * C_B + t + 1, 4, i))
                    act.activation(tmpb[:, t, :], tmpb[:, t, :], ACT.Sigmoid,
                                   bias=col(vec, lin(V_BG + DK + t, 2, i))).then_inc(sig_done, 1)
                high(C_B + 2, 2, i)
                merged(mh, 1, 0, tmpb[:, 0, :], DK, 2, i)
                merged(mh, 2, 1, tmpb[:, 1, :], DK, 2, i)
                high(C_B + 3, 2, i)
            project(C_O, 1, V_N2)
            act.wait_ge(gain_done, 1)
            ffn(0, 1, V_FP)

            ffn(1, 2, V_MX)
            root(3)

            def head_root(n):
                act.wait_ge(hq_ss, n + 1)
                act.activation(rtq[:, n % 4, :], ps[:, 5 + 2 * (n % 2), :], ACT.Sqrt, bias=eps[:],
                               scale=1.0 / HEAD_DIM).then_inc(hq_rt, 1)

            def head_square(n, c):
                act.wait_ge(acc_free, 2 * c + n % 2 + 1)
                if n >= 4:
                    act.wait_ge(hq_out, n - 3)
                act.activation(rtq[:, n % 4, :], qs[:, n % 4, :], ACT.Square).then_inc(hq_done, 1)

            for n0, c in ((0, C_FQ), (2, C_FQ + 1), (4, C_FK), (6, C_FK + 1)):
                high(c + 2)
                head_square(n0, c)
                head_square(n0 + 1, c)
                if n0:
                    head_root(n0 - 2)
                    head_root(n0 - 1)
            act.wait_ge(consts, 14)
            act.activation(selr[:], sel[:], ACT.Copy).then_inc(sel_done, 1)
            head_root(6)
            head_root(7)
            high(C_FL + 2)
            act.preload_act_table_set("natural_log_exp_and_others")
            act.wait_ge(fz_done, 1)
            act.activation(ft[:], fz[:], ACT.Abs).then_inc(act_seq, 1)
            act.wait_ge(act_seq, 1)
            act.activation(ft[:], ft[:], ACT.Exp, scale=-1.0).then_inc(act_seq, 1)
            act.wait_ge(act_seq, 2)
            act.activation(ft[:], ft[:], ACT.Ln, bias=ones[0:HEADS, 0:1]).then_inc(ft_done, 1)
            act.wait_ge(f_done, 1)
            act.activation(fFs[:], fF[:], ACT.Copy).then_inc(f_hi, 1)
            high(C_FV + 2)
            high(C_FV + 3)

            F = att["fox"]

            def fox_unit(n):
                w = P * (n % QB + 1)
                if n >= UNITS:
                    act.wait_ge(F["pt_ready"], n - UNITS + 1)
                act.wait_ge(F["lg_ready"], n + 1)
                probabilities(F, n, ps[:, 2 * (n % 2) + 1, 0:w], pu[:, n % UNITS, 0:w])

            def pair_high(A, hi, n):
                if n % (2 * QB) == QB - 1 and n >= QB:
                    h = n // QB - 1
                    act.wait_ge(A["pv_ready"], h + 1)
                    act.activation(hi[:, h // 2, :], ps[:, 7, :], ACT.Copy).then_inc(A["hi_done"], 1)

            def fox_step(n):
                if n < QB * HEADS:
                    copy_turned(F, n, 5, fpT)
                if n + 2 < QB * HEADS:
                    fox_unit(n + 2)
                pair_high(F, yfh, n)

            fox_unit(0)
            fox_unit(1)
            for j in range(6):
                for third in range(6):
                    fox_step(6 * j + third)
                high(C_SQ + j + 2)

            B = att["sb"]

            def softplus(n):
                t = pu[:, n % UNITS, 0:P * (n % QB + 1)]
                act.wait_ge(z_capped, n + 1)
                act.activation(t, t, ACT.Exp).then_inc(act_seq, 1)
                act.wait_ge(act_seq, 3 + n)
                act.activation(t, t, ACT.Ln, bias=ones[:, 0:1]).then_inc(sp_done, 1)

            def sb_unit(n):
                t = pu[:, n % UNITS, 0:P * (n % QB + 1)]
                act.wait_ge(B["lg_read"], n + 1)
                act.activation(t, t, ACT.Exp).then_inc(B["p_ready"], 1)

            def sb_step(n):
                if n < QB * HEADS:
                    copy_turned(B, n, 5, fpT)
                if n + 2 < QB * HEADS:
                    softplus(n + 2)
                if n + 1 < QB * HEADS:
                    sb_unit(n + 1)
                pair_high(B, ysh, n)

            softplus(0)
            sb_unit(0)
            softplus(1)
            for j in range(8):
                for third in range(6):
                    for n in SB_STEPS[6 * j + third]:
                        sb_step(n)
                high(C_GF + j + 2)

            act.wait_ge(acc_free, 2 * C_MX)
            with act.Fori(0, 2) as i:
                for q in range(2):
                    for kind in range(2):
                        for t in range(2):
                            g = one(gates, lin(DK * kind + 2 * q + t, 4, i))
                            act.activation(g, g, ACT.Sigmoid).then_inc(sig_done, 1)
                    merged(m2h, 2 * q + 1, 0, one(gates, lin(2 * q, 4, i)), 2 * DK, 4, i)
                    merged(m2h, 2 * q + 2, 1, one(gates, lin(2 * q + 1, 4, i)), 2 * DK, 4, i)
                    high(C_MX + q + 2, 2, i)
            project(C_O2, 4, V_F2)
            ffn(2, 4, V_PL)
            root(5)

            for j in range(4):
                c = C_PG + j
                if c + 2 < N_CHUNKS:
                    high(c + 2)
                for t in range(2):
                    act.wait_ge(acc_free, 2 * c + t + 1)
                    act.activation(sg[:, 2 * j + t, :], sg[:, 2 * j + t, :], ACT.Sigmoid).then_inc(sig_done, 1)
                if j == 1:
                    for k in range(2):
                        act.wait_ge(p_turned, k + 1)
                        act.activation(ptT[:, k, :], ps[:, 1 + 2 * k, :], ACT.Copy).then_inc(p_copied, 1)
                        act.wait_ge(p_copied, k + 1)
                        act.activation(pTh[:, k, :], ptT[:, k, :], ACT.Copy).then_inc(ph_done, 1)
            for n in range(DK):
                act.wait_ge(o_turned, n + 1)
                act.activation(ot[:, :, P * n:P * n + P], ps[:, 2 * (n % 4), :].rearrange("p (q t) -> p q t", q=QB),
                               ACT.Copy).then_inc(o_copied, 1)

        @block.vector
        def _(dve):
            steps = [0]

            def link(ins):
                ins.then_inc(dve_seq, 1)
                steps[0] += 1
                dve.wait_ge(dve_seq, steps[0])

            def stt(o, a, s, b, op0, op1):
                return dve.scalar_tensor_tensor(o, a, s, b, op0, op1)

            def clear(S):
                if S:
                    dve.wait_ge(ss_done, S)
                dve.memset(ssum[:], 0.0).then_inc(ssum_done, 1)

            def split(X, n, gain, per=0, i=None, lo=META):
                nn = lin(n, per, i)
                dve.wait_ge(xh_done, lin(DK * X + n + 1, per, i))
                stt(one(xl, nn)[:, lo:TM], one(hT, nn)[:, lo:TM], col(vec, lin(gain + n, per, i)),
                    one(xh, nn)[:, lo:TM].bitcast(F32), ALU.mult, ALU.subtract).then_inc(x_split, 1)

            def add_square(S, n, per=0, i=None, lo=META):
                dve.wait_ge(sq_done, lin(DK * S + n + 1, per, i))
                dve.wait_ge(ssum_done, lin(9 * S + 1 + n, per, i))
                dve.tensor_tensor(ssum[:, lo:TM], ssum[:, lo:TM], sq[:, lo:TM], ALU.add).then_inc(ssum_done, 1)

            def feed(S, n, gain, per=0, i=None):
                split(S, n, gain, per, i)
                add_square(S, n, per, i)
                if S == 2:
                    dve.wait_ge(sq2_done, lin(n + 1, per, i))
                    dve.wait_ge(ssum2_done, lin(n + 1, per, i))
                    dve.tensor_tensor(ssum2, ssum2, sq2, ALU.add).then_inc(ssum2_done, 1)

            def root(S):
                lo = 0 if S == 0 else META
                dve.wait_ge(rt_done, S + 1)
                dve.reciprocal(rs[:, lo:TM], rt[:, lo:TM]).then_inc(rs_done, 1)
                dve.wait_ge(rs_done, S + 1)

            def closing_root():
                r = ssum[:, META:TM]
                dve.wait_ge(rt_done, 3)
                link(dve.reciprocal(r, rt[:, META:TM]))
                link(dve.tensor_tensor(ssum2, r, r, ALU.mult))
                dve.tensor_tensor(ssum2, ssum2, ps[:, bank(C_F[1] + 1, 1) + 1, :], ALU.mult).then_inc(ms2_done, 1)
                for n in range(DK):
                    x = hT[:, n, META:TM]
                    stt(x, x, vec[:, V_FIN + n:V_FIN + n + 1], r, ALU.mult, ALU.mult).then_inc(xn_done, 1)
                dve.wait_ge(xn_done, DK)
                dve.wait_ge(rt2_done, 1)
                link(dve.reciprocal(rsx, rt[:, META:TM]))
                dve.tensor_tensor(rsx, rsx, r, ALU.mult).then_inc(rs_done, 1)
                dve.wait_ge(rs_done, 3)

            rsx = rs[:, META:TM]
            rs2 = rs[:].rearrange("p (z t) -> p z t", z=2)

            def done(c, t, per=0, i=None):
                dve.wait_ge(tile_done, lin(2 * c + t + 1, 2 * per, i))

            def scaled(o, c, t, per=0, i=None):
                done(c, t, per, i)
                dve.tensor_tensor(o, ps[0:o.shape[0], bank(c, t), :], rsx[0:o.shape[0]], ALU.mult).then_inc(acc_free, 1)

            def scaled_full(o, c, t):
                done(c, t)
                m, b = o.shape[0], bank(c, t)
                dve.tensor_tensor(o.rearrange("p (z t) -> p z t", z=2), ps[0:m, b:b + 2, 0:HALF], rs2[0:m],
                                  ALU.mult).then_inc(acc_free, 1)

            def update(n, b, factor, inc, per=0, i=None):
                x = one(hT, lin(n, per, i))[:, META:TM]
                stt(x, ps[:, b, :], factor, x, ALU.mult, ALU.add).then_inc(acc_free, inc)

            def ffn(f, S, factor, gain):
                c = C_F[f]
                if f == 1:
                    closing_root()
                else:
                    root(S)
                with dve.Fori(0, FK // 2) as i:
                    for j in range(2):
                        n = FK * f + j
                        scaled(tmp[:, 0, :], c + j, 0, 2, i)
                        scaled(tmp[:, 2, :], c + j, 1, 2, i)
                        dve.wait_ge(silu_done, lin(n + 1, 2, i))
                        dve.wait_ge(acc_free, lin(2 * (c + j) + 2, 4, i))
                        dve.tensor_tensor(tmp[:, 3, :], tmp[:, 1, :], tmp[:, 2, :], ALU.mult).then_inc(h_done, 1)
                        dve.wait_ge(h_hi, lin(n + 1, 2, i))
                        nn = lin(j, 2, i)
                        dve.tensor_tensor(one(fl, nn), tmp[:, 3, :], one(fh, nn).bitcast(F32), ALU.subtract).then_inc(h_split, 1)
                        dve.wait_ge(h_split, lin(n + 1, 2, i))
                d = C_D[f]
                clear(S + 1)
                if S + 1 == 2:
                    dve.memset(ssum2, 0.0).then_inc(ssum2_done, 1)
                with dve.Fori(0, 2) as i:
                    for j in range(2):
                        for t in range(2):
                            n = 2 * j + t
                            done(d + 3 * j + 2, t, 6, i)
                            update(n, bank(d + j, t), factor, 3, 4, i)
                            dve.wait_ge(acc_free, lin(2 * d + 6 * j + 3 * t + 3, 12, i))
                            feed(S + 1, n, gain, 4, i)

            def project(c, S, gain):
                clear(S)
                with dve.Fori(0, 2) as i:
                    for j in range(2):
                        for t in range(2):
                            n = 2 * j + t
                            done(c + j, t, 2, i)
                            update(n, bank(c + j, t), 1.0, 1, 4, i)
                            dve.wait_ge(acc_free, lin(2 * (c + j) + t + 1, 4, i))
                            feed(S, n, gain, 4, i)

            dve.memset(eps[:], EPS)
            dve.memset(ones[:], 1.0).then_inc(ones_done, 1)
            clear(0)
            dve.wait_ge(consts, 9)
            dve.tensor_copy(identr[:], ident[:])
            dve.tensor_scalar(causalr[:], causal[:], -1.0, None, ALU.mult)
            dve.tensor_copy(strictr[:], strict[:])
            dve.wait_ge(vec_done, 1)
            dve.tensor_tensor(vec[:, V_FP:V_FP + DK], vec[:, V_FIN:V_FIN + DK], vec[:, V_F1:V_F1 + DK], ALU.mult).then_inc(gain_done, 1)
            dve.wait_ge(gain_done, 1)
            for n in range(DK):
                split(0, n, V_N1, lo=0)
            for n in range(DK):
                add_square(0, n, lo=0)
            root(0)

            scaled_full(cl[:], C_LAT, 0)
            scaled_full(kw[:], C_LAT, 1)
            for t in range(2):
                scaled(qiT[:, t, :], C_QI, t)

            def query(c):
                for t in range(2):
                    done(c, t)
                    stt(qT[:, 2 * (c - C_Q) + t, :], ps[:, bank(c, t), :], ATTN_SCALE, rsx, ALU.mult, ALU.mult).then_inc(acc_free, 1)

            query(C_Q)
            dve.wait_ge(wi_turned, 1)
            dve.tensor_scalar(wi[:].rearrange("p q h -> p (q h)"), ps[:, 1, 0:QB * HEADS], INDEX_SCALE, None,
                              ALU.mult).then_inc(wi_done, 1)
            dve.wait_ge(wi_done, 1)
            for n in range(QB * HEADS):
                q, h = divmod(n, HEADS)
                w = META + P * (q + 1)
                dve.wait_ge(relu_done, n + 1)
                if h == 0:
                    dve.tensor_scalar(sc[:, q, 0:w], rl[:, n % 2, 0:w], wi[:, q, h:h + 1], None, ALU.mult).then_inc(score_acc, 1)
                else:
                    dve.wait_ge(score_acc, n)
                    stt(sc[:, q, 0:w], rl[:, n % 2, 0:w], wi[:, q, h:h + 1], sc[:, q, 0:w], ALU.mult, ALU.add).then_inc(score_acc, 1)
            dve.wait_ge(crt_done, 1)
            link(dve.reciprocal(rc[:], rt[:]))
            stt(cT[:], cl[:], vec[:, V_KV:V_KV + 1], rc[:], ALU.mult, ALU.mult).then_inc(c_done, 1)
            dve.wait_ge(score_acc, QB * HEADS)

            def search():
                for q in range(QB):
                    w = META + P * (q + 1)
                    s, diag = sc[:, q, 0:w], sc[:, q, w - P:w]
                    link(stt(diag, causal[:], -TAKEN / -NEG, diag, ALU.mult, ALU.add))
                    for _ in range(TOP_K // 8):
                        link(dve.max(m8[:], s))
                        link(dve.match_replace(s, m8[:], s, TAKEN))
                        yield
                    link(dve.tensor_scalar(s, s, TAKEN, NEG, ALU.not_equal, ALU.mult))
                    link(dve.tensor_tensor(diag, diag, causal[:], ALU.add))
                    yield

            steps_of_search = search()

            def some_search(n):
                for _ in range(n):
                    next(steps_of_search, None)

            for c in range(C_Q + 1, C_U):
                query(c)
                some_search(10)

            def pool_group(g):
                cur = u[:, g, :]
                if g:
                    dve.wait_ge(pooled_done, g)
                for d in range(g + 1):
                    sh, lo = 1 << d, (2 << d) - 1
                    nxt = win[:, d % 2, :]
                    link(dve.tensor_tensor(nxt[:, lo:TM], cur[:, lo:TM], cur[:, lo - sh:TM - sh], ALU.add))
                    cur = nxt
                stt(pooled[:, g, :], cur[:, META:TM], 1.0 / (2 << g), u[:, g, META:TM], ALU.mult, ALU.subtract).then_inc(pooled_done, 1)

            for j in range(2):
                for t in range(2):
                    scaled_full(u[:, 2 * j + t, :], C_U + j, t)
                some_search(5)
                dve.wait_ge(acc_free, 2 * (C_U + j) + 2)
                pool_group(2 * j)
                pool_group(2 * j + 1)
            dve.wait_ge(pooled_done, 4)
            for j in range(2):
                for t in range(2):
                    scaled_full(cc[:, 2 * j + t, :], C_CC + j, t)
                some_search(7)
            for j in range(2):
                for t in range(2):
                    g = 2 * j + t
                    scaled_full(cv[:], C_CU + j, t)
                    dve.wait_ge(acc_free, 2 * (C_CU + j) + t + 1)
                    link(dve.tensor_tensor(cv[:], cv[:], cc[:, g, :], ALU.mult))
                    link(dve.tensor_scalar(cy[:, g, :], cv[:, META - 2:TM - 2], vec[:, V_CW + g:V_CW + g + 1], None, ALU.mult))
                    for r in (1, 2):
                        w = V_CW + 4 * r + g
                        link(stt(cy[:, g, :], cv[:, META - 2 + r:TM - 2 + r], vec[:, w:w + 1], cy[:, g, :], ALU.mult, ALU.add))
                some_search(5)

            def gated_conv(c):
                for t in range(2):
                    g = 2 * (c - C_CB) + t
                    if g:
                        dve.wait_ge(co_split, g)
                    scaled(co[:], c, t)
                    dve.wait_ge(acc_free, 2 * c + t + 1)
                    dve.tensor_tensor(co[:], co[:], cy[:, g, :], ALU.mult).then_inc(co_done, 1)
                    dve.wait_ge(coh_done, g + 1)
                    dve.wait_ge(co_done, g + 1)
                    dve.tensor_tensor(col_[:, g, :], co[:], coh[:, g, :].bitcast(F32), ALU.subtract).then_inc(co_split, 1)

            gated_conv(C_CB)
            for g in range(4):
                dve.wait_ge(ah_done, g + 1)
                stt(al[:, g, :], ps[:, 2 * g + 1, :], vec[:, V_PS + g:V_PS + g + 1], ah[:, g, :].bitcast(F32),
                    ALU.mult, ALU.subtract).then_inc(a_split, 1)
            some_search(5)
            gated_conv(C_CB + 1)
            dve.wait_ge(co_split, 4)
            some_search(1000)

            with dve.Fori(0, 2) as i:
                for q in range(2):
                    c = C_AC + 3 * q
                    for kind in range(2):
                        for t in range(2):
                            scaled(tmp[:, 2 * kind + t, :], c + kind, t, 6, i)
                    for t in range(2):
                        done(c + 2, t, 6, i)
                        b = bank(c + 2, t)
                        dve.wait_ge(sig_done, lin(4 * q + 2 + t + 1, 8, i))
                        dve.tensor_tensor(tmp[:, t, :], tmp[:, t, :], ps[:, b, :], ALU.mult).then_inc(mul_done, 1)
                        dve.tensor_tensor(tmp[:, 2 + t, :], tmp[:, 2 + t, :], ps[:, b + 1, :], ALU.mult).then_inc(acc_free, 1)
                        dve.wait_ge(mul_done, lin(2 * q + t + 1, 4, i))
                        dve.wait_ge(acc_free, lin(2 * (c + 2) + t + 1, 12, i))
                        dve.tensor_tensor(one(msum, lin(2 * q + t, 4, i)), tmp[:, t, :], tmp[:, 2 + t, :], ALU.add).then_inc(m_done, 1)
                    dve.wait_ge(m_done, lin(2 * q + 2, 4, i))

            def normalise(A, n, probs):
                dve.wait_ge(A["exp_done"], n + 1)
                link(dve.reciprocal(rden[:, n:n + 1], den[:, n:n + 1]))
                dve.tensor_scalar(probs, probs, rden[:, n:n + 1], None, ALU.mult).then_inc(A["p_ready"], 1)

            A = att["dsa"]

            def dsa_unit(n):
                w, b = META + P * (n % QB + 1), 2 * (n % 2)
                logits = ps[:, b:b + 2, :].rearrange("p b k -> p (b k)")[:, 0:w]
                dve.wait_ge(A["lg_ready"], n + 1)
                if n >= 2:
                    dve.wait_ge(A["exp_done"], n - 1)
                dve.tensor_tensor_reduce(lm[:, n % 2, 0:w], logits, sc[:, n % QB, 0:w], -1.0, 3.0e38, ALU.add, ALU.min,
                                         nmx[:, n:n + 1]).then_inc(A["mx_done"], 1)

            def dsa_meta(n):
                h, q = divmod(n, QB)
                dve.wait_ge(A["pt_ready"], n + 1)
                if h >= 2:
                    dve.wait_ge(A["pv_ready"], h - 1)
                dve.tensor_copy(pT[h % 2][0:META, QB, P * q:P * q + P], ps[0:META, 5, 0:P]).then_inc(A["pt_copy_d"], 1)

            for n in range(2):
                dsa_unit(n)
                normalise(A, n, pr[:, n % 2, 0:META + P * (n % QB + 1)])
            for n in range(QB * HEADS + QB):
                if n + 2 < QB * HEADS:
                    dsa_unit(n + 2)
                if n < QB * HEADS:
                    dsa_meta(n)
                if n + 2 < QB * HEADS:
                    normalise(A, n + 2, pr[:, n % 2, 0:META + P * ((n + 2) % QB + 1)])
                if n % QB == QB - 1 and n >= QB:
                    h = n // QB - 1
                    dve.wait_ge(A["hi_done"], h + 1)
                    dve.tensor_tensor(atl[:, h, :], ps[:, 6 + h % 2, :], ath[:, h, :].bitcast(F32),
                                      ALU.subtract).then_inc(A["y_split"], 1)

            def merged(lo_part, hi_part, buf, n, m0, per, i):
                nn = lin(n, per, i)
                dve.wait_ge(mh_done, lin(m0 + n + 1, per, i))
                dve.tensor_tensor(one(lo_part, nn), buf, one(hi_part, nn).bitcast(F32), ALU.subtract).then_inc(m_split, 1)

            with dve.Fori(0, 4) as i:
                for t in range(2):
                    scaled(tmpb[:, t, :], C_B, t, 2, i)
                for t in range(2):
                    g = tmpb[:, t, :]
                    done(C_B + 1, t, 2, i)
                    dve.wait_ge(sig_done, lin(16 + t + 1, 2, i))
                    dve.tensor_tensor(g, g, ps[:, bank(C_B + 1, t), :], ALU.mult).then_inc(acc_free, 1)
                    dve.wait_ge(acc_free, lin(2 * (C_B + 1) + t + 1, 4, i))
                    dve.tensor_tensor(g, g, one(msum, lin(t, 2, i)), ALU.add).then_inc(m_done, 1)
                    merged(ml, mh, g, t, 0, 2, i)
                dve.wait_ge(m_split, lin(2, 2, i))
            project(C_O, 1, V_N2)
            ffn(0, 1, 1.0, V_FP)

            ffn(1, 2, 0.5, V_MX)
            root(3)

            def head_scaled(n, c):
                if n >= 4:
                    dve.wait_ge(hq_out, n - 3)
                scaled(qs[:, n % 4, :], c, n % 2)

            def head_normed(n):
                dst, g = (qF, V_QN) if n < 4 else (kF, V_KN)
                dve.wait_ge(hq_rt, n + 1)
                r = rtq[:, n % 4, :]
                link(dve.reciprocal(r, r))
                if n < 4:
                    link(dve.tensor_scalar(r, r, -(HEAD_DIM ** -0.5), None, ALU.mult))
                stt(dst[:, n % 4, :], qs[:, n % 4, :], vec[:, g:g + 1], r, ALU.mult, ALU.mult).then_inc(hq_out, 1)

            for n0, c in ((0, C_FQ), (2, C_FQ + 1), (4, C_FK), (6, C_FK + 1)):
                if n0 == 2:
                    dve.wait_ge(rtok_turned, 1)
                    dve.tensor_copy(rtok[:], ps[:, 1, :].rearrange("p (q t) -> p q t", q=QB)[:, :, 0]).then_inc(rtok_done, 1)
                head_scaled(n0, c)
                head_scaled(n0 + 1, c)
                if n0:
                    head_normed(n0 - 2)
                    head_normed(n0 - 1)
            head_normed(6)
            head_normed(7)

            def tokens_half(v, c, j, t):
                done(c, t)
                for z in range(2):
                    q = 2 * t + z
                    ins = dve.tensor_scalar(v[:, q, CW * j:CW * j + CW], ps[:, bank(c, t), CW * z:CW * z + CW],
                                            rtok[:, q:q + 1], None, ALU.mult)
                ins.then_inc(acc_free, 1)

            def tokens(v, c, j):
                for t in range(2):
                    tokens_half(v, c, j, t)

            dve.wait_ge(tile_done, 2 * C_FL + 2)
            dve.wait_ge(misc_in, 32)
            dve.tensor_tensor(fz[:], ps[0:HEADS, bank(C_FL, 0), :], rsx[0:HEADS], ALU.mult).then_inc(acc_free, 2)
            dve.wait_ge(acc_free, 2 * C_FL + 2)
            dve.tensor_scalar(fz[:], fz[:], fbias[:, 0:1], None, ALU.add).then_inc(fz_done, 1)
            dve.wait_ge(ft_done, 1)
            dve.wait_ge(fz_done, 1)
            link(stt(fz[:], fz[:], 0.0, ft[:], ALU.min, ALU.subtract))
            dve.wait_ge(consts, 14)
            dve.tensor_tensor_scan(fF[0:HEADS, :], fone[:], fz[:], 0.0, ALU.mult, ALU.add).then_inc(f_done, 1)
            dve.wait_ge(f_done, 1)
            dve.wait_ge(f_hi, 1)
            dve.tensor_tensor(fFs[SEL_LO:SEL_LO + HEADS, :], fF[0:HEADS, :], fFs[0:HEADS, :].bitcast(F32), ALU.subtract).then_inc(f_lo, 1)
            dve.wait_ge(rtok_done, 1)
            tokens(vF, C_FV, 0)
            tokens(vF, C_FV + 1, 1)

            F = att["fox"]

            def fox_unit(n):
                w = P * (n % QB + 1)
                dve.wait_ge(F["lg_ready"], n + 1)
                dve.tensor_reduce(nmx[:, n:n + 1], ps[:, 2 * (n % 2) + 1, 0:w], AX.X, ALU.min).then_inc(F["mx_done"], 1)
                normalise(F, n, pu[:, n % UNITS, 0:w])

            def pair_low(A, hi_part, lo_part, n):
                if n % (2 * QB) == QB - 1 and n >= QB:
                    h = n // QB - 1
                    dve.wait_ge(A["hi_done"], h // 2 + 1)
                    dve.tensor_tensor(lo_part[:, h // 2, :], ps[:, 7, :], hi_part[:, h // 2, :].bitcast(F32),
                                      ALU.subtract).then_inc(A["y_split"], 1)

            def fox_step(n):
                if n + 2 < QB * HEADS:
                    fox_unit(n + 2)
                pair_low(F, yfh, yfl, n)

            def sb_projection(c, t):
                if c < C_SK:
                    done(c, t)
                    stt(qS[:, 2 * (c - C_SQ) + t, :], ps[:, bank(c, t), :], HEAD_DIM ** -0.5, rsx,
                        ALU.mult, ALU.mult).then_inc(acc_free, 1)
                elif c < C_SV:
                    scaled(kS[:, 2 * (c - C_SK) + t, :], c, t)
                else:
                    tokens_half(vS, c, c - C_SV, t)

            fox_unit(0)
            fox_unit(1)
            for j in range(6):
                for third in range(6):
                    if third % 3 == 2:
                        sb_projection(C_SQ + j, third // 3)
                    fox_step(6 * j + third)

            B = att["sb"]

            def capped(n):
                w = P * (n % QB + 1)
                dve.wait_ge(B["lg_ready"], n + 1)
                if n >= UNITS:
                    dve.wait_ge(B["pt_ready"], n - UNITS + 1)
                dve.tensor_scalar(pu[:, n % UNITS, 0:w], ps[:, 2 * (n % 2) + 1, 0:w], Z_TOP, None, ALU.min).then_inc(z_capped, 1)

            def sb_unit(n):
                w = P * (n % QB + 1)
                z, R = ps[:, 2 * (n % 2) + 1, 0:w], pu[:, n % UNITS, 0:w]
                dve.wait_ge(sp_done, n + 1)
                link(dve.tensor_tensor(R, z, R, ALU.max))
                link(dve.tensor_tensor_scan(R[:, ::-1], R[:, ::-1], R[:, ::-1], 0.0, ALU.add, ALU.bypass))
                dve.tensor_tensor(R, z, R, ALU.subtract).then_inc(B["lg_read"], 1)

            def sb_step(n):
                if n + 2 < QB * HEADS:
                    capped(n + 2)
                if n + 1 < QB * HEADS:
                    sb_unit(n + 1)
                pair_low(B, ysh, ysl, n)

            dve.wait_ge(F["pt_ready"], QB * HEADS)
            capped(0)
            sb_unit(0)
            capped(1)
            for j in range(8):
                for third in range(6):
                    if third % 3 == 2:
                        scaled(gates[:, 2 * j + third // 3, :], C_GF + j, third // 3)
                    for n in SB_STEPS[6 * j + third]:
                        sb_step(n)

            with dve.Fori(0, 2) as i:
                for q in range(2):
                    c = C_MX + q
                    for t in range(2):
                        n = 2 * q + t
                        g, g2 = one(gates, lin(n, 4, i)), one(gates, lin(DK + n, 4, i))
                        done(c, t, 2, i)
                        b = bank(c, t)
                        dve.wait_ge(sig_done, lin(24 + 4 * q + 2 + t + 1, 8, i))
                        dve.tensor_tensor(g, g, ps[:, b, :], ALU.mult).then_inc(mul_done, 1)
                        dve.tensor_tensor(g2, g2, ps[:, b + 1, :], ALU.mult).then_inc(acc_free, 1)
                        dve.wait_ge(mul_done, lin(DK + n + 1, 4, i))
                        dve.wait_ge(acc_free, lin(2 * c + t + 1, 4, i))
                        dve.tensor_tensor(g, g, g2, ALU.add).then_inc(m_done, 1)
                        merged(m2l, m2h, g, n, DK, 4, i)
            project(C_O2, 4, V_F2)
            ffn(2, 4, 0.5, V_PL)
            root(5)

            for j in range(4):
                for t in range(2):
                    scaled(sg[:, 2 * j + t, :], C_PG + j, t)
                if j == 1:
                    for k in range(2):
                        dve.wait_ge(ph_done, k + 1)
                        dve.tensor_tensor(pTl[:, k, :], ptT[:, k, :], pTh[:, k, :].bitcast(F32), ALU.subtract).then_inc(p_split, 1)
            for n in range(DK):
                dve.wait_ge(tile_done, 2 * C_PP + n + 1)
                dve.wait_ge(sig_done, 40 + n + 1)
                g, x = sg[:, n, :], hT[:, n, META:TM]
                dve.tensor_tensor(g, g, ps[:, 2 * (n % 4) + 1, :], ALU.mult).then_inc(acc_free, 1)
                dve.wait_ge(acc_free, 2 * C_PP + n + 1)
                dve.tensor_tensor(x, x, g, ALU.add).then_inc(o_done, 1)


def kernel(**inputs):
    import numpy as np
    from concourse import bacc
    from concourse.bass_utils import run_bass_kernel_spmd

    nc = bacc.Bacc("TRN2", target_bir_lowering=False, num_devices=1)
    arrays, args = {}, {}
    for name, value in inputs.items():
        a = np.ascontiguousarray(value)
        arrays[f"in_{name}"] = a
        args[name] = nc.dram_tensor(f"in_{name}", a.shape, mybir.dt.from_np(a.dtype), kind="ExternalInput").ap()
    o = nc.dram_tensor("out_0", (1, T, D), F32, kind="ExternalOutput").ap()
    build(nc, args, o)
    r = run_bass_kernel_spmd(nc, [arrays], core_ids=[0])
    return r.results[0]["out_0"]
```

```python
from contextlib import ExitStack

import concourse.bass as bass
from concourse import mybir

F32 = mybir.dt.float32
F32R = mybir.dt.float32r
ACT = mybir.ActivationFunctionType
ALU = mybir.AluOpType
AX = mybir.AxisListType

P = 128
D = 1024
DK = D // P
T = 512
META = 16
TM = T + META
HALF = TM // 2
QB = T // P
CH = 2048
CW = CH // DK
EPS = 1e-6
HEADS = 8
D_LAT = 128
ATTN_SCALE = D_LAT ** -0.5
D_IDX = 32
INDEX_SCALE = HEADS ** -0.5 * D_IDX ** -0.5
TOP_K = T // 4
D_FF = 2816
FK = D_FF // P
HEAD_DIM = 64
DOWN_K = (8, 8, 6)
NEG = -1.0e30
SEL_LO = 32
UNITS = 4
Z_TOP = 60.0
TAKEN = -3.0e38

O_U, O_Q, O_C, O_QI, O_KI, O_CB, O_CC, O_CU, O_G = 0, 512, 1536, 1664, 1920, 1960, 2472, 2984, 3496
KW = D_IDX + HEADS
S_FQ, S_FK, S_FV, S_FL, S_SQ, S_SK, S_SV, S_GF, S_GS = 0, 512, 1024, 1536, 1544, 2056, 2568, 3080, 4104

C_LAT, C_QI, C_Q, C_U, C_CC, C_CU, C_CB, C_AC, C_GB, C_WB, C_O = 0, 1, 2, 6, 8, 10, 12, 14, 26, 30, 34
C_F = (38, 72, 135)
C_D = (60, 94, 157)
C_FQ, C_FK, C_FL, C_FV, C_SQ, C_SK, C_SV, C_GF, C_GS, C_MX, C_O2 = 106, 108, 110, 111, 113, 115, 117, 119, 123, 127, 131
C_PG, C_PP, N_CHUNKS = 169, 173, 174

V_N1, V_N2, V_FIN, V_F1, V_MX, V_F2, V_PL, V_BG, V_PS, V_CW, V_KV, V_QN, V_KN, V_ROWS, V_FP = (
    0, 8, 16, 24, 32, 40, 48, 56, 80, 84, 96, 97, 98, 99, 99)

SB_STEPS, _n = [], 0
for _third in range(48):
    _k = 1 if _third < 18 or _third % 3 != 1 and _third < 42 or _third in (43, 45) else 0
    SB_STEPS.append(range(_n, _n + _k))
    _n += _k

DSA_STEPS = {6 + n * 54 // (QB * HEADS + QB - 1): n for n in range(QB * HEADS + QB)}

SCORES = [(q, h, k0, min(k0 + w, META + P * (q + 1)))
          for q in range(QB) for w in [META + P * (q + 1) if q < QB - 1 else HALF]
          for h in range(HEADS) for k0 in range(0, META + P * (q + 1), w)]


def lin(value, per=0, i=None):
    return value if i is None else i * per + value


def one(t, n):
    return t[:, n, :] if isinstance(n, int) else t[:, bass.ds(n, 1), :].rearrange("p o t -> p (o t)")


def col(t, n):
    return t[:, n:n + 1] if isinstance(n, int) else t[:, bass.ds(n, 1)]


def build(nc, I, out):
    with ExitStack() as ctx:
        def sb(name, shape, dt=F32):
            return ctx.enter_context(nc.sbuf_tensor(name, shape, dt))

        def sem(name):
            return ctx.enter_context(nc.semaphore(name))

        hT = sb("hT", [P, DK, TM])
        xh = sb("xh", [P, DK, TM], F32R)
        xl = sb("xl", [P, DK, TM], F32R)
        raw = sb("raw", [P, 2, CH])
        whi = sb("whi", [P, 2, CH], F32R)
        wlo = sb("wlo", [P, 2, CH], F32R)
        rs = sb("rs", [P, TM])
        rt = sb("rt", [P, TM])
        sq = sb("sq", [P, TM])
        ssum = sb("ssum", [P, TM])
        vec = sb("vec", [P, V_ROWS + DK])
        ident = sb("ident", [P, P])
        identr = sb("identr", [P, P], F32R)
        ones = sb("ones", [P, P])
        onesblk = sb("onesblk", [P, P])
        causal = sb("causal", [P, P])
        causalr = sb("causalr", [P, P], F32R)
        strict = sb("strict", [P, P])
        strictr = sb("strictr", [P, P], F32R)
        eps = sb("eps", [P, 1])
        wi = sb("wi", [P, QB, HEADS])
        nmx = sb("nmx", [P, QB * HEADS])
        den = sb("den", [P, QB * HEADS])
        rden = sb("rden", [P, QB * HEADS])
        m8 = sb("m8", [P, 8])
        rtok = sb("rtok", [P, QB])
        fbias = sb("fbias", [8, 1])
        arena_cols = 24816
        start = (nc.sbuf_base + 31) // 32 * 32
        arena = sb("arena", [P, arena_cols])

        def at(name, off, shape, dt=F32):
            n = 1
            for s in shape[1:]:
                n *= s
            assert off + n <= arena_cols, name
            return nc.alloc_sbuf_tensor_at(name, shape, dt, offset=start + 4 * off)

        fh = at("fh", 0, [P, FK, T], F32R)
        fl = at("fl", FK * T, [P, FK, T], F32R)
        tmp = at("tmp", 2 * FK * T, [P, 4, T])
        sq2, ssum2 = tmp[:, 0, :], tmp[:, 1, :]
        xt = at("xt", 0, [P, QB, D])
        mt = at("mt", 4096, [META, D])
        vt = at("vt", 5120, [V_ROWS, P])
        cT = at("cT", 0, [P, TM])
        ctok = at("ctok", 528, [P, QB + 1, P])
        qT = at("qT", 1168, [P, HEADS, T])
        ath = at("ath", 1168, [P, HEADS, T], F32R)
        sc = at("sc", 5264, [P, QB, TM])
        ah = at("ah", 7376, [P, 4, T], F32R)
        al = at("al", 9424, [P, 4, T], F32R)
        coh = at("coh", 11472, [P, 4, T], F32R)
        col_ = at("col_", 13520, [P, 4, T], F32R)
        cl = at("cl", 15568, [P, TM])
        kw = at("kw", 16096, [KW, TM])
        qst = at("qst", 7376, [3 * D_IDX, HEADS, T], F32R)
        kst = at("kst", 11472, [3 * D_IDX, TM], F32R)
        qih = at("qih", 12000, [P, 2, T], F32R)
        qiT = at("qiT", 17152, [P, 2, T])
        rl = at("rl", 18176, [P, 2, TM])
        rc = at("rc", 19232, [P, TM])
        u = at("u", 19760, [P, 4, TM])
        pooled = at("pooled", 15568, [P, 4, T])
        win = at("win", 17616, [P, 2, TM])
        cc = at("cc", 18672, [P, 4, TM])
        cv = at("cv", 20784, [P, TM])
        cy = at("cy", 21312, [P, 4, T])
        pwt = at("pwt", 23360, [P, 4, P])
        co = at("co", 23872, [P, T])
        msum = at("msum", 15568, [P, DK, T])
        atl = at("atl", 7376, [P, HEADS, T], F32R)
        pT = at("pT", 11472, [P, QB + 1, T])
        lm = at("lm", 14032, [P, 2, TM])
        pr = at("pr", 23760, [P, 2, TM])
        gb = at("gb", 19664, [P, DK, T])
        mh = at("mh", 11472, [P, DK, T], F32R)
        ml = at("ml", 15568, [P, DK, T], F32R)
        qF = at("qF", 0, [P, 4, T])
        kF = at("kF", 2048, [P, 4, T])
        qS = at("qS", 4096, [P, 4, T])
        kS = at("kS", 6144, [P, 4, T])
        yfh = at("yfh", 0, [P, 4, T], F32R)
        yfl = at("yfl", 2048, [P, 4, T], F32R)
        ysh = at("ysh", 4096, [P, 4, T], F32R)
        ysl = at("ysl", 6144, [P, 4, T], F32R)
        vF = at("vF", 8192, [P, QB, T])
        sel = at("sel", 10240, [P, HEADS, P])
        selr = at("selr", 11264, [P, HEADS, P], F32R)
        fz = at("fz", 12288, [8, T])
        ft = at("ft", 12800, [8, T])
        fF = at("fF", 13312, [P, T])
        fFs = at("fFs", 13824, [P, T], F32R)
        fone = at("fone", 14336, [8, T])
        qs = at("qs", 14848, [P, 4, T])
        rtq = at("rtq", 22528, [P, 4, T])
        vS = at("vS", 16384, [P, QB, T])
        pu = at("pu", 22528, [P, UNITS, T])
        fpT = [at("fpT0", 18432, [P, QB, T]), at("fpT1", 20480, [P, QB, T])]
        gates = at("gates", 8192, [P, 2 * DK, T])
        m2h = at("m2h", 16384, [P, DK, T], F32R)
        m2l = at("m2l", 20480, [P, DK, T], F32R)
        sg = at("sg", 0, [P, DK, T])
        pTh = at("pTh", 4096, [P, 2, T], F32R)
        pTl = at("pTl", 5120, [P, 2, T], F32R)
        pt = at("pt", 6144, [P, QB, 256])
        ptT = at("ptT", 7168, [P, 2, T])
        ot = at("ot", 8192, [P, QB, D])

        ps = ctx.enter_context(nc.psum_tensor("ps", [P, 8, 512], F32))

        raw_in = [sem("raw_in0"), sem("raw_in1")]
        raw_taken = sem("raw_taken")
        w_hi = sem("w_hi")
        w_lo = sem("w_lo")
        tile_done = sem("tile_done")
        acc_free = sem("acc_free")
        consts, ones_done = sem("consts"), sem("ones_done")
        x_in, vec_in, misc_in = sem("x_in"), sem("vec_in"), sem("misc_in")
        x_turned, x_copied, vec_turned, vec_done = sem("x_turned"), sem("x_copied"), sem("vec_turned"), sem("vec_done")
        sq_done, ssum_done, xh_done, x_split = sem("sq_done"), sem("ssum_done"), sem("xh_done"), sem("x_split")
        ss_done, rt_done, rs_done = sem("ss_done"), sem("rt_done"), sem("rs_done")
        dve_seq = sem("dve_seq")
        act_seq = sem("act_seq")
        ks_hi, ks_lo, qi_hi, qst_hi, qst_lo, wi_turned, wi_done = (
            sem("ks_hi"), sem("ks_lo"), sem("qi_hi"), sem("qst_hi"), sem("qst_lo"), sem("wi_turned"), sem("wi_done"))
        s_ready, relu_done, score_acc = sem("s_ready"), sem("relu_done"), sem("score_acc")
        csq_done, css_done, crt_done, c_done, c_turned, ctok_done = (
            sem("csq_done"), sem("css_done"), sem("crt_done"), sem("c_done"), sem("c_turned"), sem("ctok_done"))
        pooled_done, mix_done, ah_done, a_split = sem("pooled_done"), sem("mix_done"), sem("ah_done"), sem("a_split")
        co_done, coh_done, co_split = sem("co_done"), sem("coh_done"), sem("co_split")
        sig_done, mul_done, m_done, mh_done, m_split = (
            sem("sig_done"), sem("mul_done"), sem("m_done"), sem("mh_done"), sem("m_split"))
        silu_done, h_done, h_hi, h_split = sem("silu_done"), sem("h_done"), sem("h_hi"), sem("h_split")
        xn_done, gain_done = sem("xn_done"), sem("gain_done")
        sq2_done, ssum2_done, ms2_done, rt2_done = sem("sq2_done"), sem("ssum2_done"), sem("ms2_done"), sem("rt2_done")
        att = {k: {n: sem(f"{k}_{n}") for n in (
            "lg_ready", "mx_done", "lg_read", "exp_done", "p_ready", "pt_ready", "pt_copy_a", "pt_copy_d", "pv_ready", "hi_done",
            "y_split")} for k in ("dsa", "fox", "sb")}
        hq_done, hq_ss, hq_rt, hq_out = sem("hq_done"), sem("hq_ss"), sem("hq_rt"), sem("hq_out")
        rtok_turned, rtok_done = sem("rtok_turned"), sem("rtok_done")
        fz_done, ft_done, f_done, f_hi, f_lo, sel_done = (
            sem("fz_done"), sem("ft_done"), sem("f_done"), sem("f_hi"), sem("f_lo"), sem("sel_done"))
        z_capped, sp_done = sem("z_capped"), sem("sp_done")
        p_in, p_turned, p_copied, ph_done, p_split = (
            sem("p_in"), sem("p_turned"), sem("p_copied"), sem("ph_done"), sem("p_split"))
        o_done, o_turned, o_copied, o_out = sem("o_done"), sem("o_turned"), sem("o_copied"), sem("o_out")

        def bank(c, t):
            return 2 * t if isinstance(c, int) and C_GB <= c < C_WB else 4 * (c % 2) + 2 * t

        def n_cols(c):
            if c == C_LAT:
                return DK * (P + KW)
            if c == C_FL:
                return DK * HEADS
            for d in C_D:
                if d <= c < d + 12 and (c - d) % 3 == 2:
                    return DOWN_K[2] * CW
            return CH

        def raw_level(c, per, i):
            return lin(32 * (c // 2 + 1), 16 * per, i)

        def score_bank(n):
            return 2 * (n % 4) + 1

        kin = "(k p) n -> p k n"
        w1 = I["w_in"][0].rearrange(kin, p=P)
        w2 = I["w_in_2"][0].rearrange(kin, p=P)

        block = ctx.enter_context(nc.Block())

        @block.sync
        def _(sp):
            def slot(c, k, w):
                return raw[:, c % 2, 0:k * w].rearrange("p (k n) -> p k n", k=k)

            def load(c, parts, per=0, i=None):
                if c >= 2:
                    sp.wait_ge(w_lo, lin(c - 1, per, i))
                    sp.sem_inc(raw_taken, 1)
                for dst, src in parts:
                    sp.dma_start(dst, src).then_inc(raw_in[c % 2], 16)

            def square(c, w, at_col, per=0, i=None):
                s = slot(c, DK, CW)
                sel = slice(at_col, at_col + CW) if isinstance(at_col, int) else bass.ds(sp.snap(at_col), CW)
                load(c, [(s[:, 0:4], w[:, 0:4, sel]), (s[:, 4:8], w[:, 4:8, sel])], per, i)

            def two(c, wa, wb, at_col, per, i):
                s = slot(c, DK, CW)
                sel = bass.ds(sp.snap(at_col), CW)
                load(c, [(s[:, 0:4], wa[:, :, sel]), (s[:, 4:8], wb[:, :, sel])], per, i)

            def ffn(f, gate, up, down):
                with sp.Fori(0, FK // 2) as i:
                    for j in range(2):
                        c = C_F[f] + j
                        s = slot(c, DK, CW)
                        sel = bass.ds(sp.snap(i * CW + P * j), P)
                        load(c, [(s[:, :, 0:P], gate[:, :, sel]), (s[:, :, P:CW], up[:, :, sel])], 2, i)
                with sp.Fori(0, 2) as i:
                    for j in range(2):
                        sel = bass.ds(sp.snap(i * (2 * CW) + j * CW), CW)
                        for r, kn in enumerate(DOWN_K):
                            c = C_D[f] + 3 * j + r
                            s = slot(c, kn, CW)
                            k0, hk = sum(DOWN_K[:r]), kn // 2
                            load(c, [(s[:, 0:hk], down[:, k0:k0 + hk, sel]),
                                     (s[:, hk:kn], down[:, k0 + hk:k0 + kn, sel])], 6, i)

            sp.dma_start(xt[:], I["x"][0].rearrange("(b p) d -> p b d", p=P)).then_inc(x_in, 16)
            s = slot(C_LAT, DK, P + KW)
            load(C_LAT, [(s[:, :, 0:P], w1[:, :, O_C:O_C + P]), (s[:, :, P:P + KW], w1[:, :, O_KI:O_KI + KW])])
            sp.wait_ge(x_in, 32)
            square(C_QI, w1, O_QI)
            for c0, o, n in ((C_Q, O_Q, 4), (C_U, O_U, 2), (C_CC, O_CC, 2), (C_CU, O_CU, 2), (C_CB, O_CB, 2)):
                for j in range(n):
                    square(c0 + j, w1, o + CW * j)
            wa = I["w_a"][0].rearrange(kin, p=P)
            wc = I["w_c"][0].rearrange(kin, p=P)
            with sp.Fori(0, 2) as i:
                for q in range(2):
                    c = C_AC + 3 * q
                    square(c, w1, i * (2 * CW) + (O_G + CW * q), 6, i)
                    square(c + 1, w1, i * (2 * CW) + (O_G + 2 * D + CW * q), 6, i)
                    two(c + 2, wa, wc, i * (2 * CW) + CW * q, 6, i)
            wb = I["w_b"][0].rearrange(kin, p=P)
            for j in range(4):
                square(C_GB + j, w1, O_G + D + CW * j)
            with sp.Fori(0, 2) as i:
                for q in range(2):
                    square(C_WB + q, wb, i * (2 * CW) + CW * q, 2, i)
            wo = I["w_o"][0].rearrange(kin, p=P)
            with sp.Fori(0, 2) as i:
                for j in range(2):
                    square(C_O + j, wo, i * (2 * CW) + CW * j, 2, i)
            gu = I["w_gate_up"][0].rearrange(kin, p=P)
            ffn(0, gu[:, :, 0:D_FF], gu[:, :, D_FF:2 * D_FF], I["w_down"][0].rearrange(kin, p=P))
            ffn(1, I["ffn1_w_gate_2"][0].rearrange(kin, p=P), I["ffn1_w_up_2"][0].rearrange(kin, p=P),
                I["ffn1_w_down_2"][0].rearrange(kin, p=P))
            for c0, o in ((C_FQ, S_FQ), (C_FK, S_FK)):
                for j in range(2):
                    square(c0 + j, w2, o + CW * j)
            s = slot(C_FL, DK, HEADS)
            load(C_FL, [(s[:, 0:4], w2[:, 0:4, S_FL:S_FL + HEADS]), (s[:, 4:8], w2[:, 4:8, S_FL:S_FL + HEADS])])
            for c0, o, n in ((C_FV, S_FV, 2), (C_SQ, S_SQ, 2), (C_SK, S_SK, 2), (C_SV, S_SV, 2), (C_GF, S_GF, 4), (C_GS, S_GS, 4)):
                for j in range(n):
                    square(c0 + j, w2, o + CW * j)
            wf = I["w_branch_fox_2"][0].rearrange(kin, p=P)
            ws = I["w_branch_sb_2"][0].rearrange(kin, p=P)
            with sp.Fori(0, 2) as i:
                for q in range(2):
                    two(C_MX + q, wf, ws, i * (2 * CW) + CW * q, 2, i)
            wo2 = I["w_out_2"][0].rearrange(kin, p=P)
            with sp.Fori(0, 2) as i:
                for j in range(2):
                    square(C_O2 + j, wo2, i * (2 * CW) + CW * j, 2, i)
            ffn(2, I["ffn2_w_gate_2"][0].rearrange(kin, p=P), I["ffn2_w_up_2"][0].rearrange(kin, p=P),
                I["ffn2_w_down_2"][0].rearrange(kin, p=P))
            wg = I["w_ple_gate_2"][0].rearrange(kin, p=P)
            for j in range(4):
                square(C_PG + j, wg, CW * j)
                if j == 1:
                    sp.wait_ge(tile_done, 2 * C_PG)
                    sp.dma_start(pt[:], I["p_2"][0, 0].rearrange("(b p) d -> p b d", p=P)).then_inc(p_in, 16)
            wp = I["w_ple_proj_2"][0].rearrange(kin, p=P)
            s = slot(C_PP, 2, D)
            load(C_PP, [(s[:, 0:1], wp[:, 0:1]), (s[:, 1:2], wp[:, 1:2])])
            for n in range(DK):
                sp.wait_ge(o_copied, n + 1)
                sp.dma_start(out[0].rearrange("(b p) d -> p b d", p=P)[:, :, P * n:P * n + P],
                             ot[:, :, P * n:P * n + P]).then_inc(o_out, 16)
            sp.wait_ge(o_out, 16 * DK)

        @block.gpsimd
        def _(pool):
            pool.memset(ident[:], 0.0).then_inc(consts, 1)
            pool.memset(causal[:], 0.0).then_inc(consts, 1)
            pool.memset(strict[:], 0.0).then_inc(consts, 1)
            pool.memset(onesblk[:], 0.0).then_inc(consts, 1)
            pool.wait_ge(consts, 4)
            tri = dict(pattern=[[-1, P]], channel_multiplier=1)
            pool.affine_select(out=ident[:], in_=ident[:], compare_op=ALU.not_equal, fill=1.0, base=0, **tri).then_inc(consts, 1)
            pool.affine_select(out=causal[:], in_=causal[:], compare_op=ALU.is_ge, fill=NEG, base=0, **tri).then_inc(consts, 1)
            pool.affine_select(out=strict[:], in_=strict[:], compare_op=ALU.is_ge, fill=NEG, base=-1, **tri).then_inc(consts, 1)
            for z, o in enumerate((0, HEAD_DIM)):
                pool.wait_ge(consts, 7 + z)
                pool.memset(onesblk[o:o + HEAD_DIM, o:o + HEAD_DIM], 1.0).then_inc(consts, 1)

            def low(c, per=0, i=None):
                n = n_cols(c)
                pool.wait_ge(w_hi, lin(c + 1, per, i))
                pool.tensor_tensor(wlo[:, c % 2, 0:n], raw[:, c % 2, 0:n], whi[:, c % 2, 0:n].bitcast(F32),
                                   ALU.subtract).then_inc(w_lo, 1)

            def run(c0, c1, body):
                with pool.Fori(0, (c1 - c0) // body) as i:
                    for j in range(body):
                        low(c0 + j, body, i)

            pool.wait_ge(consts, 9)
            low(C_LAT)
            low(C_QI)
            run(C_Q, C_D[0], 2)
            run(C_D[0], C_F[1], 6)
            run(C_F[1], C_D[1], 2)
            run(C_D[1], C_FQ, 6)
            run(C_FQ, C_FL, 2)
            pool.wait_ge(tile_done, 2 * C_FQ)
            pool.memset(sel[:], 0.0).then_inc(consts, 1)
            pool.memset(fF[:], 0.0).then_inc(consts, 1)
            pool.memset(fone[:], 1.0).then_inc(consts, 1)
            for z, first in enumerate((0, SEL_LO)):
                pool.wait_ge(consts, 12 + z)
                pool.affine_select(out=sel[:], in_=sel[:], compare_op=ALU.not_equal, fill=1.0, base=-first,
                                   pattern=[[-1, HEADS], [0, P]], channel_multiplier=1).then_inc(consts, 1)
            low(C_FL)
            run(C_FV, C_D[2], 2)
            run(C_D[2], C_PG, 6)
            run(C_PG, C_PP, 2)
            low(C_PP)

        @block.tensor
        def _(pe):
            def passes(o, s, w_of, xhi, xlo, first, last):
                pe.matmul(o, w_of(whi), xhi, start=first, stop=False)
                pe.matmul(o, w_of(whi), xlo, start=False, stop=False)
                return pe.matmul(o, w_of(wlo), xhi, start=False, stop=last)

            def x_ready(X, k, t):
                if t == 0:
                    pe.wait_ge(x_split, DK * X + k + 1)

            def chunk(c, hi, lo, per=0, i=None, X=None, full=(False, False), widths=(P, P), between=None, steps=None, ready=None):
                s, w = c % 2, sum(widths)
                pe.wait_ge(w_lo, lin(c + 1, per, i))
                for t in range(2):
                    if C_GB < c < C_WB:
                        pe.wait_ge(acc_free, 2 * (c - 1) + t + 1)
                    elif c >= 2:
                        pe.wait_ge(acc_free, lin(2 * (c - 2) + t + 1, 2 * per, i))
                    b, m, o0 = bank(c, t), widths[t], sum(widths[:t])
                    for k in range(DK):
                        if X is not None:
                            x_ready(X, k, t)
                        if ready is not None and t == 0:
                            pe.wait_ge(m_split, ready + k + 1)
                        w_of = lambda wt: wt[:, s, w * k + o0:w * k + o0 + m]
                        if full[t]:
                            for z in range(2):
                                cs = slice(HALF * z, HALF * z + HALF)
                                mm = passes(ps[0:m, b + z, 0:HALF], s, w_of, hi[:, k, cs], lo[:, k, cs], k == 0, k == DK - 1)
                        else:
                            cs = slice(0, T) if hi.shape[2] == T else slice(META, TM)
                            mm = passes(ps[0:m, b, :], s, w_of, hi[:, k, cs], lo[:, k, cs], k == 0, k == DK - 1)
                        if k == DK - 1:
                            mm.then_inc(tile_done, 1)
                        if steps:
                            steps(t, k)
                    if t == 0 and between:
                        between()

            THIRDS = (2, 5, DK - 1)

            def norm_sums(S, c):
                pe.wait_ge(ssum_done, 9 * (S + 1))
                if S == 0:
                    for z in range(2):
                        mm = pe.matmul(ps[:, 5 + 2 * z, 0:HALF], ones[:], ssum[:, HALF * z:HALF * z + HALF], start=True, stop=True)
                else:
                    mm = pe.matmul(ps[:, bank(c + 1, 0) + 1, :], ones[:], ssum[:, META:TM], start=True, stop=True)
                if S == 2:
                    pe.wait_ge(ssum2_done, 9)
                    mm = pe.matmul(ps[:, bank(c + 1, 1) + 1, :], ones[:], ssum2, start=True, stop=True)
                mm.then_inc(ss_done, 1)

            def pair(c, hi_a, lo_a, hi_b, lo_b, per, i):
                s = c % 2
                pe.wait_ge(w_lo, lin(c + 1, per, i))
                for t in range(2):
                    pe.wait_ge(acc_free, lin(2 * (c - 2) + t + 1, 2 * per, i))
                    for z, (h, l) in enumerate(((hi_a, lo_a), (hi_b, lo_b))):
                        for k in range(4):
                            o = CW * (4 * z + k) + P * t
                            mm = passes(ps[:, bank(c, t) + z, :], s, lambda wt: wt[:, s, o:o + P],
                                        h[:, k, :], l[:, k, :], k == 0, k == 3)
                    mm.then_inc(tile_done, 1)

            def ffn(f, S, X):
                c = C_F[f]
                chunk(c, xh, xl, X=X, between=lambda: norm_sums(S, c))
                chunk(c + 1, xh, xl)
                with pe.Fori(0, FK // 2 - 1) as i:
                    for j in range(2):
                        chunk(c + 2 + j, xh, xl, 2, i)
                c = C_D[f]
                with pe.Fori(0, 2) as i:
                    for j in range(2):
                        for r, kn in enumerate(DOWN_K):
                            cr, k0 = c + 3 * j + r, sum(DOWN_K[:r])
                            pe.wait_ge(w_lo, lin(cr + 1, 6, i))
                            if j == 0:
                                pe.wait_ge(h_split, FK * f + k0 + kn)
                            for t in range(2):
                                if r == 0:
                                    pe.wait_ge(acc_free, lin(2 * (c - 2 + j) + t + 1, 4 * j + 2 * t + 6, i))
                                for k in range(kn):
                                    o = CW * k + P * t
                                    mm = passes(ps[:, bank(c + j, t), :], cr % 2, lambda wt: wt[:, cr % 2, o:o + P],
                                                fh[:, k0 + k, :], fl[:, k0 + k, :], r == 0 and k == 0, r == 2 and k == kn - 1)
                                mm.then_inc(tile_done, 1)

            pe.wait_ge(consts, 9)
            pe.wait_ge(vec_in, 16 * 15)
            pe.transpose(ps[:, 7, 0:V_ROWS], vt[:], ident[0:V_ROWS, 0:V_ROWS]).then_inc(vec_turned, 1)
            pe.wait_ge(x_in, 32)
            for n in range(DK):
                b = 2 * (n % 4)
                if n >= 4:
                    pe.wait_ge(x_copied, 2 * (n - 3))
                for q in range(QB):
                    pe.transpose(ps[:, b, P * q:P * q + P], xt[:, q, P * n:P * n + P], ident[:])
                if n == 3:
                    pe.wait_ge(vec_done, 1)
                pe.transpose(ps[:, b + 1, 0:META], mt[:, P * n:P * n + P], ident[0:META, 0:META]).then_inc(x_turned, 1)

            pe.wait_ge(x_copied, 12)
            chunk(C_LAT, xh, xl, X=0, full=(True, True), widths=(P, KW))
            chunk(C_QI, xh, xl, steps=lambda t, k: norm_sums(0, C_QI) if (t, k) == (0, 3) else None)

            def latent_sums():
                pe.wait_ge(csq_done, 1)
                for z in range(2):
                    mm = pe.matmul(ps[:, 5 + 2 * z, 0:HALF], ones[:], sq[:, HALF * z:HALF * z + HALF], start=True, stop=True)
                mm.then_inc(css_done, 1)
                for q in range(QB):
                    mm = pe.transpose(ps[:, 1, HEADS * q:HEADS * q + HEADS], kw[D_IDX:KW, META + P * q:META + P * q + P],
                                      ident[D_IDX:KW, D_IDX:KW])
                mm.then_inc(wi_turned, 1)

            chunk(C_Q, xh, xl, between=latent_sums)

            def score(n):
                q, h, k0, k1 = SCORES[n]
                if n >= 4:
                    pe.wait_ge(relu_done, n - 3)
                pe.matmul(ps[:, score_bank(n), 0:k1 - k0], qst[:, h, P * q:P * q + P], kst[:, k0:k1],
                          start=True, stop=True).then_inc(s_ready, 1)

            for j in range(3):
                def run(t, k):
                    n = DK * (2 * j + t - 1) + k
                    if n == 0:
                        pe.wait_ge(qst_hi, 8)
                        pe.wait_ge(qst_lo, 4)
                        pe.wait_ge(ks_hi, 2)
                        pe.wait_ge(ks_lo, 1)
                        pe.wait_ge(wi_done, 1)
                        pe.wait_ge(crt_done, 1)
                    if 0 <= n < len(SCORES):
                        score(n)
                chunk(C_Q + 1 + j, xh, xl, steps=run)

            def turn_latents():
                pe.wait_ge(relu_done, len(SCORES))
                pe.wait_ge(c_done, 1)
                for q in range(QB):
                    pe.transpose(ps[:, 5, P * q:P * q + P], cT[:, META + P * q:META + P * q + P], ident[:])
                pe.transpose(ps[0:META, 7, 0:P], cT[:, 0:META], ident[:]).then_inc(c_turned, 1)

            pe.wait_ge(relu_done, len(SCORES) - 2)
            chunk(C_U, xh, xl, full=(True, True), between=turn_latents)
            pe.wait_ge(ctok_done, 2)
            for c in range(C_U + 1, C_CB):
                chunk(c, xh, xl, full=(True, True))
            chunk(C_CB, xh, xl)
            pe.wait_ge(misc_in, 32)
            pe.wait_ge(acc_free, 2 * C_CB)
            for g in range(4):
                pe.wait_ge(pooled_done, g + 1)
                pe.matmul(ps[:, 2 * g + 1, :], pwt[:, g, :], pooled[:, g, :], start=True, stop=True).then_inc(mix_done, 1)
            chunk(C_CB + 1, xh, xl)

            with pe.Fori(0, 2) as i:
                for q in range(2):
                    c = C_AC + 3 * q
                    chunk(c, xh, xl, 6, i)
                    chunk(c + 1, xh, xl, 6, i)
                    if q == 0:
                        pe.wait_ge(a_split, 4)
                        pe.wait_ge(co_split, 4)
                    pair(c + 2, ah, al, coh, col_, 6, i)

            def attention(A, read, scores, key_tiles, value_piece, bank_left, extra=0):
                def qk(n):
                    if n >= 2:
                        pe.wait_ge(A[read], n - 1)
                    scores(n).then_inc(A["lg_ready"], 1)

                def step(n):
                    if n + 2 < QB * HEADS:
                        qk(n + 2)
                    h, q = divmod(n, QB)
                    if 1 <= n <= QB * HEADS:
                        pe.wait_ge(A["pt_copy_a"], n)
                        if extra:
                            pe.wait_ge(A["pt_copy_d"], n)
                    if h >= 1:
                        if q == 0:
                            bank_left(h - 1)
                        value_piece(h - 1, q).then_inc(A["pv_ready"], 1)
                    if n < QB * HEADS:
                        pe.wait_ge(A["p_ready"], n + 1)
                        key_tiles(n, q).then_inc(A["pt_ready"], 1)
                return qk, step

            A = att["dsa"]

            def dsa_scores(n):
                h, q = divmod(n, QB)
                w = META + P * (q + 1)
                b = 1 + 2 * (n % 2)
                mm = pe.matmul(ps[:, b, 0:min(w, 512)], qT[:, h, P * q:P * q + P], cT[:, 0:min(w, 512)], start=True, stop=True)
                if w > 512:
                    mm = pe.matmul(ps[:, b + 1, 0:w - 512], qT[:, h, P * q:P * q + P], cT[:, 512:w], start=True, stop=True)
                return mm

            def dsa_turn(n, q):
                src = pr[:, n % 2]
                for j in range(q + 1):
                    pe.transpose(ps[:, 5, P * j:P * j + P], src[:, META + P * j:META + P * j + P], ident[:])
                return pe.transpose(ps[0:META, 6, 0:P], src[:, 0:META], ident[:])

            def dsa_piece(h, q):
                o = ps[:, 7, :]
                if q == 0:
                    pe.matmul(o, ctok[0:META, QB, :], pT[0:META, QB, :], start=True, stop=False)
                return pe.matmul(o[:, P * q:T], ctok[:, q, :], pT[:, q, P * q:T], start=False, stop=q == QB - 1)

            def dsa_split(h):
                if h >= 1:
                    pe.wait_ge(A["y_split"], h)

            qk, step = attention(A, "mx_done", dsa_scores, dsa_turn, dsa_piece, dsa_split, extra=1)
            pe.wait_ge(acc_free, 2 * (C_GB - 1))
            qk(0)
            qk(1)
            for j in range(4):
                def run(t, k):
                    n = DSA_STEPS.get(2 * DK * j + DK * t + k)
                    if n == 0:
                        pe.wait_ge(acc_free, 2 * C_GB)
                    if n is not None:
                        step(n)
                chunk(C_GB + j, xh, xl, steps=run)

            pe.wait_ge(att["dsa"]["y_split"], HEADS)
            pe.wait_ge(acc_free, 2 * C_WB)
            with pe.Fori(0, 2) as i:
                for j in range(2):
                    chunk(C_WB + j, ath, atl, 2, i)
            with pe.Fori(0, 2) as i:
                for j in range(2):
                    chunk(C_O + j, mh, ml, 2, i, ready=0)
            ffn(0, 1, 1)

            ffn(1, 2, 2)
            chunk(C_FQ, xh, xl, X=3, between=lambda: norm_sums(3, C_FQ))

            def head_sums(n):
                pe.wait_ge(hq_done, n + 1)
                if n >= 2:
                    pe.wait_ge(hq_rt, n - 1)
                pe.matmul(ps[:, 5 + 2 * (n % 2), :], onesblk[:], rtq[:, n % 4, :], start=True, stop=True).then_inc(hq_ss, 1)

            chunk(C_FQ + 1, xh, xl)
            pe.wait_ge(rs_done, 4)
            for q in range(QB):
                mm = pe.transpose(ps[:, 1, P * q:P * q + P], rs[:, META + P * q:META + P * q + P], ident[:])
            mm.then_inc(rtok_turned, 1)
            head_sums(0)
            head_sums(1)
            for n, c in ((2, C_FK), (4, C_FK + 1)):
                chunk(c, xh, xl)
                head_sums(n)
                head_sums(n + 1)

            def tokens(c, steps=None):
                s = c % 2
                pe.wait_ge(w_lo, c + 1)
                for t in range(2):
                    pe.wait_ge(acc_free, 2 * (c - 2) + t + 1)
                    for z in range(2):
                        q = 2 * t + z
                        o = ps[:, bank(c, t), CW * z:CW * z + CW]
                        for k in range(DK):
                            th, tl = (x[:, k, META + P * q:META + P * q + P] for x in (xh, xl))
                            ch, clo = (wt[:, s, CW * k:CW * k + CW] for wt in (whi, wlo))
                            pe.matmul(o, th, ch, start=k == 0, stop=False)
                            pe.matmul(o, th, clo, start=False, stop=False)
                            mm = pe.matmul(o, tl, ch, start=False, stop=k == DK - 1)
                            if z and k == DK - 1:
                                mm.then_inc(tile_done, 1)
                            if steps and (z, k) in ((0, 4), (1, 2), (1, DK - 1)):
                                steps(t, THIRDS[((0, 4), (1, 2), (1, DK - 1)).index((z, k))])

            pe.wait_ge(w_lo, C_FL + 1)
            pe.wait_ge(acc_free, 2 * (C_FL - 2) + 1)
            for k in range(DK):
                mm = passes(ps[0:HEADS, bank(C_FL, 0), :], 0, lambda wt: wt[:, C_FL % 2, HEADS * k:HEADS * k + HEADS],
                            xh[:, k, META:TM], xl[:, k, META:TM], k == 0, k == DK - 1)
            mm.then_inc(tile_done, 2)
            tokens(C_FV)
            head_sums(6)
            head_sums(7)
            tokens(C_FV + 1)

            F = att["fox"]

            def row(h):
                return HEAD_DIM * (h % 2)

            def fox_scores(n):
                h, q = divmod(n, QB)
                w, r = P * (q + 1), row(h)
                b = 2 * (n % 2) + 1
                if n % (2 * QB) == 0:
                    pe.wait_ge(hq_out, 5 + h // 2)
                pe.matmul(ps[:, b, 0:w], qF[r:r + HEAD_DIM, h // 2, P * q:P * q + P], kF[r:r + HEAD_DIM, h // 2, 0:w],
                          start=True, stop=False, skip_group_check=True)
                pe.matmul(ps[:, b, 0:w], selr[:, h, :], fFs[:, 0:w], start=False, stop=False, skip_group_check=True)
                return pe.matmul(ps[:, b, P * q:w], identr[:], causalr[:], start=False, stop=True, skip_group_check=True)

            def turn(n, q):
                for j in range(q + 1):
                    mm = pe.transpose(ps[:, 5, P * j:P * j + P], pu[:, n % UNITS, P * j:P * j + P], ident[:])
                return mm

            def value_piece(v):
                def piece(h, j):
                    o, r = ps[row(h):row(h) + HEAD_DIM, 7, :], row(h)
                    return pe.matmul(o[:, P * j:T], v[:, j, HEAD_DIM * h:HEAD_DIM * h + HEAD_DIM],
                                     fpT[h % 2][:, j, P * j:T], start=j == 0, stop=j == QB - 1)
                return piece

            def pair_split(A):
                def wait(h):
                    if h % 2 == 0 and h:
                        pe.wait_ge(A["y_split"], h // 2)
                return wait

            qk, step = attention(F, "exp_done", fox_scores, turn, value_piece(vF), pair_split(F))
            pe.wait_ge(hq_rt, 8)
            pe.wait_ge(f_lo, 1)
            pe.wait_ge(sel_done, 1)
            pe.wait_ge(rtok_done, 1)
            qk(0)
            qk(1)
            for j in range(6):
                c = C_SQ + j

                def run(t, k):
                    if k in THIRDS:
                        step(6 * j + 3 * t + THIRDS.index(k))

                if c < C_SV:
                    chunk(c, xh, xl, steps=run)
                else:
                    tokens(c, steps=run)

            B = att["sb"]

            def sb_scores(n):
                h, q = divmod(n, QB)
                w, r = P * (q + 1), row(h)
                b = 2 * (n % 2) + 1
                pe.matmul(ps[:, b, 0:w], qS[r:r + HEAD_DIM, h // 2, P * q:P * q + P],
                          kS[r:r + HEAD_DIM, h // 2, 0:w], start=True, stop=False, skip_group_check=True)
                return pe.matmul(ps[:, b, P * q:w], identr[:], strictr[:], start=False, stop=True, skip_group_check=True)

            qk, step = attention(B, "lg_read", sb_scores, turn, value_piece(vS), pair_split(B))
            pe.wait_ge(acc_free, 2 * C_SV)
            pe.wait_ge(F["exp_done"], QB * HEADS)
            qk(0)
            qk(1)
            pe.wait_ge(acc_free, 2 * C_GF)
            pe.wait_ge(F["y_split"], 4)
            for j in range(8):
                def run(t, k):
                    if k in THIRDS:
                        for n in SB_STEPS[6 * j + 3 * t + THIRDS.index(k)]:
                            step(n)
                chunk(C_GF + j, xh, xl, steps=run)

            pe.wait_ge(B["y_split"], 4)
            with pe.Fori(0, 2) as i:
                for q in range(2):
                    pair(C_MX + q, yfh, yfl, ysh, ysl, 2, i)
            with pe.Fori(0, 2) as i:
                for j in range(2):
                    chunk(C_O2 + j, m2h, m2l, 2, i, ready=DK)
            ffn(2, 4, 4)

            chunk(C_PG, xh, xl, X=5, between=lambda: norm_sums(5, C_PG))
            chunk(C_PG + 1, xh, xl)
            pe.wait_ge(p_in, 16)
            pe.wait_ge(rs_done, 6)
            for j in range(2):
                for q in range(QB):
                    mm = pe.transpose(ps[:, 1 + 2 * j, P * q:P * q + P], pt[:, q, P * j:P * j + P], ident[:])
                mm.then_inc(p_turned, 1)
            chunk(C_PG + 2, xh, xl)
            chunk(C_PG + 3, xh, xl)
            pe.wait_ge(p_split, 2)
            pe.wait_ge(w_lo, C_PP + 1)
            pe.wait_ge(acc_free, 2 * C_PP)

            def turn_back(n):
                pe.wait_ge(o_done, n + 1)
                if n >= 4:
                    pe.wait_ge(o_copied, n - 3)
                for q in range(QB):
                    mm = pe.transpose(ps[:, 2 * (n % 4), P * q:P * q + P], hT[:, n, META + P * q:META + P * q + P], ident[:])
                mm.then_inc(o_turned, 1)

            for n in range(DK):
                if n >= 4:
                    pe.wait_ge(acc_free, 2 * C_PP + n - 3)
                for k in range(2):
                    o = D * k + P * n
                    mm = passes(ps[:, 2 * (n % 4) + 1, :], 0, lambda wt: wt[:, C_PP % 2, o:o + P],
                                pTh[:, k, :], pTl[:, k, :], k == 0, k == 1)
                mm.then_inc(tile_done, 1)
                if n >= 2:
                    turn_back(n - 2)
            turn_back(DK - 2)
            turn_back(DK - 1)

        @block.scalar
        def _(act):
            for r0, a in ((V_N1, "norm1_g"), (V_N2, "norm2_g"), (V_FIN, "final_g"), (V_F1, "ffn1_norm_2"), (V_MX, "mix_norm_2"),
                          (V_F2, "ffn2_norm_2"), (V_PL, "ple_norm_2"), (V_BG, "b_gate"), (V_PS, "pool_scale"), (V_KV, "kv_norm_g")):
                a = I[a] if len(I[a].shape) == 1 else I[a][0]
                n = a.shape[0] // P
                act.dma_start(vt[r0:r0 + n, :], a.rearrange("(r c) -> r c", c=P)).then_inc(vec_in, 16)
            act.dma_start(vt[V_CW:V_CW + 12, :], I["conv_w"][0].rearrange("w (r c) -> (w r) c", c=P)).then_inc(vec_in, 16)
            for r0, a in ((V_QN, "q_norm_2"), (V_KN, "k_norm_2")):
                for z in range(2):
                    act.dma_start(vt[r0:r0 + 1, HEAD_DIM * z:HEAD_DIM * z + HEAD_DIM], I[a]).then_inc(vec_in, 16)
            act.dma_start(mt[:], I["meta"]).then_inc(x_in, 16)

            def high(c, per=0, i=None):
                n = n_cols(c)
                act.wait_ge(raw_in[c % 2], raw_level(c, per, i))
                if c >= 2:
                    act.wait_ge(tile_done, lin(2 * (c - 1), 2 * per, i))
                act.activation(whi[:, c % 2, 0:n], raw[:, c % 2, 0:n], ACT.Copy).then_inc(w_hi, 1)

            def gained(n, gain, per=0, i=None, lo=META):
                nn = lin(n, per, i)
                act.activation(one(xh, nn)[:, lo:TM], one(hT, nn)[:, lo:TM], ACT.Copy,
                               scale=col(vec, lin(gain + n, per, i))).then_inc(xh_done, 1)

            def added(S, n, per=0, i=None):
                if S or n:
                    act.wait_ge(ssum_done, lin(9 * S + n + (1 if n else 0), per, i))

            def square(n, per=0, i=None, lo=META):
                act.activation(sq[:, lo:TM], one(hT, lin(n, per, i))[:, lo:TM], ACT.Square).then_inc(sq_done, 1)

            def feed(S, n, gain, per=0, i=None):
                added(S, n, per, i)
                if S == 2 and n:
                    act.wait_ge(ssum2_done, lin(n + 1, per, i))
                gained(n, gain, per, i)
                square(n, per, i)
                if S == 2:
                    act.activation(sq2, one(hT, lin(n, per, i))[:, META:TM], ACT.Square,
                                   scale=col(vec, lin(V_FIN + n, per, i))).then_inc(sq2_done, 1)

            def root(S):
                act.wait_ge(ss_done, S + 1)
                if S == 0:
                    act.activation(rt[:, 0:HALF], ps[:, 5, 0:HALF], ACT.Sqrt, bias=eps[:], scale=1.0 / D)
                    act.activation(rt[:, HALF:TM], ps[:, 7, 0:HALF], ACT.Sqrt, bias=eps[:], scale=1.0 / D).then_inc(rt_done, 1)
                else:
                    c = {1: C_F[0], 2: C_F[1], 3: C_FQ, 4: C_F[2], 5: C_PG}[S]
                    act.activation(rt[:, META:TM], ps[:, bank(c + 1, 0) + 1, :], ACT.Sqrt,
                                   bias=eps[:], scale=1.0 / D).then_inc(rt_done, 1)

            def ffn(f, S, gain):
                c = C_F[f]

                def up(c, n, per=0, i=None):
                    high(c + 2, per, i)
                    act.wait_ge(acc_free, lin(2 * c + 1, 2 * per, i))
                    act.activation(tmp[:, 1, :], tmp[:, 0, :], ACT.Silu).then_inc(silu_done, 1)
                    act.wait_ge(h_done, lin(FK * f + n + 1, per, i))
                    act.activation(one(fh, lin(n, per, i)), tmp[:, 3, :], ACT.Copy).then_inc(h_hi, 1)

                root(S)
                if f == 1:
                    act.wait_ge(ms2_done, 1)
                    act.activation(rt[:, META:TM], ssum2, ACT.Sqrt, bias=eps[:], scale=1.0 / D).then_inc(rt2_done, 1)
                act.preload_act_table_set("silu_and_others")
                with act.Fori(0, FK // 2) as i:
                    for j in range(2):
                        up(c + j, j, 2, i)
                d = C_D[f]
                with act.Fori(0, 2) as i:
                    for j in range(2):
                        high(d + 3 * j + 2, 6, i)
                        high(d + 3 * j + 3, 6, i)
                        act.wait_ge(acc_free, lin(2 * d + 6 * j + 3, 12, i))
                        feed(S + 1, 2 * j, gain, 4, i)
                        act.wait_ge(acc_free, lin(2 * d + 6 * j + 6, 12, i))
                        feed(S + 1, 2 * j + 1, gain, 4, i)
                        high(d + 3 * j + 4, 6, i)

            def project(c, S, gain):
                with act.Fori(0, 2) as i:
                    for j in range(2):
                        act.wait_ge(acc_free, lin(2 * (c + j) + 1, 4, i))
                        feed(S, 2 * j, gain, 4, i)
                        act.wait_ge(acc_free, lin(2 * (c + j) + 2, 4, i))
                        feed(S, 2 * j + 1, gain, 4, i)
                        high(c + j + 2, 2, i)

            act.wait_ge(vec_turned, 1)
            act.activation(vec[:, 0:V_ROWS], ps[:, 7, 0:V_ROWS], ACT.Copy).then_inc(vec_done, 1)
            act.wait_ge(vec_done, 1)
            for n in range(DK):
                act.wait_ge(x_turned, n + 1)
                act.activation(hT[:, n, META:TM], ps[:, 2 * (n % 4), :], ACT.Copy).then_inc(x_copied, 1)
                act.activation(hT[:, n, 0:META], ps[:, 2 * (n % 4) + 1, 0:META], ACT.Copy).then_inc(x_copied, 1)
                act.wait_ge(x_copied, 2 * n + 2)
                gained(n, V_N1, lo=0)
                if n == 0:
                    high(0)
            high(1)
            for n in range(DK):
                added(0, n)
                square(n, lo=0)
            high(C_LAT + 2)
            act.wait_ge(ones_done, 1)
            root(0)
            act.wait_ge(acc_free, 2 * C_LAT + 2)
            act.activation(sq[:], cl[:], ACT.Square).then_inc(csq_done, 1)
            for z in range(2):
                act.activation(kst[D_IDX * z:D_IDX * z + D_IDX, :], kw[0:D_IDX, :], ACT.Copy).then_inc(ks_hi, 1)
            high(C_QI + 2)
            act.wait_ge(acc_free, 2 * C_QI + 2)
            act.activation(qih[:], qiT[:], ACT.Copy).then_inc(qi_hi, 1)
            for part in (0, 2):
                for g in range(4):
                    act.activation(qst[D_IDX * part:D_IDX * part + D_IDX, g:HEADS:4, :],
                                   qiT[D_IDX * g:D_IDX * g + D_IDX, :, :], ACT.Copy).then_inc(qst_hi, 1)
            act.wait_ge(css_done, 1)
            act.wait_ge(rs_done, 1)
            act.activation(rt[:, 0:HALF], ps[:, 5, 0:HALF], ACT.Sqrt, bias=eps[:], scale=1.0 / D_LAT)
            act.activation(rt[:, HALF:TM], ps[:, 7, 0:HALF], ACT.Sqrt, bias=eps[:], scale=1.0 / D_LAT).then_inc(crt_done, 1)
            high(C_Q + 2)
            for n, (q, h, k0, k1) in enumerate(SCORES):
                act.wait_ge(s_ready, n + 1)
                if n >= 2:
                    act.wait_ge(score_acc, n - 1)
                act.activation(rl[:, n % 2, 0:k1 - k0], ps[:, score_bank(n), 0:k1 - k0], ACT.Relu).then_inc(relu_done, 1)
                if n % (2 * DK) == DK - 1:
                    high(C_Q + 3 + n // (2 * DK))
            act.wait_ge(c_turned, 1)
            act.activation(ctok[:, 0:QB, :].rearrange("p q d -> p (q d)"), ps[:, 5, :], ACT.Copy).then_inc(ctok_done, 1)
            act.activation(ctok[0:META, QB, :], ps[0:META, 7, 0:P], ACT.Copy).then_inc(ctok_done, 1)
            act.dma_start(pwt[:], I["pool_w"][0].rearrange("g c d -> c g d")).then_inc(misc_in, 16)
            act.dma_start(fbias[:], I["forget_bias_2"][0].rearrange("(h o) -> h o", o=1)).then_inc(misc_in, 16)
            for c in range(C_U, C_CB):
                high(c + 2)
            high(C_CB + 2)
            for g in range(2):
                act.wait_ge(co_done, g + 1)
                act.activation(coh[:, g, :], co[:], ACT.Copy).then_inc(coh_done, 1)
            for g in range(4):
                act.wait_ge(mix_done, g + 1)
                act.activation(ah[:, g, :], ps[:, 2 * g + 1, :], ACT.Copy, scale=col(vec, V_PS + g)).then_inc(ah_done, 1)
            high(C_CB + 3)
            for g in range(2, 4):
                act.wait_ge(co_done, g + 1)
                act.activation(coh[:, g, :], co[:], ACT.Copy).then_inc(coh_done, 1)

            def gate(c, kind, q, bias, per, i):
                for t in range(2):
                    act.wait_ge(acc_free, lin(2 * c + t + 1, 2 * per, i))
                    g = tmp[:, 2 * kind + t, :]
                    b = {} if bias is None else {"bias": col(vec, lin(bias + 2 * q + t, 4, i))}
                    act.activation(g, g, ACT.Sigmoid, **b).then_inc(sig_done, 1)

            act.preload_act_table_set("sigmoid_and_others")
            with act.Fori(0, 2) as i:
                for q in range(2):
                    c = C_AC + 3 * q
                    high(c + 2, 6, i)
                    gate(c, 0, q, V_BG, 6, i)
                    high(c + 3, 6, i)
                    gate(c + 1, 1, q, V_BG + 2 * DK, 6, i)
                    high(c + 4, 6, i)

            def probabilities(A, n, src, dst):
                act.wait_ge(A["mx_done"], n + 1)
                act.activation(dst, src, ACT.Exp, bias=nmx[:, n:n + 1], scale=-1.0,
                               accum_out=den[:, n:n + 1]).then_inc(A["exp_done"], 1)

            def copy_turned(A, n, bank_no, turned, heads_kept):
                h, q = divmod(n, QB)
                act.wait_ge(A["pt_ready"], n + 1)
                if heads_kept == 2 and h >= 2:
                    act.wait_ge(A["pv_ready"], QB * (h - 1))
                if heads_kept == 1 and h >= 1:
                    act.wait_ge(A["pv_ready"], n - QB + 1)
                act.activation(turned[:, 0:q + 1, P * q:P * q + P],
                               ps[:, bank_no, 0:P * (q + 1)].rearrange("p (j t) -> p j t", j=q + 1),
                               ACT.Copy).then_inc(A["pt_copy_a"], 1)

            A = att["dsa"]
            act.preload_act_table_set("exp_and_others")

            def dsa_unit(n):
                w = META + P * (n % QB + 1)
                if n >= 2:
                    act.wait_ge(A["pt_ready"], n - 1)
                probabilities(A, n, lm[:, n % 2, 0:w], pr[:, n % 2, 0:w])

            dsa_unit(0)
            dsa_unit(1)
            for slot in range(4 * 2 * DK):
                n = DSA_STEPS.get(slot)
                if n is not None:
                    if n % QB == QB - 1 and n >= QB:
                        h = n // QB - 1
                        act.wait_ge(A["pv_ready"], QB * (h + 1))
                        act.activation(ath[:, h, :], ps[:, 7, :], ACT.Copy).then_inc(A["hi_done"], 1)
                    if n < QB * HEADS:
                        copy_turned(A, n, 5, pT, 1)
                    if n + 2 < QB * HEADS:
                        dsa_unit(n + 2)
                if slot % (2 * DK) == 2 * DK - 1:
                    high(C_GB + slot // (2 * DK) + 2)

            def merged(hi, n, t, buf, m0, per, i):
                act.wait_ge(m_done, lin(m0 + n, per, i))
                act.activation(one(hi, lin(n - 1, per, i)), buf, ACT.Copy).then_inc(mh_done, 1)

            act.preload_act_table_set("sigmoid_and_others")
            act.wait_ge(acc_free, 2 * C_WB)
            with act.Fori(0, 2) as i:
                for q in range(2):
                    for t in range(2):
                        g = one(gb, lin(2 * q + t, 4, i))
                        act.activation(g, g, ACT.Sigmoid, bias=col(vec, lin(V_BG + DK + 2 * q + t, 4, i))).then_inc(sig_done, 1)
                    merged(mh, 2 * q + 1, 0, one(gb, lin(2 * q, 4, i)), DK, 4, i)
                    merged(mh, 2 * q + 2, 1, one(gb, lin(2 * q + 1, 4, i)), DK, 4, i)
                    high(C_WB + q + 2, 2, i)
            project(C_O, 1, V_N2)
            act.wait_ge(gain_done, 1)
            ffn(0, 1, V_FP)

            ffn(1, 2, V_MX)
            root(3)

            def head_root(n):
                act.wait_ge(hq_ss, n + 1)
                act.activation(rtq[:, n % 4, :], ps[:, 5 + 2 * (n % 2), :], ACT.Sqrt, bias=eps[:],
                               scale=1.0 / HEAD_DIM).then_inc(hq_rt, 1)

            def head_square(n, c):
                act.wait_ge(acc_free, 2 * c + n % 2 + 1)
                if n >= 4:
                    act.wait_ge(hq_out, n - 3)
                act.activation(rtq[:, n % 4, :], qs[:, n % 4, :], ACT.Square).then_inc(hq_done, 1)

            for n0, c in ((0, C_FQ), (2, C_FQ + 1), (4, C_FK), (6, C_FK + 1)):
                high(c + 2)
                head_square(n0, c)
                head_square(n0 + 1, c)
                if n0:
                    head_root(n0 - 2)
                    head_root(n0 - 1)
            act.wait_ge(consts, 14)
            act.activation(selr[:], sel[:], ACT.Copy).then_inc(sel_done, 1)
            high(C_FL + 2)
            act.preload_act_table_set("natural_log_exp_and_others")
            act.wait_ge(fz_done, 1)
            act.activation(ft[:], fz[:], ACT.Abs).then_inc(act_seq, 1)
            act.wait_ge(act_seq, 1)
            act.activation(ft[:], ft[:], ACT.Exp, scale=-1.0).then_inc(act_seq, 1)
            act.wait_ge(act_seq, 2)
            act.activation(ft[:], ft[:], ACT.Ln, bias=ones[0:HEADS, 0:1]).then_inc(ft_done, 1)
            act.wait_ge(f_done, 1)
            act.activation(fFs[:], fF[:], ACT.Copy).then_inc(f_hi, 1)
            high(C_FV + 2)
            head_root(6)
            head_root(7)
            act.preload_act_table_set("natural_log_exp_and_others")
            high(C_FV + 3)

            F = att["fox"]

            def fox_unit(n):
                w = P * (n % QB + 1)
                if n >= UNITS:
                    act.wait_ge(F["pt_ready"], n - UNITS + 1)
                act.wait_ge(F["lg_ready"], n + 1)
                probabilities(F, n, ps[:, 2 * (n % 2) + 1, 0:w], pu[:, n % UNITS, 0:w])

            def pair_high(A, hi, n):
                if n % (2 * QB) == QB - 1 and n >= QB:
                    h = n // QB - 1
                    act.wait_ge(A["pv_ready"], QB * (h + 1))
                    act.activation(hi[:, h // 2, :], ps[:, 7, :], ACT.Copy).then_inc(A["hi_done"], 1)

            def fox_step(n):
                pair_high(F, yfh, n)
                if n < QB * HEADS:
                    copy_turned(F, n, 5, fpT[n // QB % 2], 2)
                if n + 2 < QB * HEADS:
                    fox_unit(n + 2)

            fox_unit(0)
            fox_unit(1)
            for j in range(6):
                for third in range(6):
                    fox_step(6 * j + third)
                high(C_SQ + j + 2)

            B = att["sb"]

            def softplus(n):
                t = pu[:, n % UNITS, 0:P * (n % QB + 1)]
                act.wait_ge(z_capped, n + 1)
                act.activation(t, t, ACT.Exp).then_inc(act_seq, 1)
                act.wait_ge(act_seq, 3 + n)
                act.activation(t, t, ACT.Ln, bias=ones[:, 0:1]).then_inc(sp_done, 1)

            def sb_unit(n):
                t = pu[:, n % UNITS, 0:P * (n % QB + 1)]
                act.wait_ge(B["lg_read"], n + 1)
                act.activation(t, t, ACT.Exp).then_inc(B["p_ready"], 1)

            def sb_step(n):
                pair_high(B, ysh, n)
                if n < QB * HEADS:
                    copy_turned(B, n, 5, fpT[n // QB % 2], 2)
                if n + 2 < QB * HEADS:
                    softplus(n + 2)
                if n + 1 < QB * HEADS:
                    sb_unit(n + 1)

            softplus(0)
            sb_unit(0)
            softplus(1)
            for j in range(8):
                for third in range(6):
                    for n in SB_STEPS[6 * j + third]:
                        sb_step(n)
                high(C_GF + j + 2)

            act.preload_act_table_set("sigmoid_and_others")
            act.wait_ge(acc_free, 2 * C_MX)
            with act.Fori(0, 2) as i:
                for q in range(2):
                    for kind in range(2):
                        for t in range(2):
                            g = one(gates, lin(DK * kind + 2 * q + t, 4, i))
                            act.activation(g, g, ACT.Sigmoid).then_inc(sig_done, 1)
                    merged(m2h, 2 * q + 1, 0, one(gates, lin(2 * q, 4, i)), 2 * DK, 4, i)
                    merged(m2h, 2 * q + 2, 1, one(gates, lin(2 * q + 1, 4, i)), 2 * DK, 4, i)
                    high(C_MX + q + 2, 2, i)
            project(C_O2, 4, V_F2)
            ffn(2, 4, V_PL)
            root(5)

            for j in range(4):
                c = C_PG + j
                if c + 2 < N_CHUNKS:
                    high(c + 2)
                for t in range(2):
                    act.wait_ge(acc_free, 2 * c + t + 1)
                    act.activation(sg[:, 2 * j + t, :], sg[:, 2 * j + t, :], ACT.Sigmoid).then_inc(sig_done, 1)
                if j == 1:
                    for k in range(2):
                        act.wait_ge(p_turned, k + 1)
                        act.activation(ptT[:, k, :], ps[:, 1 + 2 * k, :], ACT.Copy).then_inc(p_copied, 1)
                        act.wait_ge(p_copied, k + 1)
                        act.activation(pTh[:, k, :], ptT[:, k, :], ACT.Copy).then_inc(ph_done, 1)
            for n in range(DK):
                act.wait_ge(o_turned, n + 1)
                act.activation(ot[:, :, P * n:P * n + P], ps[:, 2 * (n % 4), :].rearrange("p (q t) -> p q t", q=QB),
                               ACT.Copy).then_inc(o_copied, 1)

        @block.vector
        def _(dve):
            steps = [0]

            def link(ins):
                ins.then_inc(dve_seq, 1)
                steps[0] += 1
                dve.wait_ge(dve_seq, steps[0])

            def stt(o, a, s, b, op0, op1):
                return dve.scalar_tensor_tensor(o, a, s, b, op0, op1)

            def clear(S):
                if S:
                    dve.wait_ge(ss_done, S)
                dve.memset(ssum[:], 0.0).then_inc(ssum_done, 1)

            def split(X, n, gain, per=0, i=None, lo=META):
                nn = lin(n, per, i)
                dve.wait_ge(xh_done, lin(DK * X + n + 1, per, i))
                stt(one(xl, nn)[:, lo:TM], one(hT, nn)[:, lo:TM], col(vec, lin(gain + n, per, i)),
                    one(xh, nn)[:, lo:TM].bitcast(F32), ALU.mult, ALU.subtract).then_inc(x_split, 1)

            def add_square(S, n, per=0, i=None, lo=META):
                dve.wait_ge(sq_done, lin(DK * S + n + 1, per, i))
                dve.wait_ge(ssum_done, lin(9 * S + 1 + n, per, i))
                dve.tensor_tensor(ssum[:, lo:TM], ssum[:, lo:TM], sq[:, lo:TM], ALU.add).then_inc(ssum_done, 1)

            def feed(S, n, gain, per=0, i=None):
                split(S, n, gain, per, i)
                add_square(S, n, per, i)
                if S == 2:
                    dve.wait_ge(sq2_done, lin(n + 1, per, i))
                    dve.wait_ge(ssum2_done, lin(n + 1, per, i))
                    dve.tensor_tensor(ssum2, ssum2, sq2, ALU.add).then_inc(ssum2_done, 1)

            def root(S):
                lo = 0 if S == 0 else META
                dve.wait_ge(rt_done, S + 1)
                dve.reciprocal(rs[:, lo:TM], rt[:, lo:TM]).then_inc(rs_done, 1)
                dve.wait_ge(rs_done, S + 1)

            def closing_root():
                r = ssum[:, META:TM]
                dve.wait_ge(rt_done, 3)
                link(dve.reciprocal(r, rt[:, META:TM]))
                link(dve.tensor_tensor(ssum2, r, r, ALU.mult))
                dve.tensor_tensor(ssum2, ssum2, ps[:, bank(C_F[1] + 1, 1) + 1, :], ALU.mult).then_inc(ms2_done, 1)
                for n in range(DK):
                    x = hT[:, n, META:TM]
                    stt(x, x, vec[:, V_FIN + n:V_FIN + n + 1], r, ALU.mult, ALU.mult).then_inc(xn_done, 1)
                dve.wait_ge(xn_done, DK)
                dve.wait_ge(rt2_done, 1)
                link(dve.reciprocal(rsx, rt[:, META:TM]))
                dve.tensor_tensor(rsx, rsx, r, ALU.mult).then_inc(rs_done, 1)
                dve.wait_ge(rs_done, 3)

            rsx = rs[:, META:TM]
            rs2 = rs[:].rearrange("p (z t) -> p z t", z=2)

            def done(c, t, per=0, i=None):
                dve.wait_ge(tile_done, lin(2 * c + t + 1, 2 * per, i))

            def scaled(o, c, t, per=0, i=None):
                done(c, t, per, i)
                dve.tensor_tensor(o, ps[0:o.shape[0], bank(c, t), :], rsx[0:o.shape[0]], ALU.mult).then_inc(acc_free, 1)

            def scaled_full(o, c, t):
                done(c, t)
                m, b = o.shape[0], bank(c, t)
                dve.tensor_tensor(o.rearrange("p (z t) -> p z t", z=2), ps[0:m, b:b + 2, 0:HALF], rs2[0:m],
                                  ALU.mult).then_inc(acc_free, 1)

            def update(n, b, factor, inc, per=0, i=None):
                x = one(hT, lin(n, per, i))[:, META:TM]
                stt(x, ps[:, b, :], factor, x, ALU.mult, ALU.add).then_inc(acc_free, inc)

            def ffn(f, S, factor, gain):
                c = C_F[f]
                if f == 1:
                    closing_root()
                else:
                    root(S)
                with dve.Fori(0, FK // 2) as i:
                    for j in range(2):
                        n = FK * f + j
                        scaled(tmp[:, 0, :], c + j, 0, 2, i)
                        scaled(tmp[:, 2, :], c + j, 1, 2, i)
                        dve.wait_ge(silu_done, lin(n + 1, 2, i))
                        dve.wait_ge(acc_free, lin(2 * (c + j) + 2, 4, i))
                        dve.tensor_tensor(tmp[:, 3, :], tmp[:, 1, :], tmp[:, 2, :], ALU.mult).then_inc(h_done, 1)
                        dve.wait_ge(h_hi, lin(n + 1, 2, i))
                        nn = lin(j, 2, i)
                        dve.tensor_tensor(one(fl, nn), tmp[:, 3, :], one(fh, nn).bitcast(F32), ALU.subtract).then_inc(h_split, 1)
                        dve.wait_ge(h_split, lin(n + 1, 2, i))
                d = C_D[f]
                clear(S + 1)
                if S + 1 == 2:
                    dve.memset(ssum2, 0.0).then_inc(ssum2_done, 1)
                with dve.Fori(0, 2) as i:
                    for j in range(2):
                        for t in range(2):
                            n = 2 * j + t
                            done(d + 3 * j + 2, t, 6, i)
                            update(n, bank(d + j, t), factor, 3, 4, i)
                            dve.wait_ge(acc_free, lin(2 * d + 6 * j + 3 * t + 3, 12, i))
                            feed(S + 1, n, gain, 4, i)

            def project(c, S, gain):
                clear(S)
                with dve.Fori(0, 2) as i:
                    for j in range(2):
                        for t in range(2):
                            n = 2 * j + t
                            done(c + j, t, 2, i)
                            update(n, bank(c + j, t), 1.0, 1, 4, i)
                            dve.wait_ge(acc_free, lin(2 * (c + j) + t + 1, 4, i))
                            feed(S, n, gain, 4, i)

            dve.memset(eps[:], EPS)
            dve.memset(ones[:], 1.0).then_inc(ones_done, 1)
            clear(0)
            dve.wait_ge(consts, 9)
            dve.tensor_copy(identr[:], ident[:])
            dve.tensor_scalar(causalr[:], causal[:], -1.0, None, ALU.mult)
            dve.tensor_copy(strictr[:], strict[:])
            dve.wait_ge(vec_done, 1)
            dve.tensor_tensor(vec[:, V_FP:V_FP + DK], vec[:, V_FIN:V_FIN + DK], vec[:, V_F1:V_F1 + DK], ALU.mult).then_inc(gain_done, 1)
            dve.wait_ge(gain_done, 1)
            for n in range(DK):
                split(0, n, V_N1, lo=0)
            for n in range(DK):
                add_square(0, n, lo=0)
            root(0)

            scaled_full(cl[:], C_LAT, 0)
            scaled_full(kw[:], C_LAT, 1)
            dve.wait_ge(acc_free, 2 * C_LAT + 2)
            dve.wait_ge(ks_hi, 1)
            dve.tensor_tensor(kst[2 * D_IDX:3 * D_IDX, :], kw[0:D_IDX, :], kst[0:D_IDX, :].bitcast(F32), ALU.subtract).then_inc(ks_lo, 1)
            for t in range(2):
                scaled(qiT[:, t, :], C_QI, t)
            dve.wait_ge(acc_free, 2 * C_QI + 2)
            dve.wait_ge(qi_hi, 1)
            for g in range(4):
                r = slice(D_IDX * g, D_IDX * g + D_IDX)
                dve.tensor_tensor(qst[D_IDX:2 * D_IDX, g:HEADS:4, :], qiT[r, :, :], qih[r, :, :].bitcast(F32),
                                  ALU.subtract).then_inc(qst_lo, 1)

            def query(c, t):
                done(c, t)
                stt(qT[:, 2 * (c - C_Q) + t, :], ps[:, bank(c, t), :], ATTN_SCALE, rsx, ALU.mult, ALU.mult).then_inc(acc_free, 1)

            query(C_Q, 0)
            dve.wait_ge(wi_turned, 1)
            dve.tensor_scalar(wi[:].rearrange("p q h -> p (q h)"), ps[:, 1, 0:QB * HEADS], INDEX_SCALE, None,
                              ALU.mult).then_inc(wi_done, 1)
            dve.wait_ge(wi_done, 1)
            query(C_Q, 1)

            def add_score(n):
                q, h, k0, k1 = SCORES[n]
                r, a = rl[:, n % 2, 0:k1 - k0], sc[:, q, k0:k1]
                dve.wait_ge(relu_done, n + 1)
                if h == 0:
                    dve.tensor_scalar(a, r, wi[:, q, h:h + 1], None, ALU.mult).then_inc(score_acc, 1)
                else:
                    dve.wait_ge(score_acc, n)
                    stt(a, r, wi[:, q, h:h + 1], a, ALU.mult, ALU.add).then_inc(score_acc, 1)

            def search():
                for q in range(QB):
                    dve.wait_ge(score_acc, max(n for n in range(len(SCORES)) if SCORES[n][0] == q) + 1)
                    w = META + P * (q + 1)
                    s, diag = sc[:, q, 0:w], sc[:, q, w - P:w]
                    link(stt(diag, causal[:], -TAKEN / -NEG, diag, ALU.mult, ALU.add))
                    for _ in range(TOP_K // 8):
                        link(dve.max(m8[:], s))
                        link(dve.match_replace(s, m8[:], s, TAKEN))
                        yield
                    link(dve.tensor_scalar(s, s, TAKEN, NEG, ALU.not_equal, ALU.mult))
                    link(dve.tensor_tensor(diag, diag, causal[:], ALU.add))
                    yield

            steps_of_search = search()

            def some_search(n):
                for _ in range(n):
                    next(steps_of_search, None)

            for j in range(3):
                for t in range(2):
                    for n in range(max(DK * (2 * j + t - 1), 0), DK * (2 * j + t)):
                        add_score(n)
                    query(C_Q + 1 + j, t)
                    if j == 0 and t == 0:
                        dve.wait_ge(crt_done, 1)
                        link(dve.reciprocal(rc[:], rt[:]))
                        stt(cT[:], cl[:], vec[:, V_KV:V_KV + 1], rc[:], ALU.mult, ALU.mult).then_inc(c_done, 1)
                    if j:
                        some_search(2)

            def pool_group(g):
                cur = u[:, g, :]
                if g:
                    dve.wait_ge(pooled_done, g)
                for d in range(g + 1):
                    sh, lo = 1 << d, (2 << d) - 1
                    nxt = win[:, d % 2, :]
                    link(dve.tensor_tensor(nxt[:, lo:TM], cur[:, lo:TM], cur[:, lo - sh:TM - sh], ALU.add))
                    cur = nxt
                stt(pooled[:, g, :], cur[:, META:TM], 1.0 / (2 << g), u[:, g, META:TM], ALU.mult, ALU.subtract).then_inc(pooled_done, 1)

            for j in range(2):
                for t in range(2):
                    scaled_full(u[:, 2 * j + t, :], C_U + j, t)
                some_search(5)
                dve.wait_ge(acc_free, 2 * (C_U + j) + 2)
                pool_group(2 * j)
                pool_group(2 * j + 1)
            dve.wait_ge(pooled_done, 4)
            for j in range(2):
                for t in range(2):
                    scaled_full(cc[:, 2 * j + t, :], C_CC + j, t)
                some_search(7)
            for j in range(2):
                for t in range(2):
                    g = 2 * j + t
                    scaled_full(cv[:], C_CU + j, t)
                    dve.wait_ge(acc_free, 2 * (C_CU + j) + t + 1)
                    link(dve.tensor_tensor(cv[:], cv[:], cc[:, g, :], ALU.mult))
                    link(dve.tensor_scalar(cy[:, g, :], cv[:, META - 2:TM - 2], vec[:, V_CW + g:V_CW + g + 1], None, ALU.mult))
                    for r in (1, 2):
                        w = V_CW + 4 * r + g
                        link(stt(cy[:, g, :], cv[:, META - 2 + r:TM - 2 + r], vec[:, w:w + 1], cy[:, g, :], ALU.mult, ALU.add))
                some_search(5)

            def gated_conv(c):
                for t in range(2):
                    g = 2 * (c - C_CB) + t
                    if g:
                        dve.wait_ge(co_split, g)
                    scaled(co[:], c, t)
                    dve.wait_ge(acc_free, 2 * c + t + 1)
                    dve.tensor_tensor(co[:], co[:], cy[:, g, :], ALU.mult).then_inc(co_done, 1)
                    dve.wait_ge(coh_done, g + 1)
                    dve.wait_ge(co_done, g + 1)
                    dve.tensor_tensor(col_[:, g, :], co[:], coh[:, g, :].bitcast(F32), ALU.subtract).then_inc(co_split, 1)

            gated_conv(C_CB)
            for g in range(4):
                dve.wait_ge(ah_done, g + 1)
                stt(al[:, g, :], ps[:, 2 * g + 1, :], vec[:, V_PS + g:V_PS + g + 1], ah[:, g, :].bitcast(F32),
                    ALU.mult, ALU.subtract).then_inc(a_split, 1)
            some_search(5)
            gated_conv(C_CB + 1)
            dve.wait_ge(co_split, 4)

            for i in range(2):
                for q in range(2):
                    c = C_AC + 3 * q
                    for kind in range(2):
                        for t in range(2):
                            scaled(tmp[:, 2 * kind + t, :], c + kind, t, 6, i)
                        some_search(2)
                    for t in range(2):
                        done(c + 2, t, 6, i)
                        b = bank(c + 2, t)
                        dve.wait_ge(sig_done, lin(4 * q + 2 + t + 1, 8, i))
                        dve.tensor_tensor(tmp[:, t, :], tmp[:, t, :], ps[:, b, :], ALU.mult).then_inc(mul_done, 1)
                        dve.tensor_tensor(tmp[:, 2 + t, :], tmp[:, 2 + t, :], ps[:, b + 1, :], ALU.mult).then_inc(acc_free, 1)
                        dve.wait_ge(mul_done, lin(2 * q + t + 1, 4, i))
                        dve.wait_ge(acc_free, lin(2 * (c + 2) + t + 1, 12, i))
                        dve.tensor_tensor(one(msum, lin(2 * q + t, 4, i)), tmp[:, t, :], tmp[:, 2 + t, :], ALU.add).then_inc(m_done, 1)
                    dve.wait_ge(m_done, lin(2 * q + 2, 4, i))
                    some_search(2)
            some_search(1000)

            def normalise(A, n, probs):
                dve.wait_ge(A["exp_done"], n + 1)
                link(dve.reciprocal(rden[:, n:n + 1], den[:, n:n + 1]))
                dve.tensor_scalar(probs, probs, rden[:, n:n + 1], None, ALU.mult).then_inc(A["p_ready"], 1)

            A = att["dsa"]

            def dsa_unit(n):
                w, b = META + P * (n % QB + 1), 1 + 2 * (n % 2)
                logits = ps[:, b:b + 2, :].rearrange("p b k -> p (b k)")[:, 0:w]
                dve.wait_ge(A["lg_ready"], n + 1)
                if n >= 2:
                    dve.wait_ge(A["exp_done"], n - 1)
                dve.tensor_tensor_reduce(lm[:, n % 2, 0:w], logits, sc[:, n % QB, 0:w], -1.0, 3.0e38, ALU.add, ALU.min,
                                         nmx[:, n:n + 1]).then_inc(A["mx_done"], 1)

            def dsa_meta(n):
                h, q = divmod(n, QB)
                dve.wait_ge(A["pt_ready"], n + 1)
                if h >= 1:
                    dve.wait_ge(A["pv_ready"], n - QB + 1)
                dve.tensor_copy(pT[0:META, QB, P * q:P * q + P], ps[0:META, 6, 0:P]).then_inc(A["pt_copy_d"], 1)

            for n in range(2):
                dsa_unit(n)
                normalise(A, n, pr[:, n % 2, 0:META + P * (n % QB + 1)])
            for slot in range(4 * 2 * DK):
                if slot % DK == DK - 1:
                    scaled(gb[:, slot // DK, :], C_GB + slot // (2 * DK), slot // DK % 2)
                n = DSA_STEPS.get(slot)
                if n is None:
                    continue
                if n + 2 < QB * HEADS:
                    dsa_unit(n + 2)
                if n % QB == QB - 1 and n >= QB:
                    h = n // QB - 1
                    dve.wait_ge(A["hi_done"], h + 1)
                    dve.tensor_tensor(atl[:, h, :], ps[:, 7, :], ath[:, h, :].bitcast(F32),
                                      ALU.subtract).then_inc(A["y_split"], 1)
                if n < QB * HEADS:
                    dsa_meta(n)
                if n + 2 < QB * HEADS:
                    normalise(A, n + 2, pr[:, n % 2, 0:META + P * ((n + 2) % QB + 1)])

            def merged(lo_part, hi_part, buf, n, m0, per, i):
                nn = lin(n, per, i)
                dve.wait_ge(mh_done, lin(m0 + n + 1, per, i))
                dve.tensor_tensor(one(lo_part, nn), buf, one(hi_part, nn).bitcast(F32), ALU.subtract).then_inc(m_split, 1)

            with dve.Fori(0, 2) as i:
                for n in range(4):
                    c, t = C_WB + n // 2, n % 2
                    g = one(gb, lin(n, 4, i))
                    done(c, t, 2, i)
                    dve.wait_ge(sig_done, lin(16 + n + 1, 4, i))
                    dve.tensor_tensor(g, g, ps[:, bank(c, t), :], ALU.mult).then_inc(acc_free, 1)
                    dve.wait_ge(acc_free, lin(2 * c + t + 1, 4, i))
                    dve.tensor_tensor(g, g, one(msum, lin(n, 4, i)), ALU.add).then_inc(m_done, 1)
                    dve.wait_ge(m_done, lin(DK + n + 1, 4, i))
                    merged(ml, mh, g, n, 0, 4, i)
            project(C_O, 1, V_N2)
            ffn(0, 1, 1.0, V_FP)

            ffn(1, 2, 0.5, V_MX)
            root(3)

            def head_scaled(n, c):
                if n >= 4:
                    dve.wait_ge(hq_out, n - 3)
                scaled(qs[:, n % 4, :], c, n % 2)

            def head_normed(n):
                dst, g = (qF, V_QN) if n < 4 else (kF, V_KN)
                dve.wait_ge(hq_rt, n + 1)
                r = rtq[:, n % 4, :]
                link(dve.reciprocal(r, r))
                if n < 4:
                    link(dve.tensor_scalar(r, r, -(HEAD_DIM ** -0.5), None, ALU.mult))
                stt(dst[:, n % 4, :], qs[:, n % 4, :], vec[:, g:g + 1], r, ALU.mult, ALU.mult).then_inc(hq_out, 1)

            for n0, c in ((0, C_FQ), (2, C_FQ + 1), (4, C_FK), (6, C_FK + 1)):
                if n0 == 2:
                    dve.wait_ge(rtok_turned, 1)
                    dve.tensor_copy(rtok[:], ps[:, 1, :].rearrange("p (q t) -> p q t", q=QB)[:, :, 0]).then_inc(rtok_done, 1)
                head_scaled(n0, c)
                head_scaled(n0 + 1, c)
                if n0:
                    head_normed(n0 - 2)
                    head_normed(n0 - 1)

            def tokens_half(v, c, j, t):
                done(c, t)
                for z in range(2):
                    q = 2 * t + z
                    ins = dve.tensor_scalar(v[:, q, CW * j:CW * j + CW], ps[:, bank(c, t), CW * z:CW * z + CW],
                                            rtok[:, q:q + 1], None, ALU.mult)
                ins.then_inc(acc_free, 1)

            def tokens(v, c, j):
                for t in range(2):
                    tokens_half(v, c, j, t)

            dve.wait_ge(tile_done, 2 * C_FL + 2)
            dve.wait_ge(misc_in, 32)
            dve.tensor_tensor(fz[:], ps[0:HEADS, bank(C_FL, 0), :], rsx[0:HEADS], ALU.mult).then_inc(acc_free, 2)
            dve.wait_ge(acc_free, 2 * C_FL + 2)
            dve.tensor_scalar(fz[:], fz[:], fbias[:, 0:1], None, ALU.add).then_inc(fz_done, 1)
            dve.wait_ge(ft_done, 1)
            dve.wait_ge(fz_done, 1)
            link(stt(fz[:], fz[:], 0.0, ft[:], ALU.min, ALU.subtract))
            dve.wait_ge(consts, 14)
            dve.tensor_tensor_scan(fF[0:HEADS, :], fone[:], fz[:], 0.0, ALU.mult, ALU.add).then_inc(f_done, 1)
            dve.wait_ge(f_done, 1)
            dve.wait_ge(f_hi, 1)
            dve.tensor_tensor(fFs[SEL_LO:SEL_LO + HEADS, :], fF[0:HEADS, :], fFs[0:HEADS, :].bitcast(F32), ALU.subtract).then_inc(f_lo, 1)
            dve.wait_ge(rtok_done, 1)
            tokens(vF, C_FV, 0)
            head_normed(6)
            head_normed(7)
            tokens(vF, C_FV + 1, 1)

            F = att["fox"]

            def fox_unit(n):
                w = P * (n % QB + 1)
                dve.wait_ge(F["lg_ready"], n + 1)
                dve.tensor_reduce(nmx[:, n:n + 1], ps[:, 2 * (n % 2) + 1, 0:w], AX.X, ALU.min).then_inc(F["mx_done"], 1)
                normalise(F, n, pu[:, n % UNITS, 0:w])

            def pair_low(A, hi_part, lo_part, n):
                if n % (2 * QB) == QB - 1 and n >= QB:
                    h = n // QB - 1
                    dve.wait_ge(A["hi_done"], h // 2 + 1)
                    dve.tensor_tensor(lo_part[:, h // 2, :], ps[:, 7, :], hi_part[:, h // 2, :].bitcast(F32),
                                      ALU.subtract).then_inc(A["y_split"], 1)

            def fox_step(n):
                pair_low(F, yfh, yfl, n)
                if n + 2 < QB * HEADS:
                    fox_unit(n + 2)

            def sb_projection(c, t):
                if c < C_SK:
                    done(c, t)
                    stt(qS[:, 2 * (c - C_SQ) + t, :], ps[:, bank(c, t), :], HEAD_DIM ** -0.5, rsx,
                        ALU.mult, ALU.mult).then_inc(acc_free, 1)
                elif c < C_SV:
                    scaled(kS[:, 2 * (c - C_SK) + t, :], c, t)
                else:
                    tokens_half(vS, c, c - C_SV, t)

            fox_unit(0)
            fox_unit(1)
            for j in range(6):
                for third in range(6):
                    if third % 3 == 2:
                        sb_projection(C_SQ + j, third // 3)
                    fox_step(6 * j + third)

            B = att["sb"]

            def capped(n):
                w = P * (n % QB + 1)
                dve.wait_ge(B["lg_ready"], n + 1)
                if n >= UNITS:
                    dve.wait_ge(B["pt_ready"], n - UNITS + 1)
                dve.tensor_scalar(pu[:, n % UNITS, 0:w], ps[:, 2 * (n % 2) + 1, 0:w], Z_TOP, None, ALU.min).then_inc(z_capped, 1)

            def sb_unit(n):
                w = P * (n % QB + 1)
                z, R = ps[:, 2 * (n % 2) + 1, 0:w], pu[:, n % UNITS, 0:w]
                dve.wait_ge(sp_done, n + 1)
                link(dve.tensor_tensor(R, z, R, ALU.max))
                link(dve.tensor_tensor_scan(R[:, ::-1], R[:, ::-1], R[:, ::-1], 0.0, ALU.add, ALU.bypass))
                dve.tensor_tensor(R, z, R, ALU.subtract).then_inc(B["lg_read"], 1)

            def sb_step(n):
                pair_low(B, ysh, ysl, n)
                if n + 2 < QB * HEADS:
                    capped(n + 2)
                if n + 1 < QB * HEADS:
                    sb_unit(n + 1)

            dve.wait_ge(F["pt_ready"], QB * HEADS)
            capped(0)
            sb_unit(0)
            capped(1)
            for j in range(8):
                for third in range(6):
                    if third % 3 == 2:
                        scaled(gates[:, 2 * j + third // 3, :], C_GF + j, third // 3)
                    for n in SB_STEPS[6 * j + third]:
                        sb_step(n)

            with dve.Fori(0, 2) as i:
                for q in range(2):
                    c = C_MX + q
                    for t in range(2):
                        n = 2 * q + t
                        g, g2 = one(gates, lin(n, 4, i)), one(gates, lin(DK + n, 4, i))
                        done(c, t, 2, i)
                        b = bank(c, t)
                        dve.wait_ge(sig_done, lin(24 + 4 * q + 2 + t + 1, 8, i))
                        dve.tensor_tensor(g, g, ps[:, b, :], ALU.mult).then_inc(mul_done, 1)
                        dve.tensor_tensor(g2, g2, ps[:, b + 1, :], ALU.mult).then_inc(acc_free, 1)
                        dve.wait_ge(mul_done, lin(DK + n + 1, 4, i))
                        dve.wait_ge(acc_free, lin(2 * c + t + 1, 4, i))
                        dve.tensor_tensor(g, g, g2, ALU.add).then_inc(m_done, 1)
                        merged(m2l, m2h, g, n, DK, 4, i)
            project(C_O2, 4, V_F2)
            ffn(2, 4, 0.5, V_PL)
            root(5)

            for j in range(4):
                for t in range(2):
                    scaled(sg[:, 2 * j + t, :], C_PG + j, t)
                if j == 1:
                    for k in range(2):
                        dve.wait_ge(ph_done, k + 1)
                        dve.tensor_tensor(pTl[:, k, :], ptT[:, k, :], pTh[:, k, :].bitcast(F32), ALU.subtract).then_inc(p_split, 1)
            for n in range(DK):
                dve.wait_ge(tile_done, 2 * C_PP + n + 1)
                dve.wait_ge(sig_done, 40 + n + 1)
                g, x = sg[:, n, :], hT[:, n, META:TM]
                dve.tensor_tensor(g, g, ps[:, 2 * (n % 4) + 1, :], ALU.mult).then_inc(acc_free, 1)
                dve.wait_ge(acc_free, 2 * C_PP + n + 1)
                dve.tensor_tensor(x, x, g, ALU.add).then_inc(o_done, 1)


def kernel(**inputs):
    import numpy as np
    from concourse import bacc
    from concourse.bass_utils import run_bass_kernel_spmd

    nc = bacc.Bacc("TRN2", target_bir_lowering=False, num_devices=1)
    arrays, args = {}, {}
    for name, value in inputs.items():
        a = np.ascontiguousarray(value)
        arrays[f"in_{name}"] = a
        args[name] = nc.dram_tensor(f"in_{name}", a.shape, mybir.dt.from_np(a.dtype), kind="ExternalInput").ap()
    o = nc.dram_tensor("out_0", (1, T, D), F32, kind="ExternalOutput").ap()
    build(nc, args, o)
    r = run_bass_kernel_spmd(nc, [arrays], core_ids=[0])
    return r.results[0]["out_0"]
```
